# Optimizing a Trainium2 kernel written in Bass

```python
import math, functools
import jax, jax.numpy as jnp
from jax import lax
import numpy as np

D_MODEL = 1024
BATCH = 1
SEQ = 256
DEPTH = 2

GRID_W = 64
CTX_LEN = 256
EPS = 1e-6

DN_HEADS = 4
DN_DK = 128
DN_DV = 128
DN_CHUNK = 64
DN_CONV_W = 3
QK_W = DN_HEADS * DN_DK
V_W = DN_HEADS * DN_DV
QKV_W = 2 * QK_W + V_W
POOL_WINDOWS = (2, 4, 8, 16)
POOL_GROUP = D_MODEL // 8
POOL_WIDTH = len(POOL_WINDOWS) * POOL_GROUP
MIX_WIDTH = V_W + POOL_WIDTH
EVEN_IN = QKV_W + V_W + 4 * DN_HEADS + POOL_WIDTH
SC_CONV_W = 3
N_EXPERTS = 16
D_EXPERT = D_MODEL // 2
EC_CAPACITY_FACTOR = 2

N_EVEN = (DEPTH + 1) // 2
N_ODD = DEPTH // 2


def rms_norm(x, g):
    xf = x.astype(jnp.float32)
    y = xf * lax.rsqrt(jnp.mean(xf * xf, axis=-1, keepdims=True) + EPS)
    return (y * g.astype(jnp.float32)).astype(x.dtype)

def modulate(h, shift, scale):
    return h * (1 + scale[:, None]) + shift[:, None]

def dw_conv(x, w):
    k = w.shape[0]
    pad_l = (k - 1) // 2
    return lax.conv_general_dilated(
        x, w[:, None, :].astype(x.dtype), window_strides=(1,), padding=[(pad_l, k - 1 - pad_l)],
        dimension_numbers=('NWC', 'WIO', 'NWC'), feature_group_count=x.shape[-1])

def l2norm(t):
    return t * lax.rsqrt(jnp.sum(t * t, axis=-1, keepdims=True) + EPS)

def to_heads(t, d):
    b, L, _ = t.shape
    return t.reshape(b, L, DN_HEADS, d).transpose(0, 2, 1, 3)

def gated_delta_chunked(q, k, v, beta, log_decay, s0):
    b, h, L, dk = k.shape
    dv = v.shape[-1]
    c = DN_CHUNK
    n = L // c
    k = k.reshape(b, h, n, c, dk)
    v = v.reshape(b, h, n, c, dv)
    beta = beta.reshape(b, h, n, c)
    gam = jnp.cumsum(log_decay.reshape(b, h, n, c), axis=-1)
    incl = jnp.tril(jnp.ones((c, c), dtype=bool))
    strict = jnp.tril(jnp.ones((c, c), dtype=bool), k=-1)
    diff = gam[..., :, None] - gam[..., None, :]
    decay = jnp.where(incl, jnp.exp(jnp.where(incl, diff, 0.0)), 0.0)
    kk = jnp.einsum('bhnid,bhnjd->bhnij', k, k)
    t_mat = jnp.eye(c, dtype=jnp.float32) + jnp.where(strict, kk * decay, 0.0) * beta[..., :, None]
    solve = functools.partial(lax.linalg.triangular_solve, left_side=True, lower=True, unit_diagonal=True)
    u = solve(t_mat, v * beta[..., None])
    wk = solve(t_mat, k * (beta * jnp.exp(gam))[..., None])
    k_dec = k * jnp.exp(gam[..., -1:] - gam)[..., None]
    chunk_decay = jnp.exp(gam[..., -1])[..., None, None]
    to_scan = lambda t: jnp.moveaxis(t, 2, 0)

    def advance(s, u_c, wk_c, kd_c, cd_c):
        w = u_c - jnp.einsum('bhck,bhkv->bhcv', wk_c, s)
        return w, cd_c * s + jnp.einsum('bhck,bhcv->bhkv', kd_c, w)

    if q is None:
        def step_state(s, inp):
            _, s_new = advance(s, *inp)
            return s_new, None
        s_fin, _ = lax.scan(step_state, s0, tuple(map(to_scan, (u, wk, k_dec, chunk_decay))))
        return None, s_fin

    q = q.reshape(b, h, n, c, dk)
    qk = jnp.einsum('bhnid,bhnjd->bhnij', q, k) * decay
    q_dec = q * jnp.exp(gam)[..., None]

    def step(s, inp):
        u_c, wk_c, kd_c, cd_c, qk_c, qd_c = inp
        w, s_new = advance(s, u_c, wk_c, kd_c, cd_c)
        o = jnp.einsum('bhck,bhkv->bhcv', qd_c, s) + jnp.einsum('bhij,bhjv->bhiv', qk_c, w)
        return s_new, o

    s_fin, o = lax.scan(step, s0, tuple(map(to_scan, (u, wk, k_dec, chunk_decay, qk, q_dec))))
    return jnp.moveaxis(o, 0, 2).reshape(b, h, L, dv), s_fin

def even_project(h, w_in, conv_w, a_log, dt_bias):
    proj = h @ w_in
    qkv, z, gates, pool_in = jnp.split(proj, [QKV_W, QKV_W + V_W, QKV_W + V_W + 4 * DN_HEADS], axis=-1)
    qkv = jax.nn.silu(dw_conv(qkv, conv_w)).astype(jnp.float32)
    q, k, v = jnp.split(qkv, [QK_W, 2 * QK_W], axis=-1)
    q = l2norm(to_heads(q, DN_DK)) * DN_DK ** -0.5
    k = l2norm(to_heads(k, DN_DK))
    v = to_heads(v, DN_DV)
    b, L, _ = gates.shape
    gates = gates.astype(jnp.float32).reshape(b, L, 4, DN_HEADS).transpose(2, 0, 3, 1)
    beta = jax.nn.sigmoid(gates[:2])
    a_log = a_log.astype(jnp.float32)[:, None, :, None]
    dt_bias = dt_bias.astype(jnp.float32)[:, None, :, None]
    log_decay = -jnp.exp(a_log) * jax.nn.softplus(gates[2:] + dt_bias)
    return q, k, v, z, beta, log_decay, pool_in

def centred_mean(u, n_seg, seg_len, w):
    b, L, ch = u.shape
    us = u.astype(jnp.float32).reshape(b, n_seg, seg_len, ch)
    cs = jnp.concatenate([jnp.zeros_like(us[:, :, :1]), jnp.cumsum(us, axis=2)], axis=2)
    t = jnp.arange(seg_len)
    lo = jnp.clip(t - w // 2, 0, seg_len)
    hi = jnp.clip(t + w - w // 2, 0, seg_len)
    cnt = (hi - lo).astype(jnp.float32)[:, None]
    return ((cs[:, :, hi] - cs[:, :, lo]) / cnt).reshape(b, L, ch).astype(u.dtype)

def even_output(o, z, pool_in, o_norm, pool_w, pool_scale, w_out, n_seg, seg_len):
    b, _, L, _ = o.shape
    o = o.transpose(0, 2, 1, 3)
    zh = z.reshape(b, L, DN_HEADS, DN_DV).astype(jnp.float32)
    o = (rms_norm(o, o_norm) * jax.nn.silu(zh)).reshape(b, L, V_W).astype(z.dtype)
    groups = jnp.stack([centred_mean(pg, n_seg, seg_len, w) - pg
                        for pg, w in zip(jnp.split(pool_in, len(POOL_WINDOWS), axis=-1), POOL_WINDOWS)], axis=2)
    pooled = jnp.einsum('blgc,gcd->blgd', groups, pool_w).reshape(b, L, POOL_WIDTH) * pool_scale
    return jnp.concatenate([o, pooled], axis=-1) @ w_out

def even_mixer(hl, hc, w_in, conv_w, a_log, dt_bias, o_norm, pool_w, pool_scale, w_out, rows, ctx_out):
    ql, kl, vl, zl, betal, gl, pl = even_project(hl, w_in, conv_w, a_log, dt_bias)
    qc, kc, vc, zc, betac, gc, pc = even_project(hc, w_in, conv_w, a_log, dt_bias)
    flip = lambda t: jnp.flip(t, axis=2)
    s0 = jnp.zeros((hl.shape[0], DN_HEADS, DN_DK, DN_DV), jnp.float32)
    oc_f, sc_f = gated_delta_chunked(qc if ctx_out else None, kc, vc, betac[0], gc[0], s0)
    oc_b, sc_b = gated_delta_chunked(flip(qc) if ctx_out else None, flip(kc), flip(vc), flip(betac[1]), flip(gc[1]), s0)
    ol_f, _ = gated_delta_chunked(ql, kl, vl, betal[0], gl[0], sc_f)
    ol_b, _ = gated_delta_chunked(flip(ql), flip(kl), flip(vl), flip(betal[1]), flip(gl[1]), sc_b)
    y_lat = even_output(ol_f + flip(ol_b), zl, pl, o_norm, pool_w, pool_scale, w_out, rows, GRID_W)
    if not ctx_out:
        return y_lat, None
    y_ctx = even_output(oc_f + flip(oc_b), zc, pc, o_norm, pool_w, pool_scale, w_out, 1, hc.shape[1])
    return y_lat, y_ctx

def short_conv_mixer(h, w_in, conv_w, w_out):
    gb, gc, xin = jnp.split(h @ w_in, 3, axis=-1)
    return (gb * dw_conv(gc * xin, conv_w)) @ w_out

def expert_choice_ffn(h, router, w_gate, w_up, w_down):
    b, n, _ = h.shape
    cap = EC_CAPACITY_FACTOR * n // N_EXPERTS
    aff = jax.nn.softmax(jnp.einsum('bnd,de->bne', h, router).astype(jnp.float32), axis=-1)
    gate, idx = lax.top_k(aff.transpose(0, 2, 1), cap)
    bidx = jnp.arange(b)[:, None, None]
    xg = h[bidx, idx]
    hid = jax.nn.silu(jnp.einsum('becd,edf->becf', xg, w_gate)) * jnp.einsum('becd,edf->becf', xg, w_up)
    y = jnp.einsum('becf,efd->becd', hid, w_down) * gate[..., None].astype(h.dtype)
    return jnp.zeros_like(h).at[bidx, idx].add(y)

def first_inputs(seed: int = 0) -> dict:
    key = jax.random.key(seed)
    ks = jax.random.split(key, 24)
    f32 = jnp.float32
    D = D_MODEL
    nrm = lambda k, shape, s: jax.random.normal(k, shape, f32) * s
    dt = jnp.exp(jax.random.uniform(ks[10], (N_EVEN, 2, DN_HEADS), f32, math.log(1e-3), math.log(1e-1)))
    return {
        "x": nrm(ks[0], (BATCH, SEQ, D), 1.0),
        "c": nrm(ks[1], (BATCH, D), 1.0),
        "ctx": nrm(ks[2], (BATCH, CTX_LEN, D), 1.0),
        "c_ctx": nrm(ks[3], (D,), 1.0),
        "ada_w": nrm(ks[4], (DEPTH, D, 6 * D), 0.5 * D ** -0.5),
        "ada_b": nrm(ks[5], (DEPTH, 6 * D), 0.02),
        "norm_mix": 1.0 + nrm(ks[6], (DEPTH, D), 0.02),
        "norm_ffn": 1.0 + nrm(ks[7], (DEPTH, D), 0.02),
        "norm_final": 1.0 + nrm(ks[8], (D,), 0.02),
        "ev_w_in": nrm(ks[9], (N_EVEN, D, EVEN_IN), D ** -0.5),
        "dn_conv": nrm(ks[11], (N_EVEN, DN_CONV_W, QKV_W), DN_CONV_W ** -0.5),
        "dn_a_log": jnp.log(jax.random.uniform(ks[12], (N_EVEN, 2, DN_HEADS), f32, 1.0, 16.0)),
        "dn_dt_bias": dt + jnp.log(-jnp.expm1(-dt)),
        "dn_norm": 1.0 + nrm(ks[13], (N_EVEN, DN_DV), 0.02),
        "pool_w": nrm(ks[14], (N_EVEN, len(POOL_WINDOWS), POOL_GROUP, POOL_GROUP), POOL_GROUP ** -0.5),
        "pool_scale": 1.0 + nrm(ks[15], (N_EVEN, POOL_WIDTH), 0.1),
        "ev_w_out": nrm(ks[16], (N_EVEN, MIX_WIDTH, D), MIX_WIDTH ** -0.5),
        "sc_w_in": nrm(ks[17], (N_ODD, D, 3 * D), D ** -0.5),
        "sc_conv": nrm(ks[18], (N_ODD, SC_CONV_W, D), SC_CONV_W ** -0.5),
        "sc_w_out": nrm(ks[19], (N_ODD, D, D), D ** -0.5),
        "router": nrm(ks[20], (DEPTH, D, N_EXPERTS), D ** -0.5),
        "w_gate": nrm(ks[21], (DEPTH, N_EXPERTS, D, D_EXPERT), D ** -0.5),
        "w_up": nrm(ks[22], (DEPTH, N_EXPERTS, D, D_EXPERT), D ** -0.5),
        "w_down": nrm(ks[23], (DEPTH, N_EXPERTS, D_EXPERT, D), D_EXPERT ** -0.5),
    }

def first_block(x, c, ctx, c_ctx, ada_w, ada_b, norm_mix, norm_ffn, norm_final,
              ev_w_in, dn_conv, dn_a_log, dn_dt_bias, dn_norm, pool_w, pool_scale, ev_w_out,
              sc_w_in, sc_conv, sc_w_out, router, w_gate, w_up, w_down):
    rows = x.shape[1] // GRID_W
    xl, xc = x, ctx
    for i in range(DEPTH):
        j = i // 2
        ctx_read = i % 2 == 0
        ctx_live = any(l % 2 == 0 for l in range(i + 1, DEPTH))
        sh1_l, sc1_l, g1_l, sh2_l, sc2_l, g2_l = jnp.split(jax.nn.silu(c) @ ada_w[i] + ada_b[i], 6, axis=-1)
        hl = modulate(rms_norm(xl, norm_mix[i]), sh1_l, sc1_l)
        yc = None
        if ctx_read or ctx_live:
            sh1_c, sc1_c, g1_c, sh2_c, sc2_c, g2_c = jnp.split((jax.nn.silu(c_ctx) @ ada_w[i] + ada_b[i])[None], 6, axis=-1)
            hc = modulate(rms_norm(xc, norm_mix[i]), sh1_c, sc1_c)
        if ctx_read:
            yl, yc = even_mixer(hl, hc, ev_w_in[j], dn_conv[j], dn_a_log[j], dn_dt_bias[j], dn_norm[j],
                                pool_w[j], pool_scale[j], ev_w_out[j], rows, ctx_live)
        else:
            yl = short_conv_mixer(hl, sc_w_in[j], sc_conv[j], sc_w_out[j])
            if ctx_live:
                yc = short_conv_mixer(hc, sc_w_in[j], sc_conv[j], sc_w_out[j])
        xl = xl + g1_l[:, None] * yl
        hl2 = modulate(rms_norm(xl, norm_ffn[i]), sh2_l, sc2_l)
        xl = xl + g2_l[:, None] * expert_choice_ffn(hl2, router[i], w_gate[i], w_up[i], w_down[i])
        if ctx_live:
            xc = xc + g1_c[:, None] * yc
            hc2 = modulate(rms_norm(xc, norm_ffn[i]), sh2_c, sc2_c)
            xc = xc + g2_c[:, None] * expert_choice_ffn(hc2, router[i], w_gate[i], w_up[i], w_down[i])
    return rms_norm(xl, norm_final)


CHUNK = 64
N_META = 16
N_EVEN_2 = (DEPTH + 1) // 2
N_ODD_2 = DEPTH // 2
CONV_W = 4

LRU_WIDTH = D_MODEL
LRU_BLOCKS = 4
LRU_BLOCK = LRU_WIDTH // LRU_BLOCKS
RG_LRU_C = 8.0

SSD_WIDTH = D_MODEL
SSD_HEAD_DIM = 64
SSD_HEADS = SSD_WIDTH // SSD_HEAD_DIM
SSD_GROUPS = 2
SSD_HPG = SSD_HEADS // SSD_GROUPS
SSD_STATE = 128
SSD_CHUNK = CHUNK
SSD_CONV_DIM = SSD_WIDTH + 2 * SSD_GROUPS * SSD_STATE

EVEN_SPLITS = (LRU_WIDTH, 2 * LRU_WIDTH, 2 * LRU_WIDTH + SSD_WIDTH,
               2 * LRU_WIDTH + SSD_WIDTH + SSD_CONV_DIM)
EVEN_IN_2 = 2 * LRU_WIDTH + SSD_WIDTH + SSD_CONV_DIM + SSD_HEADS
EVEN_MIX = LRU_WIDTH + SSD_WIDTH

SB_HEADS = 16
SB_HEAD_DIM = D_MODEL // SB_HEADS
SB_WIDTH = SB_HEADS * SB_HEAD_DIM
SB_BLOCK = 128
ODD_IN = 4 * SB_WIDTH


def rmsnorm(x, w):
    xf = x.astype(jnp.float32)
    y = xf * lax.rsqrt(jnp.mean(xf * xf, axis=-1, keepdims=True) + EPS)
    return (y * w.astype(jnp.float32)).astype(x.dtype)

def causal_dwconv(u, w, b):
    out = lax.conv_general_dilated(
        u, w[:, None, :].astype(u.dtype), window_strides=(1,),
        padding=[(CONV_W - 1, 0)], dimension_numbers=('NWC', 'WIO', 'NWC'),
        feature_group_count=u.shape[-1])
    return out + b

def linear_scan(a, b):
    def combine(left, right):
        al, bl = left
        ar, br = right
        return al * ar, ar * bl + br
    _, h = lax.associative_scan(combine, (a, b), axis=1)
    return h

def rg_lru(u, w_a, b_a, w_x, b_x, lam):
    bsz, L, _ = u.shape
    uf = u.astype(jnp.float32)
    ub = uf.reshape(bsz, L, LRU_BLOCKS, LRU_BLOCK)
    r = jax.nn.sigmoid(jnp.einsum('blgi,gij->blgj', ub, w_a).reshape(bsz, L, LRU_WIDTH) + b_a)
    i = jax.nn.sigmoid(jnp.einsum('blgi,gij->blgj', ub, w_x).reshape(bsz, L, LRU_WIDTH) + b_x)
    log_a = -RG_LRU_C * r * jax.nn.softplus(-lam)
    a = jnp.exp(log_a)
    mult = jnp.sqrt(-jnp.expm1(2.0 * log_a))
    return linear_scan(a, mult * i * uf)

def ssd_scan(xh, dt, a, bmat, cmat):
    bsz, L, _, _ = xh.shape
    pad = (-L) % SSD_CHUNK
    def padf(t):
        return jnp.pad(t, [(0, 0), (pad, 0)] + [(0, 0)] * (t.ndim - 2))
    f32 = jnp.float32
    xdt = padf((xh * dt[..., None]).astype(f32))
    adt = padf((dt * a).astype(f32))
    bm = padf(bmat.astype(f32))
    cm = padf(cmat.astype(f32))
    nc = (L + pad) // SSD_CHUNK
    X = xdt.reshape(bsz, nc, SSD_CHUNK, SSD_GROUPS, SSD_HPG, SSD_HEAD_DIM)
    A = adt.reshape(bsz, nc, SSD_CHUNK, SSD_GROUPS, SSD_HPG).transpose(0, 3, 4, 1, 2)
    Bc = bm.reshape(bsz, nc, SSD_CHUNK, SSD_GROUPS, SSD_STATE)
    Cc = cm.reshape(bsz, nc, SSD_CHUNK, SSD_GROUPS, SSD_STATE)
    a_cum = jnp.cumsum(A, axis=-1)
    tri = jnp.tril(jnp.ones((SSD_CHUNK, SSD_CHUNK), bool))
    seg = a_cum[..., :, None] - a_cum[..., None, :]
    decay = jnp.exp(jnp.where(tri, seg, -jnp.inf))
    cb = jnp.einsum('bclgn,bcsgn->bcgls', Cc, Bc)
    y_diag = jnp.einsum('bcgls,bgecls,bcsgep->bclgep', cb, decay, X)
    decay_states = jnp.exp(a_cum[..., -1:] - a_cum)
    states = jnp.einsum('bclgn,bgecl,bclgep->bcgepn', Bc, decay_states, X)
    chunk_tot = jnp.pad(a_cum[..., -1], [(0, 0), (0, 0), (0, 0), (1, 0)])
    cs = jnp.cumsum(chunk_tot, axis=-1)
    tri_c = jnp.tril(jnp.ones((nc + 1, nc + 1), bool))
    decay_chunk = jnp.exp(jnp.where(tri_c, cs[..., :, None] - cs[..., None, :], -jnp.inf))
    states = jnp.concatenate([jnp.zeros_like(states[:, :1]), states], axis=1)
    states = jnp.einsum('bgezc,bcgepn->bzgepn', decay_chunk, states)[:, :-1]
    y_off = jnp.einsum('bclgn,bcgepn,bgecl->bclgep', Cc, states, jnp.exp(a_cum))
    y = (y_diag + y_off).reshape(bsz, L + pad, SSD_HEADS, SSD_HEAD_DIM)
    return y[:, pad:]

def gated_group_rmsnorm(y, z, w):
    bsz, L, W = y.shape
    g = (y * jax.nn.silu(z.astype(jnp.float32))).reshape(bsz, L, SSD_GROUPS, W // SSD_GROUPS)
    g = g * lax.rsqrt(jnp.mean(g * g, axis=-1, keepdims=True) + EPS)
    return g.reshape(bsz, L, W) * w.astype(jnp.float32)

def rglru_ssd_layer(h, norm_w, w_in, lru_conv_w, lru_conv_b, lru_w_a, lru_b_a,
                    lru_w_x, lru_b_x, lru_lambda, ssd_conv_w, ssd_conv_b,
                    ssd_dt_bias, ssd_a_log, ssd_d, ssd_norm, w_out):
    bsz, L, _ = h.shape
    u = rmsnorm(h, norm_w)
    proj = u @ w_in
    lru_x, lru_g, ssd_z, ssd_xbc, ssd_dt = jnp.split(proj, EVEN_SPLITS, axis=-1)
    lx = causal_dwconv(lru_x, lru_conv_w, lru_conv_b)
    y_a = rg_lru(lx, lru_w_a, lru_b_a, lru_w_x, lru_b_x, lru_lambda) * jax.nn.silu(lru_g.astype(jnp.float32))
    xbc = jax.nn.silu(causal_dwconv(ssd_xbc, ssd_conv_w, ssd_conv_b))
    xs, bm, cm = jnp.split(xbc, (SSD_WIDTH, SSD_WIDTH + SSD_GROUPS * SSD_STATE), axis=-1)
    dt = jax.nn.softplus(ssd_dt.astype(jnp.float32) + ssd_dt_bias)
    a = -jnp.exp(ssd_a_log.astype(jnp.float32))
    xh = xs.reshape(bsz, L, SSD_HEADS, SSD_HEAD_DIM)
    y = ssd_scan(xh, dt, a,
                 bm.reshape(bsz, L, SSD_GROUPS, SSD_STATE),
                 cm.reshape(bsz, L, SSD_GROUPS, SSD_STATE))
    y = y + xh.astype(jnp.float32) * ssd_d[:, None]
    y_b = gated_group_rmsnorm(y.reshape(bsz, L, SSD_WIDTH), ssd_z, ssd_norm)
    mixed = jnp.concatenate([y_a, y_b], axis=-1).astype(h.dtype)
    return h + mixed @ w_out

def stick_breaking_block(q_blk, k_ctx, v_ctx, q0):
    tq = q_blk.shape[1]
    s_len = k_ctx.shape[1]
    z = jnp.einsum('bthd,bshd->bhts', q_blk.astype(jnp.float32),
                   k_ctx.astype(jnp.float32)) * (SB_HEAD_DIM ** -0.5)
    before = jnp.arange(s_len)[None, :] < (q0 + jnp.arange(tq))[:, None]
    log_keep = jnp.where(before, jax.nn.log_sigmoid(-z), 0.0)
    csum = jnp.cumsum(log_keep, axis=-1)
    weights = jnp.where(before, jnp.exp(jax.nn.log_sigmoid(z) + csum[..., -1:] - csum), 0.0)
    return jnp.einsum('bhts,bshd->bthd', weights, v_ctx.astype(jnp.float32))

def stick_breaking_layer(h, norm_w, w_in, w_out):
    bsz, L, _ = h.shape
    u = rmsnorm(h, norm_w)
    q, k, v, g = jnp.split(u @ w_in, 4, axis=-1)
    q = q.reshape(bsz, L, SB_HEADS, SB_HEAD_DIM)
    k = k.reshape(bsz, L, SB_HEADS, SB_HEAD_DIM)
    v = v.reshape(bsz, L, SB_HEADS, SB_HEAD_DIM)
    bounds = [0] + list(range(N_META, L, SB_BLOCK)) + [L]
    outs = [stick_breaking_block(q[:, s:e], k[:, :e], v[:, :e], s)
            for s, e in zip(bounds[:-1], bounds[1:])]
    o = jnp.concatenate(outs, axis=1).reshape(bsz, L, SB_WIDTH)
    o = (o * jax.nn.silu(g.astype(jnp.float32))).astype(h.dtype)
    return h + o @ w_out

def second_inputs(seed: int = 0) -> dict:
    key = jax.random.key(seed)
    ks = jax.random.split(key, 24)
    f32 = jnp.float32

    def nrm(k, shape, fan_in):
        return jax.random.normal(k, shape, f32) * (fan_in ** -0.5)

    def gain(k, shape):
        return 1.0 + 0.05 * jax.random.normal(k, shape, f32)

    def bias(k, shape, s=0.05):
        return s * jax.random.normal(k, shape, f32)

    x = jax.random.normal(ks[0], (BATCH, SEQ, D_MODEL), f32)
    meta = jax.random.normal(ks[1], (N_META, D_MODEL), f32)
    even_norm = gain(ks[2], (N_EVEN_2, D_MODEL))
    even_w_in = nrm(ks[3], (N_EVEN_2, D_MODEL, EVEN_IN_2), D_MODEL)
    lru_conv_w = nrm(ks[4], (N_EVEN_2, CONV_W, LRU_WIDTH), CONV_W)
    lru_conv_b = bias(ks[5], (N_EVEN_2, LRU_WIDTH))
    lru_w_a = nrm(ks[6], (N_EVEN_2, LRU_BLOCKS, LRU_BLOCK, LRU_BLOCK), LRU_BLOCK)
    lru_b_a = bias(ks[7], (N_EVEN_2, LRU_WIDTH), 0.1)
    lru_w_x = nrm(ks[8], (N_EVEN_2, LRU_BLOCKS, LRU_BLOCK, LRU_BLOCK), LRU_BLOCK)
    lru_b_x = bias(ks[9], (N_EVEN_2, LRU_WIDTH), 0.1)
    a_c = jax.random.uniform(ks[10], (N_EVEN_2, LRU_WIDTH), f32, minval=0.9, maxval=0.999)
    a0 = a_c ** (1.0 / RG_LRU_C)
    lru_lambda = jnp.log(a0) - jnp.log1p(-a0)
    ssd_conv_w = nrm(ks[11], (N_EVEN_2, CONV_W, SSD_CONV_DIM), CONV_W)
    ssd_conv_b = bias(ks[12], (N_EVEN_2, SSD_CONV_DIM))
    dt0 = jnp.exp(jax.random.uniform(ks[13], (N_EVEN_2, SSD_HEADS), f32,
                                     minval=float(np.log(1e-3)), maxval=float(np.log(1e-1))))
    ssd_dt_bias = dt0 + jnp.log(-jnp.expm1(-dt0))
    ssd_a_log = jnp.log(jax.random.uniform(ks[14], (N_EVEN_2, SSD_HEADS), f32, minval=1.0, maxval=16.0))
    ssd_d = gain(ks[15], (N_EVEN_2, SSD_HEADS))
    ssd_norm = gain(ks[16], (N_EVEN_2, SSD_WIDTH))
    even_w_out = nrm(ks[17], (N_EVEN_2, EVEN_MIX, D_MODEL), EVEN_MIX)
    odd_norm = gain(ks[18], (N_ODD_2, D_MODEL))
    odd_w_in = nrm(ks[19], (N_ODD_2, D_MODEL, ODD_IN), D_MODEL)
    odd_w_out = nrm(ks[20], (N_ODD_2, SB_WIDTH, D_MODEL), SB_WIDTH)
    final_norm = gain(ks[21], (D_MODEL,))
    return {'x': x, 'meta': meta, 'even_norm': even_norm, 'even_w_in': even_w_in,
            'lru_conv_w': lru_conv_w, 'lru_conv_b': lru_conv_b,
            'lru_w_a': lru_w_a, 'lru_b_a': lru_b_a, 'lru_w_x': lru_w_x, 'lru_b_x': lru_b_x,
            'lru_lambda': lru_lambda, 'ssd_conv_w': ssd_conv_w, 'ssd_conv_b': ssd_conv_b,
            'ssd_dt_bias': ssd_dt_bias, 'ssd_a_log': ssd_a_log, 'ssd_d': ssd_d,
            'ssd_norm': ssd_norm, 'even_w_out': even_w_out, 'odd_norm': odd_norm,
            'odd_w_in': odd_w_in, 'odd_w_out': odd_w_out, 'final_norm': final_norm}

def second_block(x, meta, even_norm, even_w_in, lru_conv_w, lru_conv_b, lru_w_a, lru_b_a,
              lru_w_x, lru_b_x, lru_lambda, ssd_conv_w, ssd_conv_b, ssd_dt_bias,
              ssd_a_log, ssd_d, ssd_norm, even_w_out, odd_norm, odd_w_in, odd_w_out,
              final_norm):
    bsz = x.shape[0]
    meta_b = jnp.broadcast_to(meta[None].astype(x.dtype), (bsz, N_META, D_MODEL))
    h = jnp.concatenate([meta_b, x], axis=1)
    for layer in range(DEPTH):
        j = layer // 2
        if layer % 2 == 0:
            h = rglru_ssd_layer(h, even_norm[j], even_w_in[j], lru_conv_w[j], lru_conv_b[j],
                                lru_w_a[j], lru_b_a[j], lru_w_x[j], lru_b_x[j], lru_lambda[j],
                                ssd_conv_w[j], ssd_conv_b[j], ssd_dt_bias[j], ssd_a_log[j],
                                ssd_d[j], ssd_norm[j], even_w_out[j])
        else:
            h = stick_breaking_layer(h, odd_norm[j], odd_w_in[j], odd_w_out[j])
    return rmsnorm(h, final_norm)[:, N_META:].astype(x.dtype)


def setup_inputs(seed=0):
    out = dict(first_inputs(seed))
    for name, value in second_inputs(seed + 1).items():
        if name != "x":
            out[name + "_2"] = value
    return out


def reference(
    x, c, ctx, c_ctx, ada_w, ada_b, norm_mix, norm_ffn, norm_final, ev_w_in, dn_conv, dn_a_log,
    dn_dt_bias, dn_norm, pool_w, pool_scale, ev_w_out, sc_w_in, sc_conv, sc_w_out, router,
    w_gate, w_up, w_down, meta_2, even_norm_2, even_w_in_2, lru_conv_w_2, lru_conv_b_2,
    lru_w_a_2, lru_b_a_2, lru_w_x_2, lru_b_x_2, lru_lambda_2, ssd_conv_w_2, ssd_conv_b_2,
    ssd_dt_bias_2, ssd_a_log_2, ssd_d_2, ssd_norm_2, even_w_out_2, odd_norm_2, odd_w_in_2,
    odd_w_out_2, final_norm_2,
):
    x = first_block(
        x, c, ctx, c_ctx, ada_w, ada_b, norm_mix, norm_ffn, norm_final, ev_w_in, dn_conv,
        dn_a_log, dn_dt_bias, dn_norm, pool_w, pool_scale, ev_w_out, sc_w_in, sc_conv, sc_w_out,
        router, w_gate, w_up, w_down,
    )
    return second_block(
        x, meta_2, even_norm_2, even_w_in_2, lru_conv_w_2, lru_conv_b_2, lru_w_a_2, lru_b_a_2,
        lru_w_x_2, lru_b_x_2, lru_lambda_2, ssd_conv_w_2, ssd_conv_b_2, ssd_dt_bias_2,
        ssd_a_log_2, ssd_d_2, ssd_norm_2, even_w_out_2, odd_norm_2, odd_w_in_2, odd_w_out_2,
        final_norm_2,
    )


_drawn_inputs = setup_inputs


def setup_inputs(seed=0):
    import zlib

    import numpy as np

    out = dict(_drawn_inputs(seed))
    spreads = {}
    factors = {'ctx': 2.724,
     'c_ctx': 3.282,
     'norm_mix': 3.169,
     'norm_ffn': 4.254,
     'dn_norm': 7.753,
     'lru_b_a_2': 8.0,
     'lru_b_x_2': 6.696,
     'ssd_d_2': 2.882}
    for name, (base, spread) in spreads.items():
        noise = np.random.default_rng([zlib.crc32(name.encode()), seed]).standard_normal(out[name].shape)
        drawn = base * np.exp(spread * noise) if base else spread * noise
        out[name] = __import__('jax').numpy.asarray(drawn.astype(out[name].dtype))
    for name, factor in factors.items():
        out[name] = (out[name] * factor).astype(out[name].dtype)
    return out
```

```python
from contextlib import ExitStack

import concourse.bass as bass
from concourse import mybir

F32 = mybir.dt.float32
ALU = mybir.AluOpType
ACT = mybir.ActivationFunctionType
AX = mybir.AxisListType

P = 128
D = 1024
KD = D // P
T = 256
TT = T // P
META = 16
L2 = T + META
HEADS = 4
UNITS = 4
ORDER = ((2, 3, 0, 1), (3, 2, 1, 0))
LEVELS = 7
EXP = 16
CAP = 32
EG = 4
GROUPS = EXP // EG
HID = 512
SSD_H = 16
SB_H = 16
TRI = L2 + (L2 - P) + META
EPS = 1e-6
SLOTS = 6
CHUNK = 4096
MOE_CHUNKS = 12
SRC = ((0, 0, P), (P, L2, P), (2 * P, L2 + L2 - P, META))


def vector_rows():
    groups = (
        (("c", 8), ("c_ctx", 8), ("ada_b", 96), ("norm_mix", 16)),
        (("norm_ffn", 16), ("norm_final", 8), ("dn_conv", 36), ("dn_norm", 1), ("pool_scale", 4),
         ("sc_conv", 24), ("even_norm", 8), ("odd_norm", 8), ("final_norm", 8), ("ssd_norm", 8)),
        (("lru_conv_w", 32), ("lru_conv_b", 8), ("lru_b_a", 8), ("lru_b_x", 8), ("lru_lambda", 8),
         ("ssd_conv_w", 48), ("ssd_conv_b", 12)),
    )
    at = {}
    for g, rows in enumerate(groups):
        r = 0
        for name, n in rows:
            at[name] = (g, r, n)
            r += n
        at[g] = r
    return at


def mixer_steps(d):
    steps = []
    for h in range(HEADS):
        steps += [("setup", h, 0)]
        if h % 2 == 1:
            steps += [("ada", 0, 0)]
    for lv in range(LEVELS):
        for h in range(HEADS + 1):
            if h < HEADS:
                steps += [("turn", lv, h)]
            if h >= 1 and lv >= 1:
                steps += [("grow", lv, h - 1)]
            if h == 1:
                steps += [("ada", 0, 0)]
    for h in range(HEADS):
        steps += [("solve", h, 0)]
    for s in range(UNITS):
        steps += [("walk", s, 0)]
        if s == 1:
            steps += [("ada", 0, 0)]
    return steps


def build(nc, x, c, ctx, c_ctx, ada_w, ada_b, norm_mix, norm_ffn, norm_final, ev_w_in, dn_conv,
          dn_a_log, dn_dt_bias, dn_norm, pool_w, pool_scale, ev_w_out, sc_w_in, sc_conv, sc_w_out,
          router, w_gate, w_up, w_down, meta_2, even_norm_2, even_w_in_2, lru_conv_w_2,
          lru_conv_b_2, lru_w_a_2, lru_b_a_2, lru_w_x_2, lru_b_x_2, lru_lambda_2, ssd_conv_w_2,
          ssd_conv_b_2, ssd_dt_bias_2, ssd_a_log_2, ssd_d_2, ssd_norm_2, even_w_out_2,
          odd_norm_2, odd_w_in_2, odd_w_out_2, final_norm_2, out):
    stack = ExitStack()
    with stack:
        def sb(name, shape, dt=F32):
            return stack.enter_context(nc.sbuf_tensor(name, shape, dt))

        def sem(name):
            return stack.enter_context(nc.semaphore(name))

        ring = sb("weight_ring", [P, SLOTS, CHUNK])
        XH = sb("residual", [P, KD, L2])
        VT = sb("vectors", [P, 3, P])
        WIDE = sb("upper_then_ones", [P, L2])
        GE = sb("lower_incl", [P, P])
        ident = sb("ident", [P, P])
        SEL = sb("select_stream", [P, 2])
        CS = sb("silu_c", [P, KD, 32])
        PART = sb("ada_partials", [P, 512])
        MOD = sb("modulation", [P, 2, 48, 2])
        GW = sb("gates_w", [P, KD, 16])
        SMALL = sb("small", [P, 700])
        A = sb("arena", [P, 23700])
        LE = WIDE[:, 0:P]
        ONES = WIDE[:, P:2 * P]
        ONE = WIDE[:, P:P + 1]
        EPSC = SMALL[:, 0:1]
        banks = [stack.enter_context(nc.psum_tensor(f"bank{i}", [P, 512], F32)) for i in range(8)]
        VB, SB = banks[0:4], banks[4:8]

        def at(off, *dims):
            n = 1
            for s in dims:
                n *= s
            v = A[:, off:off + n]
            if len(dims) == 2:
                return v.rearrange("p (a b) -> p a b", a=dims[0])
            if len(dims) == 3:
                return v.rearrange("p (a b c) -> p a b c", a=dims[0], b=dims[1])
            return v

        small_used = [1]

        def small(*dims):
            n = 1
            for s in dims:
                n *= s
            v = SMALL[:, small_used[0]:small_used[0] + n]
            small_used[0] += n
            assert small_used[0] <= 700, small_used
            if len(dims) == 2:
                return v.rearrange("p (a b) -> p a b", a=dims[0])
            if len(dims) == 3:
                return v.rearrange("p (a b c) -> p a b c", a=dims[0], b=dims[1])
            return v

        def bank(b, *dims):
            n = 1
            for s in dims:
                n *= s
            v = b[:, 0:n]
            if len(dims) == 2:
                return v.rearrange("p (a b) -> p a b", a=dims[0])
            if len(dims) == 3:
                return v.rearrange("p (a b c) -> p a b c", a=dims[0], b=dims[1])
            return v

        def mid(v, n):
            return v.unsqueeze(1).broadcast_to([v.shape[0], n, v.shape[1]])

        def last(v, n):
            return v.unsqueeze(len(v.shape)).broadcast_to(list(v.shape) + [n])

        vec_at = vector_rows()

        def vec(name, i=0, n=1):
            g, r, _ = vec_at[name]
            return VT[:, g, r + i:r + i + n]

        dtb, alog, sdtb, salog, ssdd = small(8), small(8), small(16), small(16), small(8)
        graw = small(4, 16)
        g_s, g_m, g_e = small(4, 8), small(4, 8), small(4, 8)
        BETA, G, GC, EGC, BG = small(4, 8), small(4, 8), small(4, 8), small(4, 8), small(4, 8)
        KS, CDK = small(4, 4), small(4, 4)
        ce, gain, gain_sq = small(16), small(8, 2), small(8)
        AFFT, POS = small(2, 16), small(2, 16)
        rmax, rsum, m8, SLOTN = small(2), small(2), small(8), small(32)
        nba, nbx, lc8, ln8, ltm = small(8), small(8), small(8), small(8), small(8)

        hT = at(0, 8, 512)
        KT = at(4096, 4, 512)
        VTf = at(6144, 4, 512)
        QT = at(8192, 4, 256)
        Z1 = at(9216, 4, 256)
        PADP = at(10240, 16, 80)
        Ktok, Vtok = at(11520, 4, 4, 128), at(13568, 4, 4, 128)
        OT = at(15616, 4, 256)
        CB = at(16640, 4, 2, 258)
        Xn, XnT = at(0, 4, 4, 128), at(2048, 4, 4, 128)
        Am = at(16640, 4, 4, 128)
        Amask = at(18704, 2, 4, 128)
        Qs = at(19728, 2, 4, 128)
        qdT, qkT = at(20752, 4, 256), at(21776, 4, 256)
        St, Wt = at(19728, 4, 128), at(20240, 4, 128)
        diff, Tlo, Thi, Tq = at(6144, 4, 128), at(6656, 4, 128), at(7168, 4, 128), at(7680, 2, 128)
        KBG, BV = at(6144, 2, 4, 128), at(7168, 2, 4, 128)
        LM = A[:, 22800:22800 + 896].bitcast(mybir.dt.bfloat16).rearrange(
            "p (d l j) -> p d l j", d=2, l=7)
        XIN = at(8192, 4, 1024)
        XC = at(12288, 8, 256)
        MIN = at(14336, 1024)
        SQ1 = at(16640, 8, 512)
        VEC = at(0, 3, 128)
        NR1, NV1, NT1 = at(20736, 512), at(21248, 512), at(21760, 512)
        L2S = at(0, 6, 512)
        OSQ = at(0, 2, 512)
        PTA, PTB = at(1024, 16, 80), at(16640, 16, 80)
        PG = at(2304, 4, 256)
        RCNT, IOT = at(3328, 4, 64), at(3584, 2, 256)
        MIX1 = at(4096, 8, 256)
        PW = at(18704, 4, 128)

        h2T, H2 = at(0, 8, 256), at(2048, 2, 1024)
        PT, GPT, CM = at(4096, 2, 512), at(5120, 2, 512), at(6144, 4, 256)
        XG = at(7168, 8, 128)
        HIDD, SG = at(8192, 512), at(8704, 512)
        HT, Y = at(9216, 4, 128), at(9728, 4, 1024)
        AT2, WT2, MT2, PS2 = at(13824, 256), at(14080, 256), at(14336, 256), at(14592, 256)
        RT = at(14848, 2, 8, 16)
        SQn = at(15360, 8, 272)
        NRn, NVn, NTn = at(17536, 272), at(17808, 272), at(18080, 272)
        NR4, NS5 = at(18352, 272), at(18624, 272)
        SQ3 = at(2176, 8, 272)
        GCC, CPAD, CO, MIX2 = at(2048, 8, 256), at(4096, 8, 258), at(6200, 8, 256), at(8300, 8, 256)

        hN = at(0, 8, 272)
        LX, SLG, SZ, XB = at(2176, 8, 272), at(4352, 8, 272), at(6528, 8, 272), at(8704, 12, 272)
        MIX3 = at(11968, 16, 272)
        LR, LI, LTH = at(14144, 8, 272), at(16320, 8, 272), at(18496, 8, 272)
        XTK = at(16320, 3, 1024)
        EB, CBM = at(19392, 3, 432), at(20688, 2, 432)
        CB3 = at(21120, 4, 275)
        CUM, DT3, ADT, DTm, DTn = (at(22220 + 48 * i, 3, 16) for i in range(5))
        MASK3, DTW = at(22460, 432), at(22892, 8, 16)
        GSQ, GRR = at(16320, 8, 272), at(18496, 2, 272)
        QS, KS2, VS = at(2176, 8, 272), at(4352, 8, 384), at(7424, 8, 272)
        VTK, SGT, OS = at(9600, 3, 1024), at(12672, 8, 272), at(14848, 8, 272)
        ZB, LB, PB, EBS = at(17024, 2, 432), at(17888, 2, 432), at(18752, 2, 432), at(19616, 2, 432)
        SMASK, NEG = at(20480, 432), at(20912, 432)
        OUTS = at(2176, 2, 1024)
        vec_src = {"c": c.rearrange("a (r p) -> (a r) p", p=P), "c_ctx": c_ctx.rearrange("(r p) -> r p", p=P),
                   "ada_b": ada_b.rearrange("l (r p) -> (l r) p", p=P),
                   "norm_mix": norm_mix.rearrange("l (r p) -> (l r) p", p=P),
                   "norm_ffn": norm_ffn.rearrange("l (r p) -> (l r) p", p=P),
                   "norm_final": norm_final.rearrange("(r p) -> r p", p=P),
                   "dn_conv": dn_conv.rearrange("o t (r p) -> (o t r) p", p=P),
                   "dn_norm": dn_norm, "pool_scale": pool_scale.rearrange("o (r p) -> (o r) p", p=P),
                   "sc_conv": sc_conv.rearrange("o t (r p) -> (o t r) p", p=P),
                   "even_norm": even_norm_2.rearrange("o (r p) -> (o r) p", p=P),
                   "odd_norm": odd_norm_2.rearrange("o (r p) -> (o r) p", p=P),
                   "final_norm": final_norm_2.rearrange("(r p) -> r p", p=P),
                   "ssd_norm": ssd_norm_2.rearrange("o (r p) -> (o r) p", p=P),
                   "lru_conv_w": lru_conv_w_2.rearrange("o t (r p) -> (o t r) p", p=P),
                   "lru_conv_b": lru_conv_b_2.rearrange("o (r p) -> (o r) p", p=P),
                   "lru_b_a": lru_b_a_2.rearrange("o (r p) -> (o r) p", p=P),
                   "lru_b_x": lru_b_x_2.rearrange("o (r p) -> (o r) p", p=P),
                   "lru_lambda": lru_lambda_2.rearrange("o (r p) -> (o r) p", p=P),
                   "ssd_conv_w": ssd_conv_w_2.rearrange("o t (r p) -> (o t r) p", p=P),
                   "ssd_conv_b": ssd_conv_b_2.rearrange("o (r p) -> (o r) p", p=P)}
        n_vec = len(vec_src)
        small_src = [
            (GW[:, :, :], ev_w_in[0][:, 2048:2064].rearrange("(k p) n -> p k n", p=P)),
            (dtb, dn_dt_bias.rearrange("o d h -> o (d h)").broadcast_to([P, 8])),
            (alog, dn_a_log.rearrange("o d h -> o (d h)").broadcast_to([P, 8])),
            (sdtb, ssd_dt_bias_2.broadcast_to([P, 16])),
            (salog, ssd_a_log_2.broadcast_to([P, 16])),
            (ssdd[0:64], ssd_d_2.rearrange("o (m j) -> o m j", j=2)[:, :, 0].broadcast_to([64, 8])),
            (ssdd[64:P], ssd_d_2.rearrange("o (m j) -> o m j", j=2)[:, :, 1].broadcast_to([64, 8])),
        ]
        n_small = len(small_src)

        landed = [sem(f"weights_landed_{i}") for i in range(SLOTS)]
        weights_used = sem("weights_used")
        vector_filled, vector_drained = sem("vector_bank_filled"), sem("vector_bank_drained")
        scalar_filled, scalar_drained = sem("scalar_bank_filled"), sem("scalar_bank_drained")
        vector_step, scalar_step, pool_step = sem("vector_step"), sem("scalar_step"), sem("pool_step")
        vec_in, x_in, small_in, meta_in = sem("vectors_in"), sem("x_in"), sem("small_in"), sem("meta_in")
        router_in, poolw_in, dtw_in = sem("router_in"), sem("pool_w_in"), sem("dt_w_in")
        consts_ready = sem("constants_ready")
        c_exp, c_ready = sem("c_exp"), sem("silu_c_ready")
        squares_ready, rstd_ready, h_ready = sem("squares_ready"), sem("rstd_ready"), sem("h_ready")
        h_scaled, mean_ready = sem("h_scaled"), sem("second_mean_ready")
        conv_in, conv_out, conv_act = sem("conv_in"), sem("conv_out"), sem("conv_activated")
        l2_squares, l2_rstd, l2_done = sem("l2_squares"), sem("l2_rstd"), sem("l2_done")
        gate_args, gate_exps, decay_ready = sem("gate_args"), sem("gate_exps"), sem("decay_ready")
        gam_exps, gam_done = sem("gamma_exps"), sem("gamma_scales_done")
        diff_ready, decay_exps, tri_ready = sem("diff_ready"), sem("decay_exps"), sem("triangle_ready")
        masked, scaled, kdec_ready = sem("level_masked"), sem("scaled_keys_values"), sem("kdec_ready")
        walked = sem("walk_state_ready")
        ones_ready, mix_ready = sem("norm_out_ready"), sem("mix_ready")
        iota_ready = sem("iota_ready")
        sm_args, sm_exps, aff_ready = sem("softmax_args"), sem("softmax_exps"), sem("affinity_ready")
        pooled_ready = sem("pooled_ready")
        pos_ready, pick_ready = sem("positions_ready"), sem("picks_ready")
        silu_ready, hid_ready = sem("silu_ready"), sem("hidden_ready")
        tanh_ready, logs_ready = sem("lru_tanh_ready"), sem("lru_logs_ready")
        lc_ready, half_ready = sem("lru_decay_scale_ready"), sem("lru_half_log_ready")
        mult_ready = sem("lru_mult_ready")
        dt_args, dt_exps, dt_ready = sem("dt_args"), sem("dt_exps"), sem("dt_ready")
        ssd_args, ssd_exps, ssd_w = sem("ssd_args"), sem("ssd_exps"), sem("ssd_weights_ready")
        gated, gate_sq, gate_rstd = sem("gated_ready"), sem("gated_squares"), sem("gated_rstd")
        sb_logs, sb_soft = sem("stick_logs"), sem("stick_softplus_ready")
        sb_args, sb_w = sem("stick_args"), sem("stick_weights_ready")
        o_rstd, edges_ready, lru_done, mult_args = sem("out_rstd"), sem("edges_ready"), sem("lru_done"), sem("mult_args")
        out_copied, out_done = sem("out_copied"), sem("out_done")

        def cols(w, c0, n=512):
            return ("cols", w[:, c0:c0 + n].rearrange("(k p) n -> p k n", p=P), n)

        stream = [cols(ada_w[0], 512 * i) for i in range(4)]
        W_EV = len(stream)
        ev = ev_w_in[0]
        QKV = 3 * 512
        stream += [cols(ev, 0), cols(ev, 512), cols(ev, 1024), cols(ev, QKV), cols(ev, QKV + 512 + 16)]
        W_ADA = len(stream)
        stream += [cols(ada_w[0], 512 * i) for i in range(4, 12)] + [cols(ada_w[1], 512 * i) for i in range(12)]
        W_EVO = len(stream)
        stream += [cols(ev_w_out[0], 0), cols(ev_w_out[0], 512)]
        W_MOE = [len(stream)]
        stream += [("moe", 0, None)] * (MOE_CHUNKS * GROUPS)
        W_SC = len(stream)
        sc = sc_w_in[0]
        stream += [cols(sc, o) for o in (1024, 2048, 1536, 2560, 0, 512)]
        stream += [cols(sc_w_out[0], 0), cols(sc_w_out[0], 512)]
        W_MOE.append(len(stream))
        stream += [("moe", 1, None)] * (MOE_CHUNKS * GROUPS)
        W_E2 = len(stream)
        e2 = even_w_in_2[0]
        stream += [cols(e2, 3072 + 512 * i) for i in range(3)] + [cols(e2, 0), cols(e2, 512), cols(e2, 1024)]
        W_LRU = len(stream)
        stream += [("lru", None, None)]
        stream += [cols(e2, 1536), cols(e2, 2048), cols(e2, 2560)]
        W_E2O = len(stream)
        stream += [("tall", even_w_out_2[0][:, 256 * i:256 * i + 256].rearrange("(k p) n -> p k n", p=P), 256)
                   for i in range(4)]
        W_OD = len(stream)
        stream += [cols(odd_w_in_2[0], 512 * i) for i in range(8)]
        stream += [cols(odd_w_out_2[0], 0), cols(odd_w_out_2[0], 512)]

        def landed_at(cn):
            return sum(32 if c_ == W_LRU else 16 for c_ in range(cn % SLOTS, cn + 1, SLOTS))

        def l2_buf(i):
            return L2S[:, i, :] if i < 4 else L2S[:, 4 + (i - 4) // 2, (i % 2) * T:(i % 2) * T + T]

        def chunk(n, k=8, w=512):
            return ring[:, n % SLOTS, :].rearrange("p (k w) -> p k w", k=k)

        def h_count(i, k=KD):
            return KD * (i - (i > 4)) + k

        def sq_count(i, k=KD):
            return 1 + KD * (i - 1 - (i > 4)) + (i >= 4) + k if i else 1

        released = {}
        mark = {}

        block = stack.enter_context(nc.Block())

        @block.tensor
        def _(pe):
            n = {"v": 0, "s": 0, "used": 0}

            def v_open():
                if n["v"] >= 4:
                    pe.wait_ge(vector_drained, n["v"] - 3)
                return VB[n["v"] % 4]

            def s_open():
                if n["s"] >= 4:
                    pe.wait_ge(scalar_drained, n["s"] - 3)
                return SB[n["s"] % 4]

            def v_close(mm, name=None):
                mm.then_inc(vector_filled, 1)
                n["v"] += 1
                mark[name] = n["v"]
                return n["v"]

            def s_close(mm, name=None):
                mm.then_inc(scalar_filled, 1)
                n["s"] += 1
                mark[name] = n["s"]
                return n["s"]

            def arrive(c):
                pe.wait_ge(landed[c % SLOTS], landed_at(c))

            def transposes(b, pieces):
                for dst, src in pieces:
                    k = src.shape[0]
                    mm = pe.transpose(dst, src, ident[0:k, 0:k])
                return mm

            pe.wait_ge(consts_ready, 1)
            pe.wait_ge(vec_in, 16 * n_vec)
            b = v_open()
            for g in range(3):
                mm = pe.transpose(b[:, g * P:g * P + vec_at[g]], VEC[0:vec_at[g], g, :],
                                  ident[0:vec_at[g], 0:vec_at[g]])
            v_close(mm, "vec")
            pe.wait_ge(x_in, 32)
            for tt in range(TT):
                for kh in range(2):
                    b = v_open()
                    for k in range(4):
                        mm = pe.transpose(b[:, k * P:k * P + P], XIN[:, tt, (4 * kh + k) * P:(4 * kh + k + 1) * P], ident[:, :])
                    v_close(mm, "x")
                    b = s_open()
                    for k in range(4):
                        mm = pe.transpose(b[:, k * P:k * P + P], XIN[:, 2 + tt, (4 * kh + k) * P:(4 * kh + k + 1) * P], ident[:, :])
                    s_close(mm, "ctx")
            pe.wait_ge(meta_in, 16)
            b = s_open()
            for k in range(KD):
                mm = pe.transpose(b[:, k * META:(k + 1) * META], MIN[0:META, k * P:(k + 1) * P], ident[0:META, 0:META])
            s_close(mm, "meta")

            ada = {"next": 0}

            def ada_mm():
                i = ada["next"]
                cn = i if i < 4 else W_ADA + i - 4
                arrive(cn)
                w = chunk(cn)
                if i == 0:
                    pe.wait_ge(c_ready, 1)
                b = s_open()
                for k in range(KD):
                    j = 32 * (k % 4)
                    mm = pe.matmul(b[j:j + 32, :], CS[:, k, :], w[:, k, :], start=k < 4, stop=k >= 4)
                ada["copied"] = s_close(mm, ("ada", i))
                released[cn] = (scalar_filled, n["s"])

            def ada_turn():
                pe.wait_ge(scalar_drained, ada["copied"])
                b = v_open()
                for f in range(4):
                    mm = pe.matmul(b[:, 2 * f:2 * f + 2], PART[:, f * P:f * P + P], SEL[:, :], start=True, stop=True)
                v_close(mm, ("mod", ada["next"]))
                ada["next"] += 1

            def norm_part(i, k, width, sq):
                if k == 0:
                    norm_part.bank = s_open()
                b = norm_part.bank
                pe.wait_ge(squares_ready, sq_count(i, k + 1))
                mm = pe.matmul(b[:, 0:width], ONES, sq[:, k, 0:width], start=k == 0, stop=k == KD - 1 and i != 4)
                if i == 4:
                    mm = pe.matmul(b[:, T:2 * T], gain_sq[:, k:k + 1].broadcast_to([P, P]), sq[:, k, 0:width],
                                   start=False, stop=k == KD - 1)
                if k == KD - 1:
                    s_close(mm, ("norm", i))

            for k in range(KD):
                norm_part(0, k, 512, SQ1)
            for i in range(4):
                if i == 3:
                    pe.wait_ge(vector_drained, mark[("mod", 0)])
                ada_mm()
                ada_turn()

            def project(cn, mt, rhs_of, width, opener, closer, names, kd=KD, mcols=4, view=None, norm=None, after=None):
                arrive(cn)
                w = chunk(cn) if view is None else view
                for m in range(mcols):
                    b = opener()
                    for k in range(kd):
                        if norm is not None and m == 0:
                            pe.wait_ge(h_ready, h_count(norm, k + 1))
                        mm = pe.matmul(b[:, 0:width], w[:, k, m * P:m * P + P], rhs_of(k), start=k == 0, stop=k == kd - 1)
                    closer(mm, (names, mt + m))
                    if after is not None:
                        after(mt + m)
                released[cn] = (scalar_filled, n["s"]) if closer is s_close else (vector_filled, n["v"])

            project(W_EV, 0, lambda k: hT[:, k, 0:T], T, s_open, s_close, "qkv", norm=0)
            project(W_EV + 1, 4, lambda k: hT[:, k, :], 2 * T, s_open, s_close, "qkv")
            project(W_EV + 2, 8, lambda k: hT[:, k, :], 2 * T, s_open, s_close, "qkv")
            project(W_EV + 3, 0, lambda k: hT[:, k, 0:T], T, s_open, s_close, "z")
            project(W_EV + 4, 0, lambda k: hT[:, k, 0:T], T, v_open, v_close, "pool")
            pe.wait_ge(small_in, 16 * n_small)
            b = v_open()
            for u in range(UNITS):
                for k in range(KD):
                    mm = pe.matmul(b[:, 16 * u:16 * u + 16], hT[:, k, u * P:u * P + P], GW[:, k, :],
                                   start=k == 0, stop=k == KD - 1)
            v_close(mm, "gates")

            for i in range(8):
                w = 2 * T if i < 4 else T
                pe.wait_ge(l2_squares, i + 1)
                b = s_open()
                mm = pe.matmul(b[:, 0:w], ONES, l2_buf(i), start=True, stop=True)
                s_close(mm, ("l2", i))
            for h in range(HEADS):
                pe.wait_ge(conv_act, 9 + h)
                b = v_open()
                for u in range(UNITS):
                    mm = pe.transpose(b[:, u * P:u * P + P], VTf[:, h, u * P:u * P + P], ident[:, :])
                v_close(mm, ("vtok", h))
            for h in range(HEADS):
                pe.wait_ge(l2_done, h + 1)
                b = s_open()
                for u in range(UNITS):
                    mm = pe.transpose(b[:, u * P:u * P + P], KT[:, h, u * P:u * P + P], ident[:, :])
                s_close(mm, ("ktok", h))
            pe.wait_ge(decay_ready, 1)
            b = v_open()
            for d in range(2):
                mm = pe.matmul(b[:, 16 * d:16 * d + 16], (LE, GE)[d][:, :], G[:, :, 4 * d:4 * d + 4], start=True, stop=True)
            v_close(mm, "gc")

            for d in range(2):
                M = (LE, GE)[d]
                xt_at, x_at, qs_at = {}, {}, {}
                turn, grow = 0, 0
                for kind, a, h in mixer_steps(d):
                    if kind == "ada":
                        if ada["next"] < 24:
                            ada_mm()
                            ada_turn()
                    elif kind == "setup":
                        h = a
                        if d == 0 and h == 0:
                            pe.wait_ge(l2_done, 8)
                        b = v_open()
                        for u in range(UNITS):
                            mm = pe.matmul(b[:, u * P:u * P + P], G[:, u, 4 * d + h:4 * d + h + 1].broadcast_to([P, P]),
                                           M[:, :], start=True, stop=True)
                        v_close(mm, ("gamma", d, h))
                        b = v_open()
                        for u in range(UNITS):
                            kt = KT[:, h, u * P:u * P + P]
                            mm = pe.matmul(b[:, u * P:u * P + P], kt, kt, start=True, stop=True)
                        v_close(mm, ("kk", d, h))
                        b = v_open()
                        for u in range(TT):
                            mm = pe.matmul(b[:, u * P:u * P + P], KT[:, h, u * P:u * P + P], QT[:, h, u * P:u * P + P],
                                           start=True, stop=True)
                        v_close(mm, ("qk", d, h))
                    elif kind == "turn":
                        lv, i = a, LEVELS * HEADS * d + turn
                        pe.wait_ge(masked, i + 1)
                        if lv:
                            pe.wait_ge(vector_drained, xt_at[h])
                        b = v_open() if lv == 0 else s_open()
                        for u in range(UNITS):
                            mm = pe.matmul(b[:, u * P:u * P + P], Amask[:, i % 2, u, :],
                                           XnT[:, h, u, :] if lv else ident[:, :], start=True, stop=True)
                        if lv == 0:
                            xt_at[h] = x_at[h] = v_close(mm, ("turn", d, turn))
                        else:
                            qs_at[h] = s_close(mm, ("turn", d, turn))
                        turn += 1
                    elif kind == "grow":
                        lv = a
                        pe.wait_ge(scalar_drained, qs_at[h])
                        pe.wait_ge(vector_drained, x_at[h])
                        q = Qs[:, grow % 2]
                        b = v_open()
                        for u in range(UNITS):
                            mm = pe.matmul(b[:, u * P:u * P + P], Xn[:, h, u, :], q[:, u, :], start=True, stop=True)
                        xt_at[h] = v_close(mm, ("grow", d, grow))
                        if lv < LEVELS - 1:
                            b = v_open()
                            for u in range(UNITS):
                                mm = pe.matmul(b[:, u * P:u * P + P], q[:, u, :], Xn[:, h, u, :], start=True, stop=True)
                            x_at[h] = v_close(mm, ("grow", d, grow))
                        grow += 1
                    elif kind == "solve":
                        h = a
                        pe.wait_ge(scaled, HEADS * d + h + 1)
                        pe.wait_ge(vector_drained, xt_at[h])
                        b = v_open()
                        for u in range(UNITS):
                            mm = pe.matmul(b[:, u * P:u * P + P], XnT[:, h, u, :], BV[:, h % 2, u, :], start=True, stop=True)
                        v_close(mm)
                        b = v_open()
                        for u in range(UNITS):
                            mm = pe.matmul(b[:, u * P:u * P + P], KBG[:, h % 2, u, :], XnT[:, h, u, :], start=True, stop=True)
                        v_close(mm, ("solve", d, h))
                    elif kind == "walk":
                        s = a
                        u = ORDER[d][s]
                        if s == 0:
                            pe.wait_ge(vector_drained, n["v"])
                            pe.wait_ge(kdec_ready, HEADS * (d + 1))
                        else:
                            pe.wait_ge(vector_drained, state_at)
                            b = v_open()
                            for h in range(HEADS):
                                mm = pe.matmul(b[:, h * P:h * P + P], XnT[:, h, u, :], St[:, h, :], start=True, stop=True)
                            pe.wait_ge(vector_drained, v_close(mm, ("w", d, s)))
                        if u < TT:
                            b = s_open() if d == 0 else v_open()
                            for h in range(HEADS):
                                pe.matmul(b[:, h * P:h * P + P], St[:, h, :], qdT[:, h, u * P:u * P + P], start=True, stop=False)
                                mm = pe.matmul(b[:, h * P:h * P + P], Wt[:, h, :], qkT[:, h, u * P:u * P + P], start=False, stop=True)
                            (s_close if d == 0 else v_close)(mm, ("o", d, s))
                        if s < UNITS - 1:
                            b = v_open()
                            for h in range(HEADS):
                                mm = pe.matmul(b[:, h * P:h * P + P], Am[:, h, u, :], Wt[:, h, :] if s else Xn[:, h, u, :],
                                               start=True, stop=True)
                            state_at = v_close(mm, ("state", d, s))
            assert ada["next"] == 24

            for i in range(2):
                pe.wait_ge(ones_ready, i + 1)
                b = s_open()
                mm = pe.matmul(b[:, :], ONES, OSQ[:, i, :], start=True, stop=True)
                s_close(mm, ("onorm", i))
            pe.wait_ge(poolw_in, 16)
            for g in range(4):
                pe.wait_ge(pooled_ready, g + 1)
                b = v_open()
                mm = pe.matmul(b[:, 0:T], PW[:, g, :], PG[:, g, :], start=True, stop=True)
                v_close(mm, ("poolmix", g))
            pe.wait_ge(vector_drained, n["v"])
            def norm_behind(i, width, sq):
                def after(m):
                    if m >= 1:
                        norm_part(i, m - 1, width, sq)
                    if m == KD - 1:
                        norm_part(i, m, width, sq)
                return after

            for j in range(2):
                project(W_EVO + j, 4 * j, lambda k: MIX1[:, k, :], T, v_open, v_close, "out1", after=norm_behind(1, T, SQn))

            def experts(ly):
                base = W_MOE[ly]
                pe.wait_ge(h_ready, h_count(1 + 2 * ly))
                if ly == 0:
                    pe.wait_ge(router_in, 32)
                b = v_open()
                for tt in range(TT):
                    for k in range(KD):
                        mm = pe.matmul(b[:, 16 * tt:16 * tt + 16], h2T[:, k, tt * P:tt * P + P], RT[:, ly, k, :],
                                       start=k == 0, stop=k == KD - 1)
                v_close(mm, ("logits", ly))
                for tt in range(TT):
                    for kh in range(2):
                        b = s_open()
                        for k in range(4):
                            mm = pe.transpose(b[:, k * P:k * P + P], h2T[:, 4 * kh + k, tt * P:tt * P + P], ident[:, :])
                        s_close(mm, ("h2", ly))
                pe.wait_ge(aff_ready, ly + 1)
                b = v_open()
                for tt in range(TT):
                    mm = pe.transpose(b[0:EXP, tt * P:tt * P + P], AFFT[:, tt, :], ident[:, :])
                v_close(mm, ("affT", ly))
                pe.wait_ge(pos_ready, ly + 1)
                b = v_open()
                for tt in range(TT):
                    mm = pe.transpose(b[:, 16 * tt:16 * tt + 16], PS2[0:EXP, tt * P:tt * P + P], ident[0:EXP, 0:EXP])
                v_close(mm, ("posT", ly))
                pe.wait_ge(pick_ready, ly + 1)
                for gh in range(2):
                    b = v_open()
                    for g in range(2):
                        for tt in range(TT):
                            mm = pe.transpose(b[:, (2 * g + tt) * P:(2 * g + tt + 1) * P],
                                              GPT[:, tt, (2 * gh + g) * P:(2 * gh + g + 1) * P], ident[:, :])
                    v_close(mm, ("cm", ly))
                pe.wait_ge(scalar_drained, n["s"])
                v0, s0, u0 = n["v"], n["s"], n["used"]
                mark[("group", ly)] = (v0, s0)
                for c_ in range(MOE_CHUNKS):
                    cc = base + c_
                    if c_ % 4 < 3:
                        released[cc] = (weights_used, u0 + 3 * (c_ // 4) + c_ % 4 + 1, 9)
                    elif c_ == 3:
                        released[cc] = (scalar_filled, s0 + 2, 4)
                    else:
                        released[cc] = (vector_filled, v0 + (2 if c_ == 7 else 4), 4)

                with pe.Fori(0, GROUPS) as g:
                    def arrived(c_):
                        cc = base + c_
                        pe.wait_ge(landed[cc % SLOTS], g * 32 + landed_at(cc))
                        return ring[:, cc % SLOTS, :]

                    def v_bank(i):
                        pe.wait_ge(vector_drained, g * 4 + (v0 + i - 3))
                        return VB[(v0 + i) % 4]

                    def s_bank(i):
                        pe.wait_ge(scalar_drained, g * 4 + (s0 + i - 3))
                        return SB[(s0 + i) % 4]

                    for half in range(2):
                        b = s_bank(0) if half == 0 else v_bank(0)
                        for k in range(4):
                            c0 = 256 * (2 * half + k // 2) + k % 2
                            for tt in range(TT):
                                mm = pe.matmul(b[:, k * P:k * P + P], H2[:, tt, c0:c0 + 255:2],
                                               PT[:, tt, bass.ds(g * P, P)], start=tt == 0, stop=tt == TT - 1)
                        mm.then_inc(scalar_filled if half == 0 else vector_filled, 1)
                    pe.wait_ge(scalar_drained, g * 4 + (s0 + 1))
                    pe.wait_ge(vector_drained, g * 4 + (v0 + 1))
                    for part in range(2):
                        b = s_bank(1) if part == 0 else v_bank(1)
                        for q in range(4):
                            w = arrived(4 * part + q).rearrange("p (e k n) -> p e k n", e=EG, k=2)
                            for k in range(2):
                                for e in range(EG):
                                    mm = pe.matmul(b[32 * e:32 * e + 32, :], XG[:, 2 * q + k, 32 * e:32 * e + 32],
                                                   w[:, e, k, :], start=q == 0 and k == 0, stop=q == 3 and k == 1)
                            mm.then_inc(weights_used if q < 3 else (scalar_filled, vector_filled)[part], 1)
                    pe.wait_ge(vector_drained, g * 4 + (v0 + 2))
                    for half in range(2):
                        b = s_bank(2) if half == 0 else v_bank(2)
                        for f in range(2):
                            ff = 2 * half + f
                            mm = pe.transpose(b[:, f * P:f * P + P], HIDD[:, ff * P:ff * P + P], ident[:, :])
                        mm.then_inc(scalar_filled if half == 0 else vector_filled, 1)
                    pe.wait_ge(scalar_drained, g * 4 + (s0 + 3))
                    pe.wait_ge(vector_drained, g * 4 + (v0 + 3))
                    b0, b1 = s_bank(3), v_bank(3)
                    for f in range(4):
                        w = arrived(8 + f).rearrange("p (e n) -> p e n", e=EG)
                        for half, b in ((0, b0), (1, b1)):
                            for e in range(EG):
                                mm = pe.matmul(b[32 * e:32 * e + 32, :], HT[:, f, 32 * e:32 * e + 32],
                                               w[:, e, 512 * half:512 * half + 512], start=f == 0, stop=f == 3)
                            if f == 3:
                                mm.then_inc(scalar_filled if half == 0 else vector_filled, 1)
                        if f < 3:
                            mm.then_inc(weights_used, 1)
                n["v"] += 4 * GROUPS
                n["s"] += 4 * GROUPS
                n["used"] += 9 * GROUPS
                pe.wait_ge(scalar_drained, n["s"])
                pe.wait_ge(vector_drained, n["v"])
                if ly == 1:
                    pe.wait_ge(squares_ready, sq_count(4, 0))
                    b = s_open()
                    for k in range(KD):
                        mm = pe.matmul(b[:, 0:META], ONES, SQn[:, k, T:L2], start=k == 0, stop=k == KD - 1)
                    s_close(mm, "meta_norm")
                after = norm_behind(2 + 2 * ly, T, SQn)
                for m in range(KD):
                    b = v_open()
                    for g in range(GROUPS):
                        mm = pe.matmul(b[:, 0:T], Y[:, g, m * P:m * P + P], CM[:, g, :], start=g == 0, stop=g == GROUPS - 1)
                    v_close(mm, ("combine", ly, m))
                    after(m)

            experts(0)

            h2 = lambda k: h2T[:, k, :]
            project(W_SC, 0, h2, T, s_open, s_close, "gc", norm=2)
            project(W_SC + 1, 0, h2, T, v_open, v_close, "xin")
            project(W_SC + 2, 4, h2, T, s_open, s_close, "gc")
            project(W_SC + 3, 4, h2, T, v_open, v_close, "xin")
            project(W_SC + 4, 0, h2, T, v_open, v_close, "gb")
            project(W_SC + 5, 4, h2, T, v_open, v_close, "gb")
            pe.wait_ge(vector_drained, n["v"])
            for j in range(2):
                project(W_SC + 6 + j, 4 * j, lambda k: MIX2[:, k, :], T, v_open, v_close, "out2", after=norm_behind(3, T, SQn))

            experts(1)

            h3 = lambda k: hN[:, k, :]
            for j in range(3):
                project(W_E2 + j, 4 * j, h3, L2, s_open, s_close, "conv3", norm=5 if j == 0 else None)
            for j in range(2):
                project(W_E2 + 3 + j, 12 + 4 * j, h3, L2, s_open, s_close, "conv3")
            pe.wait_ge(dtw_in, 16)
            b = v_open()
            for i, (t0, _, r) in enumerate(SRC):
                for k in range(KD):
                    mm = pe.matmul(b[0:r, 16 * i:16 * i + 16], hN[:, k, t0:t0 + r], DTW[:, k, :], start=k == 0, stop=k == KD - 1)
            v_close(mm, "dt")
            project(W_E2 + 5, 0, h3, L2, s_open, s_close, "lru_g")
            pe.wait_ge(conv_out, 12 + 20)
            arrive(W_LRU)
            wax = ring[:, W_LRU % SLOTS, :].rearrange("p (g b k n) -> p g b k n", g=2, b=4, k=2)
            for m in range(KD):
                for g in range(2):
                    b = s_open()
                    for k in range(2):
                        mm = pe.matmul(b[:, 0:L2], wax[:, g, m // 2, k, (m % 2) * P:(m % 2) * P + P], LX[:, 2 * (m // 2) + k, :],
                                       start=k == 0, stop=k == 1)
                    s_close(mm, ("lru", m, g))
            released[W_LRU] = (scalar_filled, n["s"])
            project(W_LRU + 1, 4, h3, L2, s_open, s_close, "lru_g")
            for j in range(2):
                project(W_LRU + 2 + j, 4 * j, h3, L2, s_open, s_close, "ssd_z")

            pe.wait_ge(dt_ready, 1)
            b = v_open()
            pe.matmul(b[:, 0:16], LE, ADT[:, 0, :], start=True, stop=True)
            pe.matmul(b[:, 16:32], LE, ADT[:, 1, :], start=True, stop=False)
            pe.matmul(b[:, 16:32], ONES, ADT[:, 0, :], start=False, stop=True)
            pe.matmul(b[0:META, 32:48], WIDE[0:META, 0:META], ADT[0:META, 2, :], start=True, stop=False)
            pe.matmul(b[0:META, 32:48], WIDE[:, P:P + META], ADT[:, 0, :], start=False, stop=False)
            mm = pe.matmul(b[0:META, 32:48], WIDE[:, P:P + META], ADT[:, 1, :], start=False, stop=True)
            v_close(mm, "cum")
            pe.wait_ge(conv_act, 12 + 12)
            for g in range(2):
                b = v_open()
                pe.matmul(b[:, 0:272], XB[:, 8 + g, 0:P], XB[:, 10 + g, 0:272], start=True, stop=True)
                pe.matmul(b[:, 272:416], XB[:, 8 + g, P:2 * P], XB[:, 10 + g, P:272], start=True, stop=True)
                mm = pe.matmul(b[0:META, 416:432], XB[:, 8 + g, 256:272], XB[:, 10 + g, 256:272], start=True, stop=True)
                v_close(mm, ("cb", g))
            pe.wait_ge(lru_done, 1)
            for i, (t0, _, r) in enumerate(SRC):
                for kh in range(2):
                    b = s_open()
                    for k in range(4):
                        mm = pe.transpose(b[0:r, k * P:k * P + P], XB[:, 4 * kh + k, t0:t0 + r], ident[:, :])
                    s_close(mm, ("xtk", i, kh))
            xtk_done = n["s"]

            def cum_rows(h):
                b = v_open()
                pe.matmul(b[:, 0:L2], ADT[:, 0, h:h + 1].broadcast_to([P, P]), WIDE[:, 0:L2], start=True, stop=False)
                pe.matmul(b[:, P:L2], ADT[:, 1, h:h + 1].broadcast_to([P, P]), WIDE[:, 0:L2 - P], start=False, stop=False)
                mm = pe.matmul(b[:, 2 * P:L2], ADT[0:META, 2, h:h + 1].broadcast_to([META, P]), WIDE[0:META, 0:META],
                               start=False, stop=True)
                v_close(mm, ("cumrow", h))

            cum_rows(0)
            cum_rows(1)
            for h in range(SSD_H):
                if h + 2 < SSD_H:
                    cum_rows(h + 2)
                pe.wait_ge(ssd_w, h + 1)
                if h == 0:
                    pe.wait_ge(scalar_drained, xtk_done)
                b = v_open()
                r0 = 64 * (h % 2)
                for i, (t0, c0, r) in enumerate(SRC):
                    mm = pe.matmul(b[r0:r0 + 64, t0:L2], XTK[0:r, i, 64 * h:64 * h + 64], EB[0:r, h % 3, c0:c0 + L2 - t0],
                                   start=i == 0, stop=i == 2)
                v_close(mm, ("y", h))
            for g in range(2):
                pe.wait_ge(gate_sq, g + 1)
                b = s_open()
                for k in range(4):
                    mm = pe.matmul(b[:, 0:L2], ONES, GSQ[:, 4 * g + k, :], start=k == 0, stop=k == 3)
                s_close(mm, ("gnorm", g))
            pe.wait_ge(mix_ready, 1)
            for j in range(4):
                project(W_E2O + j, 2 * j, lambda k: MIX3[:, k, :], L2, v_open, v_close, "out3", kd=16, mcols=2,
                        view=chunk(W_E2O + j, 16, 256), after=norm_behind(6, L2, SQ3))

            for j in range(2):
                project(W_OD + j, 4 * j, h3, L2, s_open, s_close, "q", norm=6 if j == 0 else None)
            for j in range(2):
                project(W_OD + 2 + j, 4 * j, h3, L2, v_open, v_close, "k")
            for j in range(2):
                project(W_OD + 4 + j, 4 * j, h3, L2, v_open, v_close, "v")
            vv = n["v"]
            for j in range(2):
                project(W_OD + 6 + j, 4 * j, h3, L2, s_open, s_close, "g")
            pe.wait_ge(vector_drained, vv)
            for i, (t0, _, r) in enumerate(SRC):
                for kh in range(2):
                    b = v_open()
                    for k in range(4):
                        mm = pe.transpose(b[0:r, k * P:k * P + P], VS[:, 4 * kh + k, t0:t0 + r], ident[:, :])
                    v_close(mm, ("vtk", i, kh))
            pe.wait_ge(vector_drained, n["v"])
            pe.wait_ge(scalar_drained, n["s"])

            def stick_scores(h):
                m, r0 = h // 2, 64 * (h % 2)
                b = s_open()
                for i, (t0, c0, _) in enumerate(SRC):
                    mm = pe.matmul(b[:, c0:c0 + L2 - t0], KS2[r0:r0 + 64, m, t0:t0 + P], QS[r0:r0 + 64, m, t0:L2],
                                   start=True, stop=True)
                s_close(mm, ("z", h))

            def stick_sums(h):
                pe.wait_ge(sb_soft, h + 1)
                q = PB[:, h % 2, :]
                b = v_open()
                pe.matmul(b[:, 0:L2], GE[:, :], q[:, 0:L2], start=True, stop=False)
                pe.matmul(b[:, P:L2], ONES, q[:, 272:416], start=False, stop=False)
                pe.matmul(b[:, 2 * P:L2], ONES, q[:, 416:432], start=False, stop=True)
                pe.matmul(b[:, 272:416], GE[:, :], q[:, 272:416], start=True, stop=False)
                pe.matmul(b[:, 400:416], ONES, q[:, 416:432], start=False, stop=True)
                mm = pe.matmul(b[:, 416:432], GE[:, :], q[:, 416:432], start=True, stop=True)
                v_close(mm, ("suffix", h))

            def stick_out(h):
                pe.wait_ge(sb_w, h + 1)
                b = v_open()
                r0 = 64 * (h % 2)
                for i, (t0, c0, r) in enumerate(SRC):
                    mm = pe.matmul(b[r0:r0 + 64, t0:L2], VTK[0:r, i, 64 * h:64 * h + 64], EBS[0:r, h % 2, c0:c0 + L2 - t0],
                                   start=i == 0, stop=i == 2)
                v_close(mm, ("o3", h))

            stick_scores(0)
            stick_scores(1)
            for h in range(SB_H):
                stick_sums(h)
                if h + 2 < SB_H:
                    stick_scores(h + 2)
                if h >= 1:
                    stick_out(h - 1)
            stick_out(SB_H - 1)
            pe.wait_ge(vector_drained, n["v"])
            for j in range(2):
                project(W_OD + 8 + j, 4 * j, lambda k: OS[:, k, :], L2, v_open, v_close, "out4",
                        after=norm_behind(7, T, SQ3))

            for tt in range(TT):
                for kh in range(2):
                    b = v_open() if kh == 0 else s_open()
                    for k in range(4):
                        pe.wait_ge(h_ready, h_count(7, 4 * kh + k + 1))
                        mm = pe.transpose(b[:, k * P:k * P + P], h2T[:, 4 * kh + k, tt * P:tt * P + P], ident[:, :])
                    (v_close if kh == 0 else s_close)(mm, ("final", tt))
            mark["v_end"], mark["s_end"] = n["v"], n["s"]

        @block.sync
        def _(sp):
            def load(cn):
                kind, src, w = stream[cn]
                k = {"cols": 8, "tall": 16}[kind]
                sp.dma_start(chunk(cn, k, w), src).then_inc(landed[cn % SLOTS], 16)

            def free_slot(cn):
                if cn >= SLOTS:
                    signal, value = released[cn - SLOTS][0:2]
                    sp.wait_ge(signal, value)

            def load_group(ly, g, c_, cn):
                dst = ring[:, cn % SLOTS, :]
                e0 = g * EG
                if c_ < 8:
                    w = (w_gate, w_up)[c_ // 4][ly]
                    q = c_ % 4
                    sp.dma_start(dst.rearrange("p (e n) -> p e n", e=EG),
                                 w[bass.ds(e0, EG), 2 * q * P:(2 * q + 2) * P, :].rearrange("e (p k) n -> p e (k n)", p=P))\
                        .then_inc(landed[cn % SLOTS], 16)
                else:
                    f = c_ - 8
                    sp.dma_start(dst.rearrange("p (e n) -> p e n", e=EG),
                                 w_down[ly][bass.ds(e0, EG), f * P:(f + 1) * P, :].rearrange("e p n -> p e n"))\
                        .then_inc(landed[cn % SLOTS], 16)

            cn = 0
            while cn < len(stream):
                if stream[cn][0] == "moe":
                    ly = stream[cn][1]
                    for c_ in range(MOE_CHUNKS):
                        free_slot(cn + c_)
                        load_group(ly, 0, c_, cn + c_)
                    with sp.Fori(1, GROUPS) as g:
                        for c_ in range(MOE_CHUNKS):
                            prior = cn + (c_ - SLOTS) % MOE_CHUNKS
                            signal, value, per_group = released[prior]
                            back = 0 if c_ >= SLOTS else per_group
                            sp.wait_ge(signal, g * per_group + (value - back))
                            load_group(ly, g, c_, cn + c_)
                    cn += MOE_CHUNKS * GROUPS
                    for i in range(MOE_CHUNKS):
                        signal, value, per_group = released[cn - MOE_CHUNKS * GROUPS + i]
                        released[cn - MOE_CHUNKS + i] = (signal, value + (GROUPS - 1) * per_group)
                    continue
                if cn == 0:
                    sp.wait_ge(vec_in, 16 * n_vec)
                if cn == 2:
                    sp.wait_ge(x_in, 32)
                free_slot(cn)
                if stream[cn][0] == "lru":
                    half = ring[:, cn % SLOTS, :].rearrange("p (g b k n) -> p g b k n", g=2, b=4, k=2)
                    for i, w in enumerate((lru_w_a_2, lru_w_x_2)):
                        sp.dma_start(half[:, i].rearrange("p b k n -> p (b k) n"), w[0].rearrange("b (k p) n -> p (b k) n", p=P))\
                            .then_inc(landed[cn % SLOTS], 16)
                else:
                    load(cn)
                cn += 1
            sp.wait_ge(out_copied, 2)
            sp.wait_ge(scalar_drained, mark["s_end"])
            for tt in range(TT):
                sp.dma_start(out[0, tt * P:(tt + 1) * P, :], OUTS[:, tt, :]).then_inc(out_done, 16)
            sp.wait_ge(out_done, 16 * TT)

        @block.gpsimd
        def _(pool):
            steps = [0]

            def then(ins):
                steps[0] += 1
                ins.then_inc(pool_step, 1)
                pool.wait_ge(pool_step, steps[0])

            def keep_if(v, pattern, base, mult, fill=0.0, op=ALU.is_ge):
                return pool.affine_select(out=v, in_=v, compare_op=op, fill=fill, base=base, pattern=pattern,
                                          channel_multiplier=mult)

            then(pool.memset(ident[:, :], 0.0))
            then(keep_if(ident[:, :], [[-1, P]], 0, 1, 1.0, ALU.not_equal))
            then(pool.memset(WIDE[:, :], 1.0))
            then(keep_if(LE, [[1, P]], 0, -1))
            then(pool.memset(GE[:, :], 1.0))
            then(keep_if(GE[:, :], [[-1, P]], 0, 1))
            then(pool.memset(SEL[:, :], 0.0))
            for q in range(4):
                then(keep_if(SEL[:, :], [[-1, 2]], -32 * q, 1, 1.0, ALU.not_equal))
            then(pool.memset(EPSC, EPS))
            pool.iota(SLOTN, pattern=[[1, CAP]], base=1, channel_multiplier=0,
                      allow_small_or_imprecise_dtypes=True).then_inc(consts_ready, 1)
            then(pool.memset(LM, 0.0))
            for lv in range(LEVELS):
                b = 1 << lv
                for d in range(2):
                    v = LM[:, d, lv, :].rearrange("p (n h j) -> p n h j", h=2, j=b)[:, :, d, :]
                    nb = P // (2 * b)
                    lo = b if d == 0 else 0
                    then(pool.memset(v, 1.0))
                    then(keep_if(v, [[-2 * b, nb], [0, b]], -lo, 1))
                    then(keep_if(v, [[2 * b, nb], [0, b]], lo + b - 1, -1))
            turn = 0
            for d in range(2):
                pool.wait_ge(tri_ready, HEADS * (d + 1))
                for lv in range(LEVELS):
                    for h in range(HEADS):
                        i = LEVELS * HEADS * d + turn % (LEVELS * HEADS)
                        k = turn % (LEVELS * HEADS)
                        if k >= 2:
                            if (k - 2) // HEADS == 0:
                                pool.wait_ge(vector_drained, mark[("turn", d, k - 2)])
                            else:
                                pool.wait_ge(scalar_filled, mark[("turn", d, k - 2)])
                        pool.tensor_tensor(Amask[:, i % 2], Am[:, h], mid(LM[:, d, lv, :], UNITS), ALU.mult).then_inc(masked, 1)
                        turn += 1
                pool.wait_ge(masked, LEVELS * HEADS * (d + 1))
                for h in range(HEADS):
                    if h >= 2:
                        pool.wait_ge(vector_filled, mark[("solve", d, h - 2)])
                    pool.tensor_tensor(KBG[:, h % 2], Ktok[:, h], last(BG[:, :, 4 * d + h], P), ALU.mult)
                    pool.tensor_tensor(BV[:, h % 2], Vtok[:, h], last(BETA[:, :, 4 * d + h], P), ALU.mult).then_inc(scaled, 1)
                for h in range(HEADS):
                    pool.tensor_tensor(Am[:, h], Ktok[:, h], last(KS[:, h, :], P), ALU.mult).then_inc(kdec_ready, 1)
            pool.wait_ge(vector_drained, mark[("o", 1, 3)])
            for g in range(4):
                hw = 1 << g
                pool.iota(IOT[:, 0, 64 * g:64 * g + 64], pattern=[[1, 64]], base=hw, channel_multiplier=0,
                          allow_small_or_imprecise_dtypes=True)
                pool.iota(IOT[:, 1, 64 * g:64 * g + 64], pattern=[[-1, 64]], base=64 + hw, channel_multiplier=0,
                          allow_small_or_imprecise_dtypes=True).then_inc(iota_ready, 1)
            pool.wait_ge(h_ready, h_count(5))
            for i, (t0, c0, _) in enumerate(SRC):
                w = L2 - t0
                pool.tensor_copy(MASK3[:, c0:c0 + w], WIDE[:, 0:w]).then_inc(iota_ready, 1)
            pool.wait_ge(h_ready, h_count(6))
            then(pool.memset(SMASK, 1.0))
            for i, (t0, c0, _) in enumerate(SRC):
                w = L2 - t0
                then(keep_if(SMASK[:, c0:c0 + w], [[1, w]], -1, -1))
            pool.tensor_scalar(NEG, SMASK, 1.0e4, -1.0e4, ALU.mult, ALU.add).then_inc(iota_ready, 1)

        @block.scalar
        def _(act):
            n = {"s": 0, "step": 0}

            def take():
                act.wait_ge(scalar_filled, n["s"] + 1)
                return SB[n["s"] % 4]

            def drained(ins):
                n["s"] += 1
                ins.then_inc(scalar_drained, 1)

            def then(ins):
                n["step"] += 1
                ins.then_inc(scalar_step, 1)
                act.wait_ge(scalar_step, n["step"])

            def logs():
                act.preload_act_table_set("natural_log_exp_and_others")

            for name, src in vec_src.items():
                g, r, k = vec_at[name]
                act.dma_start(VEC[r:r + k, g, :], src).then_inc(vec_in, 16)
            for s, src in enumerate((x, ctx)):
                act.dma_start(XIN[:, 2 * s:2 * s + 2, :], src[0].rearrange("(t p) n -> p t n", p=P)).then_inc(x_in, 16)
            act.dma_start(MIN[0:META, :], meta_2).then_inc(meta_in, 16)
            for dst, src in small_src:
                act.dma_start(dst, src, allow_slow_non_contiguous=True).then_inc(small_in, 16)

            logs()
            act.wait_ge(vector_drained, mark["vec"])
            act.activation(ce, VT[:, 0, 0:16], ACT.Exp, scale=-1.0).then_inc(c_exp, 1)
            act.wait_ge(small_in, 16 * n_small)
            act.activation(alog, alog, ACT.Exp)
            act.activation(salog, salog, ACT.Exp)
            for tt in range(TT):
                for kh in range(2):
                    b = take()
                    drained(act.activation(XC[:, 4 * kh:4 * kh + 4, tt * P:tt * P + P], bank(b, 4, P), ACT.Copy))
            b = take()
            drained(act.activation(XH[:, :, 0:META], bank(b, KD, META), ACT.Copy))

            def rstd(src, nr):
                b = take()
                drained(act.activation(nr, b[:, src], ACT.Ln, bias=EPSC, scale=1.0 / D))
                act.wait_ge(scalar_drained, n["s"])
                act.activation(nr, nr, ACT.Exp, scale=-0.5).then_inc(rstd_ready, 1)

            scaled_tiles = [0]

            def shift(v, by, signal):
                if signal:
                    scaled_tiles[0] += 1
                    act.wait_ge(h_scaled, scaled_tiles[0])
                return act.activation(v, v, ACT.Identity, bias=by)

            def norm(i, names, t0=META, width=T, sq=SQn, nr=NRn, mod=None):
                for m in range(KD):
                    act.wait_ge(vector_drained, mark[names + (m,)])
                    act.activation(sq[:, m, 0:width], XH[:, m, t0:t0 + width], ACT.Square).then_inc(squares_ready, 1)
                rstd(slice(0, width), nr[:, 0:width])
                if mod is not None:
                    ly, piece = mod
                    for k in range(KD):
                        shift(h2T[:, k, :], MOD[:, ly, piece + k, 0:1], True).then_inc(h_ready, 1)

            act.wait_ge(vector_drained, mark["x"])
            act.wait_ge(scalar_drained, n["s"])
            act.activation(SQ1[:, :, 0:T], XH[:, :, META:L2], ACT.Square)
            act.activation(SQ1[:, :, T:2 * T], XC, ACT.Square).then_inc(squares_ready, 1)
            rstd(slice(0, 512), NR1)

            ada = [0]

            def ada_copy():
                b = take()
                if ada[0]:
                    act.wait_ge(vector_filled, mark[("mod", ada[0] - 1)])
                drained(act.activation(PART[:, :], b[:, :], ACT.Copy))
                ada[0] += 1

            for i in range(4):
                ada_copy()

            for k in range(KD):
                shift(hT[:, k, 0:T], MOD[:, 0, k, 0:1], True)
                shift(hT[:, k, T:2 * T], MOD[:, 0, k, 1:2], False).then_inc(h_ready, 1)

            def silu_qkv(t):
                act.wait_ge(conv_out, t + 1)
                v = QT[:, t, :] if t < 4 else KT[:, t - 4, :] if t < 8 else VTf[:, t - 8, :]
                act.activation(v, v, ACT.Silu).then_inc(conv_act, 1)

            for t in range(12):
                b = take()
                w = 1 if t < 4 else 2
                if t < 4:
                    act.wait_ge(edges_ready, 1)
                if t >= 4:
                    act.wait_ge(conv_out, t - 3)
                drained(act.activation(CB[:, t % 4, 0:w, 1:1 + T], bank(b, w, T), ACT.Copy))
                if t >= 1:
                    silu_qkv(t - 1)
            silu_qkv(11)
            for m in range(4):
                b = take()
                drained(act.activation(Z1[:, m, :], b[:, 0:T], ACT.Silu))
            logs()
            act.wait_ge(conv_act, 8)
            act.wait_ge(vector_filled, mark["gates"])
            for i in range(8):
                v = KT[:, i, :] if i < 4 else QT[:, i - 4, :]
                act.activation(l2_buf(i), v, ACT.Square).then_inc(l2_squares, 1)
            for i in range(8):
                w = 2 * T if i < 4 else T
                b = take()
                drained(act.activation(l2_buf(i), b[:, 0:w], ACT.Ln, bias=EPSC))
                act.wait_ge(scalar_drained, n["s"])
                act.activation(l2_buf(i), l2_buf(i), ACT.Exp, scale=-0.5).then_inc(l2_rstd, 1)
            act.wait_ge(gate_args, 1)
            then(act.activation(g_e, g_e, ACT.Exp))
            act.activation(g_e, g_e, ACT.Ln, bias=ONE)
            act.activation(BETA, graw[:, :, 0:8], ACT.Exp, scale=-1.0).then_inc(gate_exps, 1)
            for h in range(HEADS):
                b = take()
                drained(act.activation(Ktok[:, h], bank(b, 4, P), ACT.Copy))
            act.wait_ge(vector_drained, mark["gc"])
            act.activation(EGC, GC, ACT.Exp).then_inc(gam_exps, 1)

            for d in range(2):
                g = 0
                for kind, a, h in mixer_steps(d):
                    if kind == "ada":
                        ada_copy()
                    elif kind == "setup":
                        h = a
                        act.wait_ge(diff_ready, HEADS * d + h + 1)
                        act.activation(Tlo, Tlo, ACT.Exp, scale=-1.0)
                        act.activation(Thi, Thi, ACT.Exp)
                        for u in range(TT):
                            ins = act.activation(Tq[:, u, :], diff[:, u, :], ACT.Exp, bias=GC[:, u, 4 * d + h:4 * d + h + 1])
                        ins.then_inc(decay_exps, 1)
                    elif kind == "turn" and a >= 1:
                        b = take()
                        if g >= 2:
                            act.wait_ge(vector_filled, mark[("grow", d, g - 2)])
                        drained(act.activation(Qs[:, g % 2], bank(b, 4, P), ACT.Copy))
                        g += 1
                    elif kind == "walk" and d == 0 and a >= 2:
                        b = take()
                        u = ORDER[d][a]
                        drained(act.activation(OT[:, :, u * P:u * P + P], bank(b, 4, P), ACT.Copy))

            act.wait_ge(vector_drained, mark[("o", 1, 3)])
            act.dma_start(PW, pool_w[0].rearrange("g c d -> c g d")).then_inc(poolw_in, 16)
            for ly in range(2):
                act.dma_start(RT[:, ly], router[ly].rearrange("(k p) e -> p k e", p=P)).then_inc(router_in, 16)
            act.dma_start(DTW, even_w_in_2[0][:, 4608:4624].rearrange("(k p) n -> p k n", p=P)).then_inc(dtw_in, 16)
            for i in range(2):
                act.activation(OSQ[:, i, :].rearrange("p (h t) -> p h t", h=2), OT[:, 2 * i:2 * i + 2, :], ACT.Square)\
                    .then_inc(ones_ready, 1)
            for i in range(2):
                b = take()
                drained(act.activation(OSQ[:, i, :], b[:, :], ACT.Ln, bias=EPSC, scale=1.0 / P))
                act.wait_ge(scalar_drained, n["s"])
                act.activation(OSQ[:, i, :], OSQ[:, i, :], ACT.Exp, scale=-0.5).then_inc(o_rstd, 1)

            def experts(ly):
                act.wait_ge(sm_args, ly + 1)
                act.activation(AFFT, AFFT, ACT.Exp).then_inc(sm_exps, 1)
                for tt in range(TT):
                    for kh in range(2):
                        b = take()
                        drained(act.activation(H2[:, tt, 512 * kh:512 * kh + 512], b[:, :], ACT.Copy))
                s0 = n["s"]
                with act.Fori(0, GROUPS) as g:
                    def filled(i):
                        act.wait_ge(scalar_filled, g * 4 + (s0 + i + 1))
                        return SB[(s0 + i) % 4]
                    b = filled(0)
                    act.activation(XG[:, 0:4], bank(b, 4, P), ACT.Copy).then_inc(scalar_drained, 1)
                    b = filled(1)
                    act.activation(SG, b[:, :], ACT.Silu).then_inc(scalar_drained, 1)
                    b = filled(2)
                    act.activation(HT[:, 0:2], bank(b, 2, P), ACT.Copy).then_inc(scalar_drained, 1)
                    b = filled(3)
                    act.activation(Y[:, bass.ds(g, 1), 0:512].rearrange("p a n -> p (a n)"), b[:, :], ACT.Copy).then_inc(scalar_drained, 1)
                n["s"] += 4 * GROUPS
                logs()

            norm(1, ("out1",), mod=(0, 24))
            experts(0)
            norm(2, ("combine", 0), mod=(1, 0))
            for m in range(KD):
                b = take()
                drained(act.activation(GCC[:, m, :], b[:, 0:T], ACT.Copy))
            norm(3, ("out2",), mod=(1, 24))
            experts(1)
            act.activation(SQn[:, :, T:L2], XH[:, :, 0:META], ACT.Square).then_inc(squares_ready, 1)
            rstd(slice(0, META), NRn[:, 0:META])
            norm(4, ("combine", 1), nr=NR4)
            act.wait_ge(mean_ready, 1)
            then(act.activation(NRn[:, META:L2], NS5[:, 0:T], ACT.Ln, bias=EPSC, scale=1.0 / D))
            act.activation(NRn[:, META:L2], NRn[:, META:L2], ACT.Exp, scale=-0.5).then_inc(rstd_ready, 1)

            def silu3(t):
                act.wait_ge(conv_out, 12 + t + 1)
                act.activation(XB[:, t, :], XB[:, t, :], ACT.Silu).then_inc(conv_act, 1)

            act.wait_ge(edges_ready, 2)
            for t in range(20):
                b = take()
                if t >= 4:
                    act.wait_ge(conv_out, 12 + t - 3)
                drained(act.activation(CB3[:, t % 4, 3:3 + L2], b[:, 0:L2], ACT.Copy))
                if 1 <= t <= 12:
                    silu3(t - 1)
            act.wait_ge(dt_args, 1)
            logs()
            then(act.activation(DTn, DTn, ACT.Exp))
            then(act.activation(ln8, ln8, ACT.Exp))
            act.activation(DTn, DTn, ACT.Ln, bias=ONE)
            act.activation(ln8, ln8, ACT.Ln, bias=ONE).then_inc(dt_exps, 1)
            def lru_gate_silu(m):
                b = take()
                drained(act.activation(SLG[:, m, :], b[:, 0:L2], ACT.Silu))

            for m in range(4):
                lru_gate_silu(m)
            for m in range(KD):
                for g, (dst, name) in enumerate(((LR, "lru_b_a"), (LI, "lru_b_x"))):
                    b = take()
                    drained(act.activation(dst[:, m, :], b[:, 0:L2], ACT.Sigmoid, bias=vec(name, m)))
            act.wait_ge(scalar_drained, n["s"])
            act.wait_ge(lc_ready, 1)
            for m in range(KD):
                ins = act.activation(LTH[:, m, :], LR[:, m, :], ACT.Tanh, scale=lc8[:, m:m + 1])
            ins.then_inc(tanh_ready, 1)
            act.wait_ge(tanh_ready, 1)
            logs()
            for m in range(KD):
                ins = act.activation(LR[:, m, :], LR[:, m, :], ACT.Exp, scale=lc8[:, m:m + 1])
            act.wait_ge(mult_args, 1)
            then(act.activation(LX, LTH, ACT.Ln, bias=ONE))
            act.activation(LTH, LTH, ACT.Ln, scale=2.0).then_inc(logs_ready, 1)
            act.wait_ge(half_ready, 1)
            act.activation(LTH, LTH, ACT.Exp, scale=0.5).then_inc(mult_ready, 1)
            for m in range(4, KD):
                lru_gate_silu(m)
            for m in range(KD):
                b = take()
                drained(act.activation(SZ[:, m, :], b[:, 0:L2], ACT.Silu))
            logs()
            for i, (_, _, r) in enumerate(SRC):
                for kh in range(2):
                    b = take()
                    drained(act.activation(XTK[0:r, i, 512 * kh:512 * kh + 512], b[0:r, :], ACT.Copy))
            for h in range(SSD_H):
                act.wait_ge(ssd_args, h + 1)
                act.activation(EB[:, h % 3, :], EB[:, h % 3, :], ACT.Exp).then_inc(ssd_exps, 1)
            for g in range(2):
                act.wait_ge(gated, 2)
                act.activation(GSQ[:, 4 * g:4 * g + 4, :], MIX3[:, 8 + 4 * g:12 + 4 * g, :], ACT.Square).then_inc(gate_sq, 1)
            for g in range(2):
                b = take()
                drained(act.activation(GRR[:, g, :], b[:, 0:L2], ACT.Ln, bias=EPSC, scale=1.0 / 512))
                act.wait_ge(scalar_drained, n["s"])
                act.activation(GRR[:, g, :], GRR[:, g, :], ACT.Exp, scale=-0.5).then_inc(gate_rstd, 1)

            norm(6, ("out3",), 0, L2, SQ3)
            for m in range(KD):
                b = take()
                drained(act.activation(QS[:, m, :], b[:, 0:L2], ACT.Copy, scale=64 ** -0.5))
            for m in range(KD):
                b = take()
                drained(act.activation(SGT[:, m, :], b[:, 0:L2], ACT.Silu))

            logs()

            def stick_logs(h):
                b = take()
                act.activation(ZB[:, h % 2, :], b[:, 0:TRI], ACT.Copy)
                drained(act.activation(LB[:, h % 2, :], b[:, 0:TRI], ACT.Abs))
                act.wait_ge(scalar_drained, n["s"])
                then(act.activation(LB[:, h % 2, :], LB[:, h % 2, :], ACT.Exp, scale=-1.0))
                act.activation(LB[:, h % 2, :], LB[:, h % 2, :], ACT.Ln, bias=ONE).then_inc(sb_logs, 1)

            stick_logs(0)
            stick_logs(1)
            for h in range(SB_H):
                act.wait_ge(sb_args, h + 1)
                act.activation(EBS[:, h % 2, :], EBS[:, h % 2, :], ACT.Exp).then_inc(sb_w, 1)
                if h + 2 < SB_H:
                    stick_logs(h + 2)
            norm(7, ("out4",), sq=SQ3)
            for tt in range(TT):
                b = take()
                drained(act.activation(OUTS[:, tt, 512:1024], b[:, :], ACT.Copy))
            assert n["s"] == mark["s_end"]

        @block.vector
        def _(dve):
            n = {"v": 0, "step": 0}

            def take():
                dve.wait_ge(vector_filled, n["v"] + 1)
                return VB[n["v"] % 4]

            def drained(ins, wait=False):
                n["v"] += 1
                ins.then_inc(vector_drained, 1)
                if wait:
                    dve.wait_ge(vector_drained, n["v"])

            def then(ins):
                n["step"] += 1
                ins.then_inc(vector_step, 1)
                dve.wait_ge(vector_step, n["step"])

            def tt(out_, a, b, op):
                return dve.tensor_tensor(out_, a, b, op)

            def stt(out_, a, s, b, op0, op1):
                return dve.scalar_tensor_tensor(out_, a, s, b, op0, op1)

            MUL, ADD, SUB, MAX, MIN = ALU.mult, ALU.add, ALU.subtract, ALU.max, ALU.min

            dve.memset(CS[:, :, :], 0.0)
            b = take()
            for g in range(3):
                ins = dve.tensor_copy(VT[:, g, 0:vec_at[g]], b[:, g * P:g * P + vec_at[g]])
            drained(ins, True)
            tt(gain_sq, vec("norm_final", 0, 8), vec("norm_final", 0, 8), MUL)
            dve.wait_ge(c_exp, 1)
            then(dve.tensor_scalar(ce, ce, 1.0, None, ADD))
            then(dve.reciprocal(ce, ce))
            tt(CS[:, :, 0:2].rearrange("p k r -> p r k"), VT[:, 0, 0:16].rearrange("p (r k) -> p r k", r=2),
               ce.rearrange("p (r k) -> p r k", r=2), MUL).then_inc(c_ready, 1)
            for t_ in range(TT):
                for kh in range(2):
                    b = take()
                    drained(dve.tensor_copy(XH[:, 4 * kh:4 * kh + 4, META + t_ * P:META + t_ * P + P], bank(b, 4, P)))

            ada = [0]

            def ada_bias():
                i = ada[0]
                ly, c0 = i // 12, 4 * (i % 12)
                b = take()
                drained(tt(MOD[:, ly, c0:c0 + 4, :], bank(b, 4, 2), last(vec("ada_b", 48 * ly + c0, 4), 2), ADD))
                ada[0] += 1

            roots = [0]

            def negated_half(src, v):
                return dve.tensor_scalar(v, src, -0.5 / D, -0.5 * EPS, MUL, ADD)

            def newton(v, y, t_):
                roots[0] += 1
                dve.wait_ge(rstd_ready, roots[0])
                then(tt(t_, y, y, MUL))
                then(tt(t_, t_, v, MUL))
                then(stt(y, t_, 1.5, y, ADD, MUL))

            def root(name, width, nv, nr, nt):
                dve.wait_ge(scalar_drained, mark[name])
                negated_half(SB[(mark[name] - 1) % 4][:, 0:width], nv[:, 0:width])
                newton(nv[:, 0:width], nr[:, 0:width], nt[:, 0:width])

            def norm(i, g_name, g_at, t0=META, width=T, mod=None):
                dst = h2T if width == T else hN
                if mod is not None:
                    ly, piece = mod
                    stt(gain[:, :, 0], MOD[:, ly, piece + 8:piece + 16, 0], 1.0, vec(g_name, g_at, 8), ADD, MUL)
                root(("norm", i), width, NVn, NRn, NTn)
                for k in range(KD):
                    g = gain[:, k, 0:1] if mod is not None else vec(g_name, g_at + k)
                    stt(dst[:, k, :], XH[:, k, t0:t0 + width], g, NRn[:, 0:width], MUL, MUL)\
                        .then_inc(h_ready if mod is None else h_scaled, 1)

            root(("norm", 0), 512, NV1, NR1, NT1)
            for i in range(4):
                ada_bias()
            dve.wait_ge(vector_drained, n["v"])
            for r in range(2):
                ins = stt(gain[:, :, r], MOD[:, 0, 8:16, r], 1.0, vec("norm_mix", 0, 8), ADD, MUL)
            then(ins)
            for k in range(KD):
                stt(hT[:, k, 0:T], XH[:, k, META:L2], gain[:, k, 0:1], NR1[:, 0:T], MUL, MUL)
                stt(hT[:, k, T:2 * T], XC[:, k, :], gain[:, k, 1:2], NR1[:, T:2 * T], MUL, MUL).then_inc(h_scaled, 1)
            dve.memset(CB[:, :, :, 0:1], 0.0)
            dve.memset(CB[:, :, :, T + 1:T + 2], 0.0).then_inc(edges_ready, 1)
            dve.memset(PADP, 0.0)

            for t in range(12):
                w = 1 if t < 4 else 2
                dst = QT[:, t, :] if t < 4 else KT[:, t - 4, :] if t < 8 else VTf[:, t - 8, :]
                dst = dst.rearrange("p (s t) -> p s t", s=w)
                src = CB[:, t % 4, 0:w, :]
                dve.wait_ge(scalar_drained, mark[("qkv", t)])
                then(dve.tensor_scalar(dst, src[:, :, 0:T], vec("dn_conv", t), None, MUL))
                then(stt(dst, src[:, :, 1:1 + T], vec("dn_conv", 12 + t), dst, MUL, ADD))
                stt(dst, src[:, :, 2:2 + T], vec("dn_conv", 24 + t), dst, MUL, ADD).then_inc(conv_out, 1)
            for g in range(4):
                b = take()
                drained(dve.tensor_copy(PADP[:, 4 * g:4 * g + 4, 8:72], bank(b, 4, 64)))
            b = take()
            drained(dve.tensor_copy(graw, bank(b, 4, 16)), True)
            then(tt(g_s, graw[:, :, 8:16], mid(dtb, 4), ADD))
            then(dve.tensor_scalar(g_m, g_s, 0.0, None, MAX))
            stt(g_e, g_m, -2.0, g_s, MUL, ADD).then_inc(gate_args, 1)
            for h in range(HEADS):
                b = take()
                drained(dve.tensor_copy(Vtok[:, h], bank(b, 4, P)))
            for i in range(8):
                dve.wait_ge(l2_rstd, i + 1)
                if i < 4:
                    tt(KT[:, i, :], KT[:, i, :], l2_buf(i), MUL).then_inc(l2_done, 1)
                else:
                    stt(QT[:, i - 4, :], QT[:, i - 4, :], float(P) ** -0.5, l2_buf(i), MUL, MUL).then_inc(l2_done, 1)
            dve.wait_ge(gate_exps, 1)
            then(tt(g_m, g_m, g_e, ADD))
            then(dve.tensor_scalar(BETA, BETA, 1.0, None, ADD))
            then(dve.reciprocal(BETA, BETA))
            stt(G, g_m, -1.0, mid(alog, 4), MUL, MUL).then_inc(decay_ready, 1)
            b = take()
            for d in range(2):
                ins = dve.tensor_copy(GC[:, :, 4 * d:4 * d + 4], b[:, 16 * d:16 * d + 16].rearrange("p (u h) -> p u h", u=4))
            drained(ins, True)
            dve.wait_ge(gam_exps, 1)
            then(tt(BG, BETA, EGC, MUL))

            for d in range(2):
                M = (LE, GE)[d]
                lastc = P - 1 if d == 0 else 0
                grow = 0
                for kind, a, h in mixer_steps(d):
                    if kind == "ada":
                        ada_bias()
                    elif kind == "setup":
                        h = a
                        dh = 4 * d + h
                        b = take()
                        drained(tt(diff, bank(b, 4, P), last(GC[:, :, dh], P), SUB), True)
                        dve.tensor_scalar(Tlo, diff, 0.0, None, MAX)
                        dve.tensor_scalar(Thi, diff, 0.0, None, MIN).then_inc(diff_ready, 1)
                        dve.wait_ge(decay_exps, dh + 1)
                        then(dve.tensor_copy(KS[:, h, :], Thi[:, :, lastc]))
                        tt(CDK[:, h, :], KS[:, h, :], EGC[:, :, dh], MUL)
                        b = take()
                        for u in range(UNITS):
                            ins = stt(Am[:, h, u, :], Tlo[:, u, :], BETA[:, u, dh:dh + 1], b[:, u * P:u * P + P], MUL, MUL)
                        drained(ins)
                        then(tt(Thi[:, 0:TT], Thi[:, 0:TT], mid(M[:, :], TT), MUL))
                        b = take()
                        drained(tt(qkT[:, h, :], Thi[:, 0:TT].rearrange("p u j -> p (u j)"), b[:, 0:T], MUL))
                        tt(qdT[:, h, :], QT[:, h, :], Tq.rearrange("p u j -> p (u j)"), MUL).then_inc(tri_ready, 1)
                        dve.wait_ge(tri_ready, dh + 1)
                    elif kind == "turn" and a == 0:
                        i = LEVELS * HEADS * d + h
                        dve.wait_ge(masked, i + 1)
                        tt(Xn[:, h], mid(ident[:, :], 4), Amask[:, i % 2], SUB)
                        b = take()
                        drained(tt(XnT[:, h], mid(ident[:, :], 4), bank(b, 4, P), SUB))
                    elif kind == "grow":
                        b = take()
                        drained(tt(XnT[:, h], XnT[:, h], bank(b, 4, P), SUB))
                        if a < LEVELS - 1:
                            b = take()
                            drained(tt(Xn[:, h], Xn[:, h], bank(b, 4, P), SUB))
                    elif kind == "solve":
                        h = a
                        b = take()
                        b2 = VB[(n["v"] + 1) % 4]
                        dve.wait_ge(vector_filled, n["v"] + 2)
                        drained(dve.tensor_copy(Xn[:, h], bank(b, 4, P)))
                        drained(dve.tensor_copy(XnT[:, h], bank(b2, 4, P)))
                    elif kind == "walk":
                        s, u = a, ORDER[d][a]
                        if s:
                            b = take()
                            drained(tt(Wt, Xn[:, :, u, :], bank(b, 4, P), SUB))
                        if u < TT and d == 1:
                            b = take()
                            o = OT[:, :, u * P:u * P + P]
                            drained(tt(o, o, bank(b, 4, P), ADD))
                        if s < UNITS - 1:
                            b = take()
                            if s == 0:
                                drained(dve.tensor_copy(St, bank(b, 4, P)), True)
                            else:
                                then(tt(St, St, last(CDK[:, :, u], P), MUL))
                                drained(tt(St, St, bank(b, 4, P), ADD), True)

            dve.wait_ge(vector_drained, n["v"])
            then(tt(PTA[:, :, 0:79], PADP[:, :, 0:79], PADP[:, :, 1:80], ADD))
            then(tt(PTB[:, 4:16, 0:77], PTA[:, 4:16, 0:77], PTA[:, 4:16, 2:79], ADD))
            then(tt(PTA[:, 8:16, 0:73], PTB[:, 8:16, 0:73], PTB[:, 8:16, 4:77], ADD))
            then(tt(PTB[:, 12:16, 0:65], PTA[:, 12:16, 0:65], PTA[:, 12:16, 8:73], ADD))
            dve.wait_ge(iota_ready, 4)
            for g in range(4):
                i0, i1 = IOT[:, 0, 64 * g:64 * g + 64], IOT[:, 1, 64 * g:64 * g + 64]
                then(stt(i0, i0, float(2 << g), i1, MIN, MIN))
                then(dve.reciprocal(RCNT[:, g, :], i0))
                src = (PTA, PTB)[g % 2][:, 4 * g:4 * g + 4, 8 - (1 << g):72 - (1 << g)]
                dst = PG[:, g, :].rearrange("p (s t) -> p s t", s=4)
                then(tt(dst, src, mid(RCNT[:, g, :], 4), MUL))
                tt(dst, dst, PADP[:, 4 * g:4 * g + 4, 8:72], SUB).then_inc(pooled_ready, 1)
            for i in range(2):
                dve.wait_ge(o_rstd, i + 1)
                o = OT[:, 2 * i:2 * i + 2, :]
                then(tt(o, o, OSQ[:, i, :].rearrange("p (h t) -> p h t", h=2), MUL))
                stt(MIX1[:, 2 * i:2 * i + 2, :], o, vec("dn_norm"), Z1[:, 2 * i:2 * i + 2, :], MUL, MUL)
            for g in range(4):
                b = take()
                drained(dve.tensor_scalar(MIX1[:, 4 + g, :], b[:, 0:T], vec("pool_scale", g), None, MUL))

            def residual(ly, piece, m):
                b = take()
                xm = XH[:, m, META:L2]
                drained(stt(xm, b[:, 0:T], MOD[:, ly, piece + m, 0:1], xm, MUL, ADD))

            for m in range(KD):
                residual(0, 16, m)

            def experts(ly):
                dve.wait_ge(vector_drained, n["v"])
                norm(1 + 2 * ly, "norm_ffn", 8 * ly, mod=(ly, 24))
                b = take()
                lg = bank(b, 2, 16)
                then(dve.reduce_max(rmax, lg, AX.X))
                drained(tt(AFFT, lg, last(rmax, 16), SUB), True)
                dve.tensor_copy(rsum, rmax).then_inc(sm_args, 1)
                dve.wait_ge(sm_exps, ly + 1)
                then(dve.reduce_sum(rsum, AFFT, AX.X))
                then(dve.reciprocal(rsum, rsum))
                tt(AFFT, AFFT, last(rsum, 16), MUL).then_inc(aff_ready, 1)
                b = take()
                drained(dve.tensor_copy(AT2[0:EXP, :], b[0:EXP, 0:T]), True)
                for r in range(CAP // 8):
                    src = AT2 if r == 0 else WT2
                    then(dve.max(m8[0:EXP, :], src[0:EXP, :]))
                    then(dve.match_replace(out=WT2[0:EXP, :], in_to_replace=m8[0:EXP, :], in_values=src[0:EXP, :], imm_value=-1.0))
                then(dve.tensor_scalar(MT2[0:EXP, :], WT2[0:EXP, :], 0.0, None, ALU.is_lt))
                then(dve.tensor_tensor_scan(PS2[0:EXP, :], WIDE[0:EXP, P:P + 1].broadcast_to([EXP, T]), MT2[0:EXP, :], 0.0, MUL, ADD))
                tt(PS2[0:EXP, :], PS2[0:EXP, :], MT2[0:EXP, :], MUL).then_inc(pos_ready, 1)
                b = take()
                drained(dve.tensor_copy(POS, bank(b, 2, 16)), True)
                for t_ in range(TT):
                    pt = PT[:, t_, :].rearrange("p (e s) -> p e s", e=EXP)
                    then(tt(pt, last(POS[:, t_, :], CAP), mid(SLOTN, EXP), ALU.is_equal))
                    ins = tt(GPT[:, t_, :].rearrange("p (e s) -> p e s", e=EXP), pt, last(AFFT[:, t_, :], CAP), MUL)
                ins.then_inc(pick_ready, 1)
                for gh in range(2):
                    b = take()
                    drained(dve.tensor_copy(CM[:, 2 * gh:2 * gh + 2, :], bank(b, 2, T)))
                v0 = n["v"]
                s0 = mark[("group", ly)][1]
                with dve.Fori(0, GROUPS) as g:
                    def filled(i):
                        dve.wait_ge(vector_filled, g * 4 + (v0 + i + 1))
                        return VB[(v0 + i) % 4]
                    b = filled(0)
                    dve.tensor_copy(XG[:, 4:8], bank(b, 4, P)).then_inc(vector_drained, 1)
                    b = filled(1)
                    dve.wait_ge(scalar_drained, g * 4 + (s0 + 2))
                    tt(HIDD, SG, b[:, :], MUL).then_inc(vector_drained, 1)
                    b = filled(2)
                    dve.tensor_copy(HT[:, 2:4], bank(b, 2, P)).then_inc(vector_drained, 1)
                    b = filled(3)
                    dve.tensor_copy(Y[:, bass.ds(g, 1), 512:1024].rearrange("p a n -> p (a n)"), b[:, :]).then_inc(vector_drained, 1)
                n["v"] += 4 * GROUPS
                if ly == 1:
                    root("meta_norm", META, NVn, NRn, NTn)
                for m in range(KD):
                    residual(ly, 40, m)

            experts(0)

            dve.wait_ge(vector_drained, n["v"])
            norm(2, "norm_mix", 8, mod=(1, 0))
            dve.memset(CPAD[:, :, 0:1], 0.0)
            then(dve.memset(CPAD[:, :, T + 1:T + 2], 0.0))
            for m in range(KD):
                dve.wait_ge(scalar_drained, mark[("gc", m)])
                b = take()
                drained(tt(CPAD[:, m, 1:1 + T], b[:, 0:T], GCC[:, m, :], MUL), True)
                then(dve.tensor_scalar(CO[:, m, :], CPAD[:, m, 0:T], vec("sc_conv", m), None, MUL))
                then(stt(CO[:, m, :], CPAD[:, m, 1:1 + T], vec("sc_conv", 8 + m), CO[:, m, :], MUL, ADD))
                then(stt(CO[:, m, :], CPAD[:, m, 2:2 + T], vec("sc_conv", 16 + m), CO[:, m, :], MUL, ADD))
            for m in range(KD):
                b = take()
                drained(tt(MIX2[:, m, :], b[:, 0:T], CO[:, m, :], MUL))
            for m in range(KD):
                residual(1, 16, m)

            experts(1)

            dve.wait_ge(vector_drained, n["v"])
            dve.memset(CB3[:, :, 0:3], 0.0).then_inc(edges_ready, 1)
            root(("norm", 4), T, NVn, NR4, NTn)
            then(tt(NS5[:, 0:T], NR4[:, 0:T], NR4[:, 0:T], MUL))
            tt(NS5[:, 0:T], NS5[:, 0:T], SB[(mark[("norm", 4)] - 1) % 4][:, T:2 * T], MUL).then_inc(mean_ready, 1)
            for k in range(KD):
                v = XH[:, k, META:L2]
                ins = stt(v, v, vec("norm_final", k), NR4[:, 0:T], MUL, MUL)
            dve.wait_ge(mean_ready, 1)
            then(negated_half(NS5[:, 0:T], NVn[:, 0:T]))
            newton(NVn[:, 0:T], NRn[:, META:L2], NTn[:, 0:T])
            for k in range(KD):
                stt(hN[:, k, :], XH[:, k, :], vec("even_norm", k), NRn[:, 0:L2], MUL, MUL).then_inc(h_ready, 1)
            then(dve.tensor_scalar(lc8, vec("lru_lambda", 0, 8), -1.0, 0.0, MUL, MAX))
            then(stt(ln8, lc8, -2.0, vec("lru_lambda", 0, 8), MUL, SUB))

            for t in range(20):
                dve.wait_ge(scalar_drained, mark[("conv3", t)])
                dst = XB[:, t, :] if t < 12 else LX[:, t - 12, :]
                wn, wt, nt_, m = ("ssd_conv", 12, 12, t) if t < 12 else ("lru_conv", 8, 8, t - 12)
                src = CB3[:, t % 4, :]
                then(dve.tensor_scalar(dst, src[:, 0:L2], vec(wn + "_w", m), vec(wn + "_b", m), MUL, ADD))
                for j in range(1, 4):
                    ins = stt(dst, src[:, j:j + L2], vec(wn + "_w", j * wt + m), dst, MUL, ADD)
                    if j < 3:
                        then(ins)
                ins.then_inc(conv_out, 1)
            dve.memset(CUM, 0.0)
            then(dve.memset(DT3, 0.0))
            b = take()
            dve.tensor_copy(DT3[:, 0:2, :], bank(b, 2, 16))
            drained(dve.tensor_copy(DT3[0:META, 2, :], b[0:META, 32:48]), True)
            then(tt(DT3, DT3, mid(sdtb, 3), ADD))
            then(dve.tensor_scalar(DTm, DT3, 0.0, None, MAX))
            stt(DTn, DTm, -2.0, DT3, MUL, ADD).then_inc(dt_args, 1)
            dve.wait_ge(dt_exps, 1)
            then(tt(DT3, DTm, DTn, ADD))
            stt(ADT, DT3, -1.0, mid(salog, 3), MUL, MUL).then_inc(dt_ready, 1)
            then(tt(lc8, lc8, ln8, ADD))
            dve.tensor_scalar(lc8, lc8, -8.0, None, MUL).then_inc(lc_ready, 1)
            dve.wait_ge(scalar_drained, mark[("lru", KD - 1, 1)])
            then(tt(LI, LI, LX, MUL))
            dve.wait_ge(tanh_ready, 1)
            dve.tensor_scalar(LTH, LTH, -1.0, 1e-18, MUL, MAX).then_inc(mult_args, 1)
            dve.wait_ge(logs_ready, 1)
            tt(LTH, LTH, LX, SUB).then_inc(half_ready, 1)
            dve.wait_ge(mult_ready, 1)
            then(tt(LI, LI, LTH, MUL))
            for m in range(KD):
                ins = dve.tensor_tensor_scan(MIX3[:, m, :], LR[:, m, :], LI[:, m, :], 0.0, MUL, ADD)
            then(ins)
            dve.wait_ge(scalar_drained, mark[("lru_g", KD - 1)])
            tt(MIX3[:, 0:8, :], MIX3[:, 0:8, :], SLG, MUL).then_inc(lru_done, 1)
            b = take()
            dve.tensor_copy(CUM[:, 0:2, :], bank(b, 2, 16))
            drained(dve.tensor_copy(CUM[0:META, 2, :], b[0:META, 32:48]), True)
            dve.wait_ge(iota_ready, 7)
            for g in range(2):
                b = take()
                tt(CBM[:, g, 0:416], b[:, 0:416], MASK3[:, 0:416], MUL)
                drained(tt(CBM[0:META, g, 416:432], b[0:META, 416:432], MASK3[0:META, 416:432], MUL), True)

            def ssd_arg(h):
                b = take()
                e = EB[:, h % 3, :]
                dve.tensor_scalar(e[:, 0:272], b[:, 0:272], CUM[:, 0, h:h + 1], 0.0, SUB, MIN)
                dve.tensor_scalar(e[:, 272:416], b[:, 128:272], CUM[:, 1, h:h + 1], 0.0, SUB, MIN)
                drained(dve.tensor_scalar(e[:, 416:432], b[:, 256:272], CUM[:, 2, h:h + 1], 0.0, SUB, MIN), True)
                dve.tensor_copy(ltm, lc8).then_inc(ssd_args, 1)

            ssd_arg(0)
            ssd_arg(1)
            for h in range(SSD_H):
                g, e = h // 8, EB[:, h % 3, :]
                dve.wait_ge(ssd_exps, h + 1)
                stt(e[:, 0:272], e[:, 0:272], DT3[:, 0, h:h + 1], CBM[:, g, 0:272], MUL, MUL)
                stt(e[:, 272:416], e[:, 272:416], DT3[:, 1, h:h + 1], CBM[:, g, 272:416], MUL, MUL)
                stt(e[0:META, 416:432], e[0:META, 416:432], DT3[0:META, 2, h:h + 1], CBM[0:META, g, 416:432], MUL, MUL)\
                    .then_inc(ssd_w, 1)
                if h + 2 < SSD_H:
                    ssd_arg(h + 2)
                r0, m = 64 * (h % 2), h // 2
                b = take()
                drained(stt(MIX3[r0:r0 + 64, 8 + m, :], XB[r0:r0 + 64, m, :], ssdd[r0:r0 + 64, m:m + 1], b[r0:r0 + 64, 0:L2], MUL, ADD),
                        True)
                if h % 2 == 1:
                    ins = tt(MIX3[:, 8 + m, :], MIX3[:, 8 + m, :], SZ[:, m, :], MUL)
                    if h % 8 == 7:
                        ins.then_inc(gated, 1)
            for g in range(2):
                dve.wait_ge(gate_rstd, g + 1)
                for k in range(4):
                    v = MIX3[:, 8 + 4 * g + k, :]
                    ins = stt(v, v, vec("ssd_norm", 4 * g + k), GRR[:, g, :], MUL, MUL)
            ins.then_inc(mix_ready, 1)
            for m in range(KD):
                b = take()
                drained(tt(XH[:, m, :], b[:, 0:L2], XH[:, m, :], ADD))

            dve.wait_ge(vector_drained, n["v"])
            norm(6, "odd_norm", 0, 0, L2)
            dve.memset(KS2[:, :, L2:384], 0.0)
            for m in range(KD):
                b = take()
                drained(dve.tensor_copy(KS2[:, m, 0:L2], b[:, 0:L2]))
            for m in range(KD):
                b = take()
                drained(dve.tensor_copy(VS[:, m, :], b[:, 0:L2]))
            for i, (_, _, r) in enumerate(SRC):
                for kh in range(2):
                    b = take()
                    drained(dve.tensor_copy(VTK[0:r, i, 512 * kh:512 * kh + 512], b[0:r, :]))
            dve.wait_ge(iota_ready, 8)

            def soft(h):
                dve.wait_ge(sb_logs, h + 1)
                q = PB[:, h % 2, :]
                then(stt(q, ZB[:, h % 2, :], 0.0, LB[:, h % 2, :], MAX, ADD))
                tt(q, q, SMASK, MUL).then_inc(sb_soft, 1)

            def stick_o(h):
                r0, m = 64 * (h % 2), h // 2
                b = take()
                drained(tt(OS[r0:r0 + 64, m, :], b[r0:r0 + 64, 0:L2], SGT[r0:r0 + 64, m, :], MUL))

            soft(0)
            for h in range(SB_H):
                if h + 1 < SB_H:
                    soft(h + 1)
                b = take()
                e = EBS[:, h % 2, :]
                drained(stt(e, b[:, 0:TRI], -1.0, ZB[:, h % 2, :], MUL, ADD), True)
                stt(e, e, 0.0, NEG, MIN, ADD).then_inc(sb_args, 1)
                if h >= 1:
                    stick_o(h - 1)
            stick_o(SB_H - 1)
            for m in range(KD):
                b = take()
                drained(tt(XH[:, m, :], b[:, 0:L2], XH[:, m, :], ADD))
            dve.wait_ge(vector_drained, n["v"])
            norm(7, "final_norm", 0)
            for t_ in range(TT):
                b = take()
                n["v"] += 1
                dve.tensor_copy(OUTS[:, t_, 0:512], b[:, :]).then_inc(out_copied, 1)
            assert n["v"] == mark["v_end"]


_INS = ['x', 'c', 'ctx', 'c_ctx', 'ada_w', 'ada_b', 'norm_mix', 'norm_ffn', 'norm_final', 'ev_w_in', 'dn_conv',
        'dn_a_log', 'dn_dt_bias', 'dn_norm', 'pool_w', 'pool_scale', 'ev_w_out', 'sc_w_in', 'sc_conv', 'sc_w_out',
        'router', 'w_gate', 'w_up', 'w_down', 'meta_2', 'even_norm_2', 'even_w_in_2', 'lru_conv_w_2',
        'lru_conv_b_2', 'lru_w_a_2', 'lru_b_a_2', 'lru_w_x_2', 'lru_b_x_2', 'lru_lambda_2', 'ssd_conv_w_2',
        'ssd_conv_b_2', 'ssd_dt_bias_2', 'ssd_a_log_2', 'ssd_d_2', 'ssd_norm_2', 'even_w_out_2', 'odd_norm_2',
        'odd_w_in_2', 'odd_w_out_2', 'final_norm_2']
_OUTS = [((1, T, D), 'float32')]


def kernel(**inputs):
    import numpy as _np
    import concourse.bacc as _bacc
    from concourse import mybir as _mybir
    from concourse.bass_utils import run_bass_kernel_spmd as _run

    nc = _bacc.Bacc("TRN2", target_bir_lowering=False, num_devices=1)
    arrays, args = {}, []
    for name in _INS:
        a = _np.ascontiguousarray(inputs[name])
        arrays[f"in_{name}_dram"] = a
        args.append(nc.dram_tensor(f"in_{name}_dram", a.shape, _mybir.dt.from_np(a.dtype), kind="ExternalInput").ap())
    for i, (shape, dtype) in enumerate(_OUTS):
        dt = _mybir.dt.from_np(_np.dtype(dtype))
        args.append(nc.dram_tensor(f"out_{i}_dram", shape, dt, kind="ExternalOutput").ap())
    build(nc, *args)
    r = _run(nc, [arrays], core_ids=[0])
    got = tuple(r.results[0][f"out_{i}_dram"] for i in range(len(_OUTS)))
    return got[0]
```

```python
from contextlib import ExitStack

import concourse.bass as bass
from concourse import mybir

F32 = mybir.dt.float32
F32R = mybir.dt.float32r
ALU = mybir.AluOpType
ACT = mybir.ActivationFunctionType
AX = mybir.AxisListType

P = 128
D = 1024
KD = D // P
T = 256
TT = T // P
META = 16
L2 = T + META
HEADS = 4
UNITS = 4
ORDER = ((2, 3, 0, 1), (3, 2, 1, 0))
LEVELS = 7
EXP = 16
CAP = 32
EG = 4
GROUPS = EXP // EG
HID = 512
SSD_H = 16
SB_H = 16
TRI = L2 + (L2 - P) + META
EPS = 1e-6
SLOTS = 4
MOE_SLOTS = 6
CHUNK = 4096
MOE_CHUNKS = 12
SRC = ((0, 0, P), (P, L2, P), (2 * P, L2 + L2 - P, META))


def vector_rows():
    groups = (
        (("c", 8), ("c_ctx", 8), ("ada_b", 96), ("norm_mix", 16)),
        (("norm_ffn", 16), ("norm_final", 8), ("dn_conv", 36), ("dn_norm", 1), ("pool_scale", 4),
         ("sc_conv", 24), ("even_norm", 8), ("odd_norm", 8), ("final_norm", 8), ("ssd_norm", 8)),
        (("lru_conv_w", 32), ("lru_conv_b", 8), ("lru_b_a", 8), ("lru_b_x", 8), ("lru_lambda", 8),
         ("ssd_conv_w", 48), ("ssd_conv_b", 12)),
    )
    at = {}
    for g, rows in enumerate(groups):
        r = 0
        for name, n in rows:
            at[name] = (g, r, n)
            r += n
        at[g] = r
    return at


def mixer_steps(d):
    steps = [("gamma", 0, 0)]
    for h in range(HEADS):
        if h + 1 < HEADS:
            steps += [("gamma", h + 1, 0)]
        steps += [("setup", h, 0)]
        if h % 2 == 1:
            steps += [("ada", 0, 0)]
    for lv in range(LEVELS):
        for h in range(HEADS + 1):
            if h < HEADS:
                steps += [("turn", lv, h)]
            if h >= 1 and lv >= 1:
                steps += [("grow", lv, h - 1)]
            if h == 1:
                steps += [("ada", 0, 0)]
    for h in range(HEADS):
        steps += [("solve", h, 0)]
    for s in range(UNITS):
        steps += [("walk", s, 0)]
        if s == 1:
            steps += [("ada", 0, 0)]
    return steps


def build(nc, x, c, ctx, c_ctx, ada_w, ada_b, norm_mix, norm_ffn, norm_final, ev_w_in, dn_conv,
          dn_a_log, dn_dt_bias, dn_norm, pool_w, pool_scale, ev_w_out, sc_w_in, sc_conv, sc_w_out,
          router, w_gate, w_up, w_down, meta_2, even_norm_2, even_w_in_2, lru_conv_w_2,
          lru_conv_b_2, lru_w_a_2, lru_b_a_2, lru_w_x_2, lru_b_x_2, lru_lambda_2, ssd_conv_w_2,
          ssd_conv_b_2, ssd_dt_bias_2, ssd_a_log_2, ssd_d_2, ssd_norm_2, even_w_out_2,
          odd_norm_2, odd_w_in_2, odd_w_out_2, final_norm_2, out):
    stack = ExitStack()
    with stack:
        def sb(name, shape, dt=F32):
            return stack.enter_context(nc.sbuf_tensor(name, shape, dt))

        def sem(name):
            return stack.enter_context(nc.semaphore(name))

        ring = sb("weight_ring", [P, SLOTS, CHUNK])
        XH = sb("residual", [P, KD, L2])
        VT = sb("vectors", [P, 3, P])
        WIDE = sb("upper_then_ones", [P, L2])
        GE = sb("lower_incl", [P, P])
        ident = sb("ident", [P, P])
        SEL = sb("select_stream", [P, 2])
        CS = sb("silu_c", [P, 2 * KD + 30])
        WHI, WLO = (sb(f"weights_{part}", [P, 2, KD, P], F32R) for part in ("high", "low"))
        XHI, XLO = (sb(f"input_{part}", [P, KD, L2], F32R) for part in ("high", "low"))
        PART = sb("ada_partials", [P, 512])
        MOD = sb("modulation", [P, 2, 48, 2])
        GW = sb("gates_w", [P, KD, 16])
        SMALL = sb("small", [P, 700])
        A = sb("arena", [P, 23696])
        LE = WIDE[:, 0:P]
        ONES = WIDE[:, P:2 * P]
        ONE = WIDE[:, P:P + 1]
        EPSC = SMALL[:, 0:1]
        banks = [stack.enter_context(nc.psum_tensor(f"bank{i}", [P, 512], F32)) for i in range(8)]
        VB, SB = banks[0:4], banks[4:8]

        def at(off, *dims):
            n = 1
            for s in dims:
                n *= s
            v = A[:, off:off + n]
            if len(dims) == 2:
                return v.rearrange("p (a b) -> p a b", a=dims[0])
            if len(dims) == 3:
                return v.rearrange("p (a b c) -> p a b c", a=dims[0], b=dims[1])
            return v

        small_used = [1]

        def small(*dims):
            n = 1
            for s in dims:
                n *= s
            v = SMALL[:, small_used[0]:small_used[0] + n]
            small_used[0] += n
            assert small_used[0] <= 700, small_used
            if len(dims) == 2:
                return v.rearrange("p (a b) -> p a b", a=dims[0])
            if len(dims) == 3:
                return v.rearrange("p (a b c) -> p a b c", a=dims[0], b=dims[1])
            return v

        def bank(b, *dims):
            n = 1
            for s in dims:
                n *= s
            v = b[:, 0:n]
            if len(dims) == 2:
                return v.rearrange("p (a b) -> p a b", a=dims[0])
            if len(dims) == 3:
                return v.rearrange("p (a b c) -> p a b c", a=dims[0], b=dims[1])
            return v

        def mid(v, n):
            return v.unsqueeze(1).broadcast_to([v.shape[0], n, v.shape[1]])

        def last(v, n):
            return v.unsqueeze(len(v.shape)).broadcast_to(list(v.shape) + [n])

        vec_at = vector_rows()

        def vec(name, i=0, n=1):
            g, r, _ = vec_at[name]
            return VT[:, g, r + i:r + i + n]

        dtb, alog, sdtb, salog, ssdd = small(8), small(8), small(16), small(16), small(8)
        graw = small(4, 16)
        g_s, g_m, g_e = small(4, 8), small(4, 8), small(4, 8)
        BETA, G, GC, EGC, BG = small(4, 8), small(4, 8), small(4, 8), small(4, 8), small(4, 8)
        KS, CDK = small(4, 4), small(4, 4)
        ce, gain, gain_sq = small(16), small(8, 2), small(8)
        AFFT, POS = small(2, 16), small(2, 16)
        rmax, rsum, m8, SLOTN = small(2), small(2), small(8), small(32)
        lc8, ln8 = small(8), small(8)

        hT = at(0, 8, 512)
        KT = at(4096, 4, 512)
        VTf = at(6144, 4, 512)
        QT = at(8192, 4, 256)
        Z1 = at(9216, 4, 256)
        PADP = at(10240, 16, 80)
        Ktok, Vtok = at(11520, 4, 4, 128), at(13568, 4, 4, 128)
        OT = at(15616, 4, 256)
        CB = at(16640, 4, 2, 258)
        Xn, XnT = at(0, 4, 4, 128), at(2048, 4, 4, 128)
        Am = at(16640, 4, 4, 128)
        Amask = at(18704, 2, 4, 128)
        Qs = at(19728, 2, 4, 128)
        qdT, qkT = at(20752, 4, 256), at(21776, 4, 256)
        St, Wt = at(19728, 4, 128), at(20240, 4, 128)
        decay_bufs = [(at(o, 4, 128), at(o + 512, 4, 128), at(o + 1024, 4, 128), at(o + 1536, 2, 128)) for o in (6144, 0)]
        KBG, BV = at(6144, 2, 4, 128), at(7168, 2, 4, 128)
        LM = A[:, 22800:22800 + 896].bitcast(mybir.dt.bfloat16).rearrange(
            "p (d l j) -> p d l j", d=2, l=7)
        XIN = at(8192, 4, 1024)
        XC = at(12288, 8, 256)
        MIN = at(14336, 1024)
        SQ1 = at(16640, 8, 512)
        VEC = at(22272, 3, 128)
        NR1, NV1, NT1 = at(20736, 512), at(21248, 512), at(21760, 512)
        L2S = at(18704, 6, 512)
        OSQ = at(0, 2, 512)
        PTA, PTB = at(21776, 4, 80), at(22096, 4, 80)
        RCNT, IOT = at(17152, 4, 64), at(16640, 2, 256)
        MIX1 = at(4096, 8, 256)
        PW = at(18704, 4, 128)

        h2T, H2 = at(0, 8, 256), at(2048, 2, 1024)
        PT, GPT, CM = at(4096, 2, 512), at(5120, 2, 512), at(6144, 4, 256)
        XG = at(7168, 8, 128)
        HIDD, SG = at(8192, 512), at(8704, 512)
        HT, Y = at(9216, 4, 128), at(9728, 4, 1024)
        AT2, WT2, MT2, PS2 = at(13824, 256), at(14080, 256), at(14336, 256), at(14592, 256)
        RT = at(14848, 2, 8, 16)
        SQn = at(7168, 8, 272)
        NRn, NVn, NTn = at(2304, 272), at(2576, 272), at(2848, 272)
        NR4, NS5 = at(3120, 272), at(3392, 272)
        arena_slots = [at(15504 + CHUNK * i, CHUNK) for i in range(MOE_SLOTS - SLOTS)]
        SQ3 = at(2176, 8, 272)
        NR6, NV6, NT6 = at(17536, 272), at(17808, 272), at(18080, 272)
        GCC, CPAD, CO, MIX2 = at(2048, 8, 256), at(4096, 8, 258), at(6200, 8, 256), at(8300, 8, 256)

        hN = at(0, 8, 272)
        LX, SLG, SZ, XB = at(2176, 8, 272), at(4352, 8, 272), at(6528, 8, 272), at(8704, 12, 272)
        MIX3 = at(11968, 16, 272)
        LR, LI, LTH = at(14144, 8, 272), at(16320, 8, 272), at(18496, 8, 272)
        XTK = at(16320, 3, 1024)
        EB, CBM = at(19392, 3, 432), at(20688, 2, 432)
        CB3 = at(21120, 4, 275)
        CUM, DT3, ADT, DTm, DTn = (at(22220 + 48 * i, 3, 16) for i in range(5))
        MASK3, DTW = at(22460, 432), at(22892, 8, 16)
        GSQ, GRR = at(2176, 8, 272), at(4352, 2, 272)
        QS, KS2, VS = at(2176, 8, 272), at(4352, 8, 384), at(7424, 8, 272)
        VTK, SGT, OS = at(9600, 3, 1024), at(12672, 8, 272), at(14848, 8, 272)
        ZB, LB, PB, EBS = at(21344, 3, 432), at(17024, 3, 432), at(18320, 2, 432), at(19184, 2, 432)
        SMASK, NEG = at(20480, 432), at(20912, 432)
        OUTS = at(2176, 2, 1024)
        vec_src = {"c": c.rearrange("a (r p) -> (a r) p", p=P), "c_ctx": c_ctx.rearrange("(r p) -> r p", p=P),
                   "ada_b": ada_b.rearrange("l (r p) -> (l r) p", p=P),
                   "norm_mix": norm_mix.rearrange("l (r p) -> (l r) p", p=P),
                   "norm_ffn": norm_ffn.rearrange("l (r p) -> (l r) p", p=P),
                   "norm_final": norm_final.rearrange("(r p) -> r p", p=P),
                   "dn_conv": dn_conv.rearrange("o t (r p) -> (o t r) p", p=P),
                   "dn_norm": dn_norm, "pool_scale": pool_scale.rearrange("o (r p) -> (o r) p", p=P),
                   "sc_conv": sc_conv.rearrange("o t (r p) -> (o t r) p", p=P),
                   "even_norm": even_norm_2.rearrange("o (r p) -> (o r) p", p=P),
                   "odd_norm": odd_norm_2.rearrange("o (r p) -> (o r) p", p=P),
                   "final_norm": final_norm_2.rearrange("(r p) -> r p", p=P),
                   "ssd_norm": ssd_norm_2.rearrange("o (r p) -> (o r) p", p=P),
                   "lru_conv_w": lru_conv_w_2.rearrange("o t (r p) -> (o t r) p", p=P),
                   "lru_conv_b": lru_conv_b_2.rearrange("o (r p) -> (o r) p", p=P),
                   "lru_b_a": lru_b_a_2.rearrange("o (r p) -> (o r) p", p=P),
                   "lru_b_x": lru_b_x_2.rearrange("o (r p) -> (o r) p", p=P),
                   "lru_lambda": lru_lambda_2.rearrange("o (r p) -> (o r) p", p=P),
                   "ssd_conv_w": ssd_conv_w_2.rearrange("o t (r p) -> (o t r) p", p=P),
                   "ssd_conv_b": ssd_conv_b_2.rearrange("o (r p) -> (o r) p", p=P)}
        first_vecs = ("c", "c_ctx", "ada_b", "norm_mix")
        n_vec = len(vec_src)
        small_src = [
            (GW[:, :, :], ev_w_in[0][:, 2048:2064].rearrange("(k p) n -> p k n", p=P)),
            (dtb, dn_dt_bias.rearrange("o d h -> o (d h)").broadcast_to([P, 8])),
            (alog, dn_a_log.rearrange("o d h -> o (d h)").broadcast_to([P, 8])),
            (sdtb, ssd_dt_bias_2.broadcast_to([P, 16])),
            (salog, ssd_a_log_2.broadcast_to([P, 16])),
            (ssdd[0:64], ssd_d_2.rearrange("o (m j) -> o m j", j=2)[:, :, 0].broadcast_to([64, 8])),
            (ssdd[64:P], ssd_d_2.rearrange("o (m j) -> o m j", j=2)[:, :, 1].broadcast_to([64, 8])),
        ]
        n_small = len(small_src)

        landed = [sem(f"weights_landed_{i}") for i in range(MOE_SLOTS)]
        weights_used = sem("weights_used")
        vector_filled, vector_drained = sem("vector_bank_filled"), sem("vector_bank_drained")
        scalar_filled, scalar_drained = sem("scalar_bank_filled"), sem("scalar_bank_drained")
        vector_step, scalar_step, pool_step = sem("vector_step"), sem("scalar_step"), sem("pool_step")
        first_vec_in, vec_in, x_in, small_in, meta_in = sem("first_vectors_in"), sem("vectors_in"), sem("x_in"), sem("small_in"), sem("meta_in")
        router_in, poolw_in, dtw_in = sem("router_in"), sem("pool_w_in"), sem("dt_w_in")
        consts_ready = sem("constants_ready")
        c_exp, c_ready = sem("c_exp"), sem("silu_c_ready")
        squares_ready, rstd_ready, h_ready = sem("squares_ready"), sem("rstd_ready"), sem("h_ready")
        weights_high, weights_split, input_split = sem("weights_high_part"), sem("weights_split"), sem("input_split")
        h_scaled, mean_ready = sem("h_scaled"), sem("second_mean_ready")
        conv_out, conv_act = sem("conv_out"), sem("conv_activated")
        l2_squares, l2_rstd, l2_done = sem("l2_squares"), sem("l2_rstd"), sem("l2_done")
        gate_args, gate_exps, decay_ready = sem("gate_args"), sem("gate_exps"), sem("decay_ready")
        gam_exps = sem("gamma_exps")
        diff_ready, decay_exps, tri_ready = sem("diff_ready"), sem("decay_exps"), sem("triangle_ready")
        masked, scaled, kdec_ready = sem("level_masked"), sem("scaled_keys_values"), sem("kdec_ready")
        ones_ready = sem("norm_out_ready")
        iota_ready = sem("iota_ready")
        sm_args, sm_exps, aff_ready = sem("softmax_args"), sem("softmax_exps"), sem("affinity_ready")
        pooled_ready = sem("pooled_ready")
        pos_ready, pick_ready = sem("positions_ready"), sem("picks_ready")
        tanh_ready, logs_ready = sem("lru_tanh_ready"), sem("lru_logs_ready")
        lc_ready, half_ready = sem("lru_decay_scale_ready"), sem("lru_half_log_ready")
        gate_silus, tokens_scaled = sem("lru_gate_silus"), sem("ssd_tokens_scaled")
        mult_ready = sem("lru_mult_ready")
        dt_args, dt_exps, dt_ready = sem("dt_args"), sem("dt_exps"), sem("dt_ready")
        ssd_args, ssd_exps, ssd_w = sem("ssd_args"), sem("ssd_exps"), sem("ssd_weights_ready")
        gated, gate_sq, gate_rstd = sem("gated_ready"), sem("gated_squares"), sem("gated_rstd")
        sb_logs, sb_soft = sem("stick_logs"), sem("stick_softplus_ready")
        sb_args, sb_w = sem("stick_args"), sem("stick_weights_ready")
        o_rstd, edges_ready, lru_done, mult_args = sem("out_rstd"), sem("edges_ready"), sem("lru_done"), sem("mult_args")
        out_copied, out_done = sem("out_copied"), sem("out_done")

        def cols(w, c0, n=512):
            return ("cols", w[:, c0:c0 + n].rearrange("(k p) n -> p k n", p=P), n)

        stream = [cols(ada_w[0], 512 * i) for i in range(4)]
        W_EV = len(stream)
        ev = ev_w_in[0]
        QKV = 3 * 512
        stream += [cols(ev, 0), cols(ev, 512), cols(ev, 1024), cols(ev, QKV), cols(ev, QKV + 512 + 16)]
        W_ADA = len(stream)
        stream += [cols(ada_w[0], 512 * i) for i in range(4, 12)] + [cols(ada_w[1], 512 * i) for i in range(12)]
        W_EVO = len(stream)
        stream += [cols(ev_w_out[0], 0), cols(ev_w_out[0], 512)]
        W_MOE = [len(stream)]
        stream += [("moe", 0, None)] * (MOE_CHUNKS * GROUPS)
        W_SC = len(stream)
        sc = sc_w_in[0]
        stream += [cols(sc, o) for o in (1024, 2048, 1536, 2560, 0, 512)]
        stream += [cols(sc_w_out[0], 0), cols(sc_w_out[0], 512)]
        W_MOE.append(len(stream))
        stream += [("moe", 1, None)] * (MOE_CHUNKS * GROUPS)
        W_E2 = len(stream)
        e2 = even_w_in_2[0]
        stream += [cols(e2, 3072 + 512 * i) for i in range(3)] + [cols(e2, 0), cols(e2, 512), cols(e2, 1024)]
        W_LRU = len(stream)
        stream += [("lru", None, None)]
        stream += [cols(e2, 1536), cols(e2, 2048), cols(e2, 2560)]
        W_E2O = len(stream)
        stream += [cols(even_w_out_2[0][r:r + D], c0) for r in (0, D) for c0 in (0, 512)]
        W_OD = len(stream)
        stream += [cols(odd_w_in_2[0], 512 * i) for i in range(8)]
        stream += [cols(odd_w_out_2[0], 0), cols(odd_w_out_2[0], 512)]

        def slot_of(cn):
            if stream[cn][0] == "moe":
                return (cn - W_MOE[stream[cn][1]]) % MOE_SLOTS
            return (cn - (W_MOE[0] if cn < W_MOE[0] else W_MOE[1] if cn < W_MOE[1] else W_E2)) % SLOTS

        def slot(cn):
            i = slot_of(cn)
            return ring[:, i, :] if i < SLOTS else arena_slots[i - SLOTS]

        def landed_at(cn):
            return sum(32 if c_ == W_LRU else 16 for c_ in range(cn + 1) if slot_of(c_) == slot_of(cn))

        def l2_buf(i):
            return L2S[:, i, :] if i < 4 else L2S[:, 4 + (i - 4) // 2, (i % 2) * T:(i % 2) * T + T]

        def chunk(n, k=8, w=512):
            return slot(n).rearrange("p (k w) -> p k w", k=k)

        def h_count(i, k=KD):
            return KD * (i - (i > 4)) + k

        def sq_count(i, k=KD):
            return 1 + KD * (i - 1 - (i > 4)) + (i >= 4) + k if i else 1

        released = {}
        mark = {}

        quarters = []

        block = stack.enter_context(nc.Block())

        @block.tensor
        def _(pe):
            n = {"v": 0, "s": 0, "used": 0, "inputs": 0}

            def v_open():
                if n["v"] >= 4:
                    pe.wait_ge(vector_drained, n["v"] - 3)
                return VB[n["v"] % 4]

            def s_open():
                if n["s"] >= 4:
                    pe.wait_ge(scalar_drained, n["s"] - 3)
                return SB[n["s"] % 4]

            def v_close(mm, name=None):
                mm.then_inc(vector_filled, 1)
                n["v"] += 1
                mark[name] = n["v"]
                return n["v"]

            def s_close(mm, name=None):
                mm.then_inc(scalar_filled, 1)
                n["s"] += 1
                mark[name] = n["s"]
                return n["s"]

            def arrive(c):
                pe.wait_ge(landed[slot_of(c)], landed_at(c))

            def transposes(b, pieces):
                for dst, src in pieces:
                    k = src.shape[0]
                    mm = pe.transpose(dst, src, ident[0:k, 0:k])
                return mm

            pe.wait_ge(consts_ready, 1)
            def vec_transposes(tiles, name):
                b = v_open()
                for g in tiles:
                    mm = pe.transpose(b[:, g * P:g * P + vec_at[g]], VEC[0:vec_at[g], g, :],
                                      ident[0:vec_at[g], 0:vec_at[g]])
                v_close(mm, name)

            pe.wait_ge(first_vec_in, 16 * len(first_vecs))
            vec_transposes((0,), "vec")
            pe.wait_ge(x_in, 32)
            for tt in range(TT):
                for kh in range(2):
                    b = v_open()
                    for k in range(4):
                        mm = pe.transpose(b[:, k * P:k * P + P], XIN[:, tt, (4 * kh + k) * P:(4 * kh + k + 1) * P], ident[:, :])
                    v_close(mm, "x")
                    b = s_open()
                    for k in range(4):
                        mm = pe.transpose(b[:, k * P:k * P + P], XIN[:, 2 + tt, (4 * kh + k) * P:(4 * kh + k + 1) * P], ident[:, :])
                    s_close(mm, "ctx")

            ada = {"next": 0, "turned": 0}

            def ada_mm():
                i = ada["next"]
                cn = i if i < 4 else W_ADA + i - 4
                arrive(cn)
                w = chunk(cn)
                if i == 0:
                    pe.wait_ge(c_ready, 1)
                b = s_open()
                for k in range(KD):
                    j = 32 * (k % 4)
                    mm = pe.matmul(b[j:j + 32, :], CS[:, 2 * k:2 * k + 32], w[:, k, :], start=k < 4, stop=k >= 4)
                ada["copied"] = s_close(mm, ("ada", i))
                released[cn] = (scalar_filled, n["s"])
                ada["next"] += 1

            def ada_turn():
                b = v_open()
                for f in range(4):
                    mm = pe.matmul(b[:, 2 * f:2 * f + 2], PART[:, f * P:f * P + P], SEL[:, :], start=True, stop=True)
                v_close(mm, ("mod", ada["turned"]))
                ada["turned"] += 1

            def norm_part(i, k, width, sq):
                if k == 0:
                    norm_part.bank = s_open()
                b = norm_part.bank
                pe.wait_ge(squares_ready, sq_count(i, k + 1))
                mm = pe.matmul(b[:, 0:width], ONES, sq[:, k, 0:width], start=k == 0, stop=k == KD - 1 and i != 4)
                if i == 4:
                    mm = pe.matmul(b[:, T:2 * T], gain_sq[:, k:k + 1].broadcast_to([P, P]), sq[:, k, 0:width],
                                   start=False, stop=k == KD - 1)
                if k == KD - 1:
                    s_close(mm, ("norm", i))

            for k in range(KD):
                norm_part(0, k, 512, SQ1)
            for i in range(4):
                if i == 3:
                    pe.wait_ge(vector_drained, mark[("mod", 0)])
                ada_mm()
                if i >= 1:
                    pe.wait_ge(scalar_drained, ada["copied"] - 1)
                    ada_turn()
            pe.wait_ge(scalar_drained, ada["copied"])
            ada_turn()

            pe.wait_ge(meta_in, 16)
            b = s_open()
            for k in range(KD):
                mm = pe.transpose(b[:, k * META:(k + 1) * META], MIN[0:META, k * P:(k + 1) * P], ident[0:META, 0:META])
            s_close(mm, "meta")

            pe.wait_ge(vec_in, 16 * (n_vec - len(first_vecs)))
            vec_transposes((1, 2), "more_vecs")

            def project(cn, mt, rhs_of, width, opener, closer, names, norm=None):
                arrive(cn)
                w = chunk(cn)
                for m in range(4):
                    b = opener()
                    for k in range(KD):
                        if norm is not None and m == 0:
                            pe.wait_ge(h_ready, h_count(norm, k + 1))
                        mm = pe.matmul(b[:, 0:width], w[:, k, m * P:m * P + P], rhs_of(k), start=k == 0, stop=k == KD - 1)
                    closer(mm, (names, mt + m))
                released[cn] = (scalar_filled, n["s"]) if closer is s_close else (vector_filled, n["v"])

            def product(cn, mt, width, opener, closer, names, new_input=False, after=None):
                n["inputs"] += new_input
                for m in range(4):
                    j = len(quarters)
                    pe.wait_ge(weights_split, j + 1)
                    b = opener()
                    hi, lo = WHI[:, j % 2], WLO[:, j % 2]
                    for k in range(KD):
                        if m == 0 and new_input:
                            pe.wait_ge(input_split, KD * (n["inputs"] - 1) + k + 1)
                        pe.matmul(b[:, 0:width], hi[:, k, :], XHI[:, k, 0:width], start=k == 0, stop=False)
                        pe.matmul(b[:, 0:width], hi[:, k, :], XLO[:, k, 0:width], start=False, stop=False)
                        mm = pe.matmul(b[:, 0:width], lo[:, k, :], XHI[:, k, 0:width], start=False, stop=k == KD - 1)
                    done = closer(mm, (names, mt + m))
                    quarters.append((cn, m, scalar_filled if closer is s_close else vector_filled, done))
                    if after is not None:
                        after(mt + m)
                released[cn] = (weights_split, len(quarters))

            project(W_EV, 0, lambda k: hT[:, k, 0:T], T, s_open, s_close, "qkv", norm=0)
            project(W_EV + 1, 4, lambda k: hT[:, k, :], 2 * T, s_open, s_close, "qkv")
            project(W_EV + 2, 8, lambda k: hT[:, k, :], 2 * T, s_open, s_close, "qkv")
            project(W_EV + 3, 0, lambda k: hT[:, k, 0:T], T, s_open, s_close, "z")
            def l2_sum(i):
                w = 2 * T if i < 4 else T
                pe.wait_ge(l2_squares, i + 1)
                b = s_open()
                mm = pe.matmul(b[:, 0:w], ONES, l2_buf(i), start=True, stop=True)
                s_close(mm, ("l2", i))

            for i in range(4):
                l2_sum(i)
            project(W_EV + 4, 0, lambda k: hT[:, k, 0:T], T, v_open, v_close, "pool")
            for i in range(4, 8):
                l2_sum(i)
            pe.wait_ge(small_in, 16 * n_small)
            b = v_open()
            for u in range(UNITS):
                for k in range(KD):
                    mm = pe.matmul(b[:, 16 * u:16 * u + 16], hT[:, k, u * P:u * P + P], GW[:, k, :],
                                   start=k == 0, stop=k == KD - 1)
            v_close(mm, "gates")

            for h in range(HEADS):
                pe.wait_ge(conv_act, 9 + h)
                b = v_open()
                for u in range(UNITS):
                    mm = pe.transpose(b[:, u * P:u * P + P], VTf[:, h, u * P:u * P + P], ident[:, :])
                v_close(mm, ("vtok", h))
            for h in range(HEADS):
                pe.wait_ge(l2_done, h + 1)
                b = s_open()
                for u in range(UNITS):
                    mm = pe.transpose(b[:, u * P:u * P + P], KT[:, h, u * P:u * P + P], ident[:, :])
                s_close(mm, ("ktok", h))
            pe.wait_ge(decay_ready, 1)
            b = v_open()
            for d in range(2):
                mm = pe.matmul(b[:, 16 * d:16 * d + 16], (LE, GE)[d][:, :], G[:, :, 4 * d:4 * d + 4], start=True, stop=True)
            v_close(mm, "gc")

            for d in range(2):
                M = (LE, GE)[d]
                xt_at, x_at, qs_at = {}, {}, {}
                turn, grow = 0, 0
                for kind, a, h in mixer_steps(d):
                    if kind == "ada":
                        if ada["turned"] < ada["next"]:
                            pe.wait_ge(scalar_drained, ada["copied"])
                            ada_turn()
                        ada_mm()
                    elif kind == "gamma":
                        h = a
                        b = v_open()
                        for u in range(UNITS):
                            mm = pe.matmul(b[:, u * P:u * P + P], G[:, u, 4 * d + h:4 * d + h + 1].broadcast_to([P, P]),
                                           M[:, :], start=True, stop=True)
                        v_close(mm, ("gamma", d, h))
                    elif kind == "setup":
                        h = a
                        if d == 0 and h == 0:
                            pe.wait_ge(l2_done, 8)
                        b = v_open()
                        for u in range(UNITS):
                            kt = KT[:, h, u * P:u * P + P]
                            mm = pe.matmul(b[:, u * P:u * P + P], kt, kt, start=True, stop=True)
                        v_close(mm, ("kk", d, h))
                        b = v_open()
                        for u in range(TT):
                            mm = pe.matmul(b[:, u * P:u * P + P], KT[:, h, u * P:u * P + P], QT[:, h, u * P:u * P + P],
                                           start=True, stop=True)
                        v_close(mm, ("qk", d, h))
                    elif kind == "turn":
                        lv, i = a, LEVELS * HEADS * d + turn
                        pe.wait_ge(masked, i + 1)
                        if lv:
                            pe.wait_ge(vector_drained, xt_at[h])
                        b = v_open() if lv == 0 else s_open()
                        for u in range(UNITS):
                            mm = pe.matmul(b[:, u * P:u * P + P], Amask[:, i % 2, u, :],
                                           XnT[:, h, u, :] if lv else ident[:, :], start=True, stop=True)
                        if lv == 0:
                            xt_at[h] = x_at[h] = v_close(mm, ("turn", d, turn))
                        else:
                            qs_at[h] = s_close(mm, ("turn", d, turn))
                        turn += 1
                    elif kind == "grow":
                        lv = a
                        pe.wait_ge(scalar_drained, qs_at[h])
                        pe.wait_ge(vector_drained, x_at[h])
                        q = Qs[:, grow % 2]
                        b = v_open()
                        for u in range(UNITS):
                            mm = pe.matmul(b[:, u * P:u * P + P], Xn[:, h, u, :], q[:, u, :], start=True, stop=True)
                        xt_at[h] = v_close(mm, ("grow", d, grow))
                        if lv < LEVELS - 1:
                            b = v_open()
                            for u in range(UNITS):
                                mm = pe.matmul(b[:, u * P:u * P + P], q[:, u, :], Xn[:, h, u, :], start=True, stop=True)
                            x_at[h] = v_close(mm, ("grow", d, grow))
                        grow += 1
                    elif kind == "solve":
                        h = a
                        pe.wait_ge(scaled, HEADS * d + h + 1)
                        pe.wait_ge(vector_drained, xt_at[h])
                        b = v_open()
                        for u in range(UNITS):
                            mm = pe.matmul(b[:, u * P:u * P + P], XnT[:, h, u, :], BV[:, h % 2, u, :], start=True, stop=True)
                        v_close(mm)
                        b = v_open()
                        for u in range(UNITS):
                            mm = pe.matmul(b[:, u * P:u * P + P], KBG[:, h % 2, u, :], XnT[:, h, u, :], start=True, stop=True)
                        v_close(mm, ("solve", d, h))
                    elif kind == "walk":
                        s = a
                        u = ORDER[d][s]
                        if s == 0:
                            pe.wait_ge(vector_drained, n["v"])
                            pe.wait_ge(kdec_ready, HEADS * (d + 1))
                        else:
                            pe.wait_ge(vector_drained, state_at)
                            b = v_open()
                            for h in range(HEADS):
                                mm = pe.matmul(b[:, h * P:h * P + P], XnT[:, h, u, :], St[:, h, :], start=True, stop=True)
                            pe.wait_ge(vector_drained, v_close(mm, ("w", d, s)))
                        if u < TT:
                            b = s_open() if d == 0 else v_open()
                            for h in range(HEADS):
                                pe.matmul(b[:, h * P:h * P + P], St[:, h, :], qdT[:, h, u * P:u * P + P], start=True, stop=False)
                                mm = pe.matmul(b[:, h * P:h * P + P], Wt[:, h, :], qkT[:, h, u * P:u * P + P], start=False, stop=True)
                            (s_close if d == 0 else v_close)(mm, ("o", d, s))
                        if s < UNITS - 1:
                            b = v_open()
                            for h in range(HEADS):
                                mm = pe.matmul(b[:, h * P:h * P + P], Am[:, h, u, :], Wt[:, h, :] if s else Xn[:, h, u, :],
                                               start=True, stop=True)
                            state_at = v_close(mm, ("state", d, s))
            pe.wait_ge(scalar_drained, ada["copied"])
            ada_turn()
            assert ada["turned"] == 24

            for i in range(2):
                pe.wait_ge(ones_ready, i + 1)
                b = s_open()
                mm = pe.matmul(b[:, :], ONES, OSQ[:, i, :], start=True, stop=True)
                s_close(mm, ("onorm", i))
            pe.wait_ge(poolw_in, 16)
            for g in range(4):
                pe.wait_ge(pooled_ready, g + 1)
                b = v_open()
                mm = pe.matmul(b[:, 0:T], PW[:, g, :], PADP[:, 4 * g:4 * g + 4, 8:72], start=True, stop=True)
                v_close(mm, ("poolmix", g))
            pe.wait_ge(vector_drained, n["v"])
            def norm_behind(i, width, sq):
                def after(m):
                    if m >= 1:
                        norm_part(i, m - 1, width, sq)
                    if m == KD - 1:
                        norm_part(i, m, width, sq)
                return after

            for j in range(2):
                product(W_EVO + j, 4 * j, T, v_open, v_close, "out1", new_input=j == 0, after=norm_behind(1, T, SQn))
            mark[("split", 0)] = len(quarters)

            def experts(ly):
                base = W_MOE[ly]
                pe.wait_ge(h_ready, h_count(1 + 2 * ly))
                if ly == 0:
                    pe.wait_ge(router_in, 32)
                b = v_open()
                for tt in range(TT):
                    for k in range(KD):
                        mm = pe.matmul(b[:, 16 * tt:16 * tt + 16], h2T[:, k, tt * P:tt * P + P], RT[:, ly, k, :],
                                       start=k == 0, stop=k == KD - 1)
                v_close(mm, ("logits", ly))
                pe.wait_ge(aff_ready, ly + 1)
                b = v_open()
                for tt in range(TT):
                    mm = pe.transpose(b[0:EXP, tt * P:tt * P + P], AFFT[:, tt, :], ident[:, :])
                v_close(mm, ("affT", ly))
                for tt in range(TT):
                    for kh in range(2):
                        b = s_open()
                        for k in range(4):
                            mm = pe.transpose(b[:, k * P:k * P + P], h2T[:, 4 * kh + k, tt * P:tt * P + P], ident[:, :])
                        s_close(mm, ("h2", ly))
                pe.wait_ge(pos_ready, ly + 1)
                b = v_open()
                for tt in range(TT):
                    mm = pe.transpose(b[:, 16 * tt:16 * tt + 16], PS2[0:EXP, tt * P:tt * P + P], ident[0:EXP, 0:EXP])
                v_close(mm, ("posT", ly))
                pe.wait_ge(pick_ready, 2 * ly + 1)
                pe.wait_ge(scalar_drained, n["s"])
                v0, s0, u0 = n["v"], n["s"], n["used"]
                mark[("group", ly)] = (v0, s0)
                for c_ in range(MOE_CHUNKS):
                    cc = base + c_
                    if c_ % 4 < 3:
                        released[cc] = (weights_used, u0 + 3 * (c_ // 4) + c_ % 4 + 1, 9)
                    elif c_ == 3:
                        released[cc] = (scalar_filled, s0 + 2, 4)
                    else:
                        released[cc] = (vector_filled, v0 + (2 if c_ == 7 else 4), 4)

                with pe.Fori(0, GROUPS) as g:
                    def arrived(c_):
                        cc = base + c_
                        pe.wait_ge(landed[slot_of(cc)], g * (16 * MOE_CHUNKS // MOE_SLOTS) + landed_at(cc))
                        return slot(cc)

                    def v_bank(i):
                        pe.wait_ge(vector_drained, g * 4 + (v0 + i - 3))
                        return VB[(v0 + i) % 4]

                    def s_bank(i):
                        pe.wait_ge(scalar_drained, g * 4 + (s0 + i - 3))
                        return SB[(s0 + i) % 4]

                    for half in range(2):
                        b = s_bank(0) if half == 0 else v_bank(0)
                        for k in range(4):
                            c0 = 256 * (2 * half + k // 2) + k % 2
                            for tt in range(TT):
                                mm = pe.matmul(b[:, k * P:k * P + P], H2[:, tt, c0:c0 + 255:2],
                                               PT[:, tt, bass.ds(g * P, P)], start=tt == 0, stop=tt == TT - 1)
                        mm.then_inc(scalar_filled if half == 0 else vector_filled, 1)
                    pe.wait_ge(scalar_drained, g * 4 + (s0 + 1))
                    pe.wait_ge(vector_drained, g * 4 + (v0 + 1))
                    for part in range(2):
                        b = s_bank(1) if part == 0 else v_bank(1)
                        for q in range(4):
                            w = arrived(4 * part + q).rearrange("p (e k n) -> p e k n", e=EG, k=2)
                            for k in range(2):
                                for e in range(EG):
                                    mm = pe.matmul(b[32 * e:32 * e + 32, :], XG[:, 2 * q + k, 32 * e:32 * e + 32],
                                                   w[:, e, k, :], start=q == 0 and k == 0, stop=q == 3 and k == 1)
                            mm.then_inc(weights_used if q < 3 else (scalar_filled, vector_filled)[part], 1)
                    pe.wait_ge(vector_drained, g * 4 + (v0 + 2))
                    for half in range(2):
                        b = s_bank(2) if half == 0 else v_bank(2)
                        for f in range(2):
                            ff = 2 * half + f
                            mm = pe.transpose(b[:, f * P:f * P + P], HIDD[:, ff * P:ff * P + P], ident[:, :])
                        mm.then_inc(scalar_filled if half == 0 else vector_filled, 1)
                    pe.wait_ge(scalar_drained, g * 4 + (s0 + 3))
                    pe.wait_ge(vector_drained, g * 4 + (v0 + 3))
                    b0, b1 = s_bank(3), v_bank(3)
                    for f in range(4):
                        w = arrived(8 + f).rearrange("p (e n) -> p e n", e=EG)
                        for half, b in ((0, b0), (1, b1)):
                            for e in range(EG):
                                mm = pe.matmul(b[32 * e:32 * e + 32, :], HT[:, f, 32 * e:32 * e + 32],
                                               w[:, e, 512 * half:512 * half + 512], start=f == 0, stop=f == 3)
                            if f == 3:
                                mm.then_inc(scalar_filled if half == 0 else vector_filled, 1)
                        if f < 3:
                            mm.then_inc(weights_used, 1)
                n["v"] += 4 * GROUPS
                n["s"] += 4 * GROUPS
                n["used"] += 9 * GROUPS
                pe.wait_ge(pick_ready, 2 * ly + 2)
                for gh in range(2):
                    b = v_open()
                    for g in range(2):
                        for tt in range(TT):
                            mm = pe.transpose(b[:, (2 * g + tt) * P:(2 * g + tt + 1) * P],
                                              GPT[:, tt, (2 * gh + g) * P:(2 * gh + g + 1) * P], ident[:, :])
                    v_close(mm, ("cm", ly))
                pe.wait_ge(scalar_drained, n["s"])
                pe.wait_ge(vector_drained, n["v"])
                if ly == 1:
                    pe.wait_ge(squares_ready, sq_count(4, 0))
                    b = s_open()
                    for k in range(KD):
                        mm = pe.matmul(b[:, 0:META], ONES, SQn[:, k, T:L2], start=k == 0, stop=k == KD - 1)
                    s_close(mm, "meta_norm")
                after = norm_behind(2 + 2 * ly, T, SQn)
                for m in range(KD):
                    b = v_open()
                    for g in range(GROUPS):
                        mm = pe.matmul(b[:, 0:T], Y[:, g, m * P:m * P + P], CM[:, g, :], start=g == 0, stop=g == GROUPS - 1)
                    v_close(mm, ("combine", ly, m))
                    after(m)

            experts(0)

            product(W_SC, 0, T, s_open, s_close, "gc", new_input=True)
            product(W_SC + 1, 0, T, v_open, v_close, "xin")
            product(W_SC + 2, 4, T, s_open, s_close, "gc")
            product(W_SC + 3, 4, T, v_open, v_close, "xin")
            product(W_SC + 4, 0, T, v_open, v_close, "gb")
            product(W_SC + 5, 4, T, v_open, v_close, "gb")
            for j in range(2):
                product(W_SC + 6 + j, 4 * j, T, v_open, v_close, "out2", new_input=j == 0, after=norm_behind(3, T, SQn))
            mark[("split", 1)] = len(quarters)

            experts(1)

            for j in range(5):
                product(W_E2 + j, 4 * j, L2, s_open, s_close, "conv3", new_input=j == 0)
            pe.wait_ge(dtw_in, 16)
            b = v_open()
            for i, (t0, _, r) in enumerate(SRC):
                for k in range(KD):
                    mm = pe.matmul(b[0:r, 16 * i:16 * i + 16], hN[:, k, t0:t0 + r], DTW[:, k, :], start=k == 0, stop=k == KD - 1)
            v_close(mm, "dt")
            product(W_E2 + 5, 0, L2, s_open, s_close, "lru_g")
            pe.wait_ge(conv_out, 12 + 20)
            arrive(W_LRU)
            wax = slot(W_LRU).rearrange("p (g b k n) -> p g b k n", g=2, b=4, k=2)
            for m in range(KD):
                for g in range(2):
                    b = s_open()
                    for k in range(2):
                        mm = pe.matmul(b[:, 0:L2], wax[:, g, m // 2, k, (m % 2) * P:(m % 2) * P + P], LX[:, 2 * (m // 2) + k, :],
                                       start=k == 0, stop=k == 1)
                    s_close(mm, ("lru", m, g))
            released[W_LRU] = (scalar_filled, n["s"])
            product(W_LRU + 1, 4, L2, s_open, s_close, "lru_g")
            for j in range(2):
                product(W_LRU + 2 + j, 4 * j, L2, s_open, s_close, "ssd_z")
            for j in range(2):
                product(W_E2O + j, 4 * j, L2, v_open, v_close, "out3a", new_input=j == 0)

            pe.wait_ge(dt_ready, 1)
            b = v_open()
            pe.matmul(b[:, 0:16], LE, ADT[:, 0, :], start=True, stop=True)
            pe.matmul(b[:, 16:32], LE, ADT[:, 1, :], start=True, stop=False)
            pe.matmul(b[:, 16:32], ONES, ADT[:, 0, :], start=False, stop=True)
            pe.matmul(b[0:META, 32:48], WIDE[0:META, 0:META], ADT[0:META, 2, :], start=True, stop=False)
            pe.matmul(b[0:META, 32:48], WIDE[:, P:P + META], ADT[:, 0, :], start=False, stop=False)
            mm = pe.matmul(b[0:META, 32:48], WIDE[:, P:P + META], ADT[:, 1, :], start=False, stop=True)
            v_close(mm, "cum")
            pe.wait_ge(conv_act, 12 + 12)
            for g in range(2):
                b = v_open()
                pe.matmul(b[:, 0:272], XB[:, 8 + g, 0:P], XB[:, 10 + g, 0:272], start=True, stop=True)
                pe.matmul(b[:, 272:416], XB[:, 8 + g, P:2 * P], XB[:, 10 + g, P:272], start=True, stop=True)
                mm = pe.matmul(b[0:META, 416:432], XB[:, 8 + g, 256:272], XB[:, 10 + g, 256:272], start=True, stop=True)
                v_close(mm, ("cb", g))
            pe.wait_ge(lru_done, 1)
            for i, (t0, _, r) in enumerate(SRC):
                for kh in range(2):
                    b = s_open()
                    for k in range(4):
                        mm = pe.transpose(b[0:r, k * P:k * P + P], XB[:, 4 * kh + k, t0:t0 + r], ident[:, :])
                    s_close(mm, ("xtk", i, kh))

            def cum_rows(h):
                b = v_open()
                pe.matmul(b[:, 0:L2], ADT[:, 0, h:h + 1].broadcast_to([P, P]), WIDE[:, 0:L2], start=True, stop=False)
                pe.matmul(b[:, P:L2], ADT[:, 1, h:h + 1].broadcast_to([P, P]), WIDE[:, 0:L2 - P], start=False, stop=False)
                mm = pe.matmul(b[:, 2 * P:L2], ADT[0:META, 2, h:h + 1].broadcast_to([META, P]), WIDE[0:META, 0:META],
                               start=False, stop=True)
                v_close(mm, ("cumrow", h))

            def gated_norm(g):
                b = s_open()
                for k in range(4):
                    pe.wait_ge(gate_sq, 4 * g + k + 1)
                    mm = pe.matmul(b[:, 0:L2], ONES, GSQ[:, 4 * g + k, :], start=k == 0, stop=k == 3)
                s_close(mm, ("gnorm", g))

            cum_rows(0)
            cum_rows(1)
            for h in range(SSD_H):
                if h + 2 < SSD_H:
                    cum_rows(h + 2)
                pe.wait_ge(ssd_w, h + 1)
                if h == 0:
                    pe.wait_ge(tokens_scaled, len(SRC))
                b = v_open()
                r0 = 64 * (h % 2)
                for i, (t0, c0, r) in enumerate(SRC):
                    mm = pe.matmul(b[r0:r0 + 64, t0:L2], XTK[0:r, i, 64 * h:64 * h + 64], EB[0:r, h % 3, c0:c0 + L2 - t0],
                                   start=i == 0, stop=i == 2)
                v_close(mm, ("y", h))
                if h == SSD_H - 2:
                    gated_norm(0)
            gated_norm(1)
            for j in range(2):
                product(W_E2O + 2 + j, 4 * j, L2, v_open, v_close, "out3", new_input=j == 0, after=norm_behind(6, L2, SQ3))

            for j in range(2):
                product(W_OD + j, 4 * j, L2, s_open, s_close, "q", new_input=j == 0)
            for j in range(2):
                product(W_OD + 2 + j, 4 * j, L2, v_open, v_close, "k")
            for j in range(2):
                product(W_OD + 4 + j, 4 * j, L2, v_open, v_close, "v")
            vv = n["v"]
            for j in range(2):
                product(W_OD + 6 + j, 4 * j, L2, s_open, s_close, "g")
            pe.wait_ge(vector_drained, vv)
            for i, (t0, _, r) in enumerate(SRC):
                for kh in range(2):
                    b = v_open()
                    for k in range(4):
                        mm = pe.transpose(b[0:r, k * P:k * P + P], VS[:, 4 * kh + k, t0:t0 + r], ident[:, :])
                    v_close(mm, ("vtk", i, kh))
            pe.wait_ge(vector_drained, n["v"])
            pe.wait_ge(scalar_drained, n["s"])

            def stick_scores(h):
                m, r0 = h // 2, 64 * (h % 2)
                b = s_open()
                for i, (t0, c0, _) in enumerate(SRC):
                    mm = pe.matmul(b[:, c0:c0 + L2 - t0], KS2[r0:r0 + 64, m, t0:t0 + P], QS[r0:r0 + 64, m, t0:L2],
                                   start=True, stop=True)
                s_close(mm, ("z", h))

            def stick_sums(h):
                pe.wait_ge(sb_soft, h + 1)
                q = PB[:, h % 2, :]
                b = v_open()
                pe.matmul(b[:, 0:L2], GE[:, :], q[:, 0:L2], start=True, stop=False)
                pe.matmul(b[:, P:L2], ONES, q[:, 272:416], start=False, stop=False)
                pe.matmul(b[:, 2 * P:L2], ONES, q[:, 416:432], start=False, stop=True)
                pe.matmul(b[:, 272:416], GE[:, :], q[:, 272:416], start=True, stop=False)
                pe.matmul(b[:, 400:416], ONES, q[:, 416:432], start=False, stop=True)
                mm = pe.matmul(b[:, 416:432], GE[:, :], q[:, 416:432], start=True, stop=True)
                v_close(mm, ("suffix", h))

            def stick_out(h):
                pe.wait_ge(sb_w, h + 1)
                b = v_open()
                r0 = 64 * (h % 2)
                for i, (t0, c0, r) in enumerate(SRC):
                    mm = pe.matmul(b[r0:r0 + 64, t0:L2], VTK[0:r, i, 64 * h:64 * h + 64], EBS[0:r, h % 2, c0:c0 + L2 - t0],
                                   start=i == 0, stop=i == 2)
                v_close(mm, ("o3", h))

            for h in range(3):
                stick_scores(h)
            for h in range(SB_H):
                stick_sums(h)
                if h + 3 < SB_H:
                    stick_scores(h + 3)
                if h >= 1:
                    stick_out(h - 1)
            stick_out(SB_H - 1)
            pe.wait_ge(vector_drained, n["v"])
            for j in range(2):
                product(W_OD + 8 + j, 4 * j, L2, v_open, v_close, "out4", new_input=j == 0, after=norm_behind(7, T, SQ3))
            mark[("split", 2)] = len(quarters)

            for tt in range(TT):
                for kh in range(2):
                    b = v_open() if kh == 0 else s_open()
                    for k in range(4):
                        pe.wait_ge(h_ready, h_count(7, 4 * kh + k + 1))
                        mm = pe.transpose(b[:, k * P:k * P + P], h2T[:, 4 * kh + k, tt * P:tt * P + P], ident[:, :])
                    (v_close if kh == 0 else s_close)(mm, ("final", tt))
            mark["v_end"], mark["s_end"] = n["v"], n["s"]

        @block.sync
        def _(sp):
            def load(cn):
                sp.dma_start(chunk(cn), stream[cn][1]).then_inc(landed[slot_of(cn)], 16)

            def free_slot(cn):
                before = [c_ for c_ in range(cn) if slot_of(c_) == slot_of(cn)]
                if before:
                    signal, value = released[before[-1]][0:2]
                    sp.wait_ge(signal, value)
                elif slot_of(cn) >= SLOTS:
                    sp.wait_ge(input_split, KD)

            def load_group(ly, g, c_, cn):
                dst = slot(cn)
                e0 = g * EG
                if c_ < 8:
                    w = (w_gate, w_up)[c_ // 4][ly]
                    q = c_ % 4
                    sp.dma_start(dst.rearrange("p (e n) -> p e n", e=EG),
                                 w[bass.ds(e0, EG), 2 * q * P:(2 * q + 2) * P, :].rearrange("e (p k) n -> p e (k n)", p=P))\
                        .then_inc(landed[slot_of(cn)], 16)
                else:
                    f = c_ - 8
                    sp.dma_start(dst.rearrange("p (e n) -> p e n", e=EG),
                                 w_down[ly][bass.ds(e0, EG), f * P:(f + 1) * P, :].rearrange("e p n -> p e n"))\
                        .then_inc(landed[slot_of(cn)], 16)

            cn = 0
            while cn < len(stream):
                if stream[cn][0] == "moe":
                    ly = stream[cn][1]
                    for c_ in range(MOE_CHUNKS):
                        free_slot(cn + c_)
                        load_group(ly, 0, c_, cn + c_)
                    with sp.Fori(1, GROUPS) as g:
                        for c_ in range(MOE_CHUNKS):
                            prior = cn + (c_ - MOE_SLOTS) % MOE_CHUNKS
                            signal, value, per_group = released[prior]
                            back = 0 if c_ >= MOE_SLOTS else per_group
                            sp.wait_ge(signal, g * per_group + (value - back))
                            load_group(ly, g, c_, cn + c_)
                    cn += MOE_CHUNKS * GROUPS
                    for i in range(MOE_CHUNKS):
                        signal, value, per_group = released[cn - MOE_CHUNKS * GROUPS + i]
                        released[cn - MOE_CHUNKS + i] = (signal, value + (GROUPS - 1) * per_group)
                    continue
                if cn == 0:
                    sp.wait_ge(first_vec_in, 16 * len(first_vecs))
                if cn == 2:
                    sp.wait_ge(x_in, 32)
                free_slot(cn)
                if stream[cn][0] == "lru":
                    half = slot(cn).rearrange("p (g b k n) -> p g b k n", g=2, b=4, k=2)
                    for i, w in enumerate((lru_w_a_2, lru_w_x_2)):
                        sp.dma_start(half[:, i].rearrange("p b k n -> p (b k) n"), w[0].rearrange("b (k p) n -> p (b k) n", p=P))\
                            .then_inc(landed[slot_of(cn)], 16)
                else:
                    load(cn)
                cn += 1
            sp.wait_ge(out_copied, 2)
            sp.wait_ge(scalar_drained, mark["s_end"])
            for tt in range(TT):
                sp.dma_start(out[0, tt * P:(tt + 1) * P, :], OUTS[:, tt, :]).then_inc(out_done, 16)
            sp.wait_ge(out_done, 16 * TT)

        @block.gpsimd
        def _(pool):
            steps = [0]

            def then(ins):
                steps[0] += 1
                ins.then_inc(pool_step, 1)
                pool.wait_ge(pool_step, steps[0])

            def keep_if(v, pattern, base, mult, fill=0.0, op=ALU.is_ge):
                return pool.affine_select(out=v, in_=v, compare_op=op, fill=fill, base=base, pattern=pattern,
                                          channel_multiplier=mult)

            then(pool.memset(ident[:, :], 0.0))
            then(keep_if(ident[:, :], [[-1, P]], 0, 1, 1.0, ALU.not_equal))
            then(pool.memset(WIDE[:, :], 1.0))
            then(keep_if(LE, [[1, P]], 0, -1))
            then(pool.memset(GE[:, :], 1.0))
            then(keep_if(GE[:, :], [[-1, P]], 0, 1))
            then(pool.memset(SEL[:, :], 0.0))
            for q in range(4):
                then(keep_if(SEL[:, :], [[-1, 2]], -32 * q, 1, 1.0, ALU.not_equal))
            then(pool.memset(EPSC, EPS))
            pool.iota(SLOTN, pattern=[[1, CAP]], base=1, channel_multiplier=0,
                      allow_small_or_imprecise_dtypes=True).then_inc(consts_ready, 1)
            then(pool.memset(LM, 0.0))
            for lv in range(LEVELS):
                b = 1 << lv
                for d in range(2):
                    v = LM[:, d, lv, :].rearrange("p (n h j) -> p n h j", h=2, j=b)[:, :, d, :]
                    nb = P // (2 * b)
                    lo = b if d == 0 else 0
                    then(pool.memset(v, 1.0))
                    then(keep_if(v, [[-2 * b, nb], [0, b]], -lo, 1))
                    then(keep_if(v, [[2 * b, nb], [0, b]], lo + b - 1, -1))
            pool.wait_ge(conv_out, 12)
            for g in range(4):
                hw = 1 << g
                pool.iota(IOT[:, 0, 64 * g:64 * g + 64], pattern=[[1, 64]], base=hw, channel_multiplier=0,
                          allow_small_or_imprecise_dtypes=True)
                pool.iota(IOT[:, 1, 64 * g:64 * g + 64], pattern=[[-1, 64]], base=64 + hw, channel_multiplier=0,
                          allow_small_or_imprecise_dtypes=True).then_inc(iota_ready, 1)
            turn = 0
            for d in range(2):
                for lv in range(LEVELS):
                    for h in range(HEADS):
                        if lv == 0:
                            pool.wait_ge(tri_ready, HEADS * d + h + 1)
                        i = LEVELS * HEADS * d + turn % (LEVELS * HEADS)
                        k = turn % (LEVELS * HEADS)
                        if k >= 2:
                            if (k - 2) // HEADS == 0:
                                pool.wait_ge(vector_drained, mark[("turn", d, k - 2)])
                            else:
                                pool.wait_ge(scalar_filled, mark[("turn", d, k - 2)])
                        pool.tensor_tensor(Amask[:, i % 2], Am[:, h], mid(LM[:, d, lv, :], UNITS), ALU.mult).then_inc(masked, 1)
                        turn += 1
                pool.wait_ge(masked, LEVELS * HEADS * (d + 1))
                for h in range(HEADS):
                    if h >= 2:
                        pool.wait_ge(vector_filled, mark[("solve", d, h - 2)])
                    pool.tensor_tensor(KBG[:, h % 2], Ktok[:, h], last(BG[:, :, 4 * d + h], P), ALU.mult)
                    pool.tensor_tensor(BV[:, h % 2], Vtok[:, h], last(BETA[:, :, 4 * d + h], P), ALU.mult).then_inc(scaled, 1)
                for h in range(HEADS):
                    pool.tensor_tensor(Am[:, h], Ktok[:, h], last(KS[:, h, :], P), ALU.mult).then_inc(kdec_ready, 1)
            pool.wait_ge(h_ready, h_count(5))
            for i, (t0, c0, _) in enumerate(SRC):
                w = L2 - t0
                pool.tensor_copy(MASK3[:, c0:c0 + w], WIDE[:, 0:w]).then_inc(iota_ready, 1)
            pool.wait_ge(vector_drained, mark[("cb", 1)])
            for h in range(SSD_H):
                pool.wait_ge(ssd_exps, h + 1)
                e = EB[:, h % 3, :]
                pool.tensor_tensor(e, e, CBM[:, h // 8, :], ALU.mult).then_inc(ssd_w, 1)
            pool.wait_ge(h_ready, h_count(6))
            then(pool.memset(SMASK, 1.0))
            for i, (t0, c0, _) in enumerate(SRC):
                w = L2 - t0
                then(keep_if(SMASK[:, c0:c0 + w], [[1, w]], -1, -1))
            pool.tensor_scalar(NEG, SMASK, 1.0e4, -1.0e4, ALU.mult, ALU.add).then_inc(iota_ready, 1)

        @block.scalar
        def _(act):
            n = {"s": 0, "step": 0}

            def take():
                act.wait_ge(scalar_filled, n["s"] + 1)
                return SB[n["s"] % 4]

            def drained(ins):
                n["s"] += 1
                ins.then_inc(scalar_drained, 1)

            def then(ins):
                n["step"] += 1
                ins.then_inc(scalar_step, 1)
                act.wait_ge(scalar_step, n["step"])

            def logs():
                act.preload_act_table_set("natural_log_exp_and_others")

            n["high"] = n["segment"] = 0

            def high():
                j = n["high"]
                if j == mark[("split", n["segment"])]:
                    return
                cn, m, _, _ = quarters[j]
                if m == 0:
                    act.wait_ge(landed[slot_of(cn)], landed_at(cn))
                if j >= 2:
                    act.wait_ge(quarters[j - 2][2], quarters[j - 2][3])
                act.activation(WHI[:, j % 2], chunk(cn)[:, :, m * P:m * P + P], ACT.Copy).then_inc(weights_high, 1)
                n["high"] += 1

            def load_vecs(names, signal):
                for name in names:
                    g, r, k = vec_at[name]
                    act.dma_start(VEC[r:r + k, g, :], vec_src[name]).then_inc(signal, 16)

            load_vecs(first_vecs, first_vec_in)
            for s, src in enumerate((x, ctx)):
                act.dma_start(XIN[:, 2 * s:2 * s + 2, :], src[0].rearrange("(t p) n -> p t n", p=P)).then_inc(x_in, 16)

            logs()
            act.wait_ge(vector_drained, mark["vec"])
            act.activation(ce, VT[:, 0, 0:16], ACT.Exp, scale=-1.0).then_inc(c_exp, 1)
            for tt in range(TT):
                for kh in range(2):
                    b = take()
                    drained(act.activation(XC[:, 4 * kh:4 * kh + 4, tt * P:tt * P + P], bank(b, 4, P), ACT.Copy))

            def rstd(src, nr):
                b = take()
                drained(act.activation(nr, b[:, src], ACT.Ln, bias=EPSC, scale=1.0 / D))
                act.wait_ge(scalar_drained, n["s"])
                act.activation(nr, nr, ACT.Exp, scale=-0.5).then_inc(rstd_ready, 1)

            scaled_tiles = [0]

            def shift(v, by, signal, high=None):
                if signal:
                    scaled_tiles[0] += 1
                    act.wait_ge(h_scaled, scaled_tiles[0])
                return act.activation(v if high is None else high, v, ACT.Identity, bias=by)

            def norm(i, names, t0=META, width=T, sq=SQn, nr=NRn, mod=None):
                for m in range(KD):
                    act.wait_ge(vector_drained, mark[names + (m,)])
                    act.activation(sq[:, m, 0:width], XH[:, m, t0:t0 + width], ACT.Square).then_inc(squares_ready, 1)
                    if names[0] != "combine" or m in (3, 4):
                        high()
                rstd(slice(0, width), nr[:, 0:width])
                if mod is not None:
                    ly, piece = mod
                    for k in range(KD):
                        shift(h2T[:, k, :], MOD[:, ly, piece + k, 0:1], True, XHI[:, k, 0:T] if i == 2 else None).then_inc(h_ready, 1)

            def high_parts(src):
                for k in range(KD):
                    scaled_tiles[0] += 1
                    act.wait_ge(h_scaled, scaled_tiles[0])
                    act.activation(XHI[:, k, :], src[:, k, :], ACT.Copy).then_inc(h_ready, 1)

            act.wait_ge(vector_drained, mark["x"])
            act.wait_ge(scalar_drained, n["s"])
            act.activation(SQ1[:, :, 0:T], XH[:, :, META:L2], ACT.Square)
            act.activation(SQ1[:, :, T:2 * T], XC, ACT.Square).then_inc(squares_ready, 1)
            act.dma_start(MIN[0:META, :], meta_2).then_inc(meta_in, 16)
            load_vecs([name for name in vec_src if name not in first_vecs], vec_in)
            for dst, src in small_src:
                act.dma_start(dst, src, allow_slow_non_contiguous=True).then_inc(small_in, 16)
            rstd(slice(0, 512), NR1)

            ada = [0]

            def ada_copy():
                b = take()
                if ada[0]:
                    act.wait_ge(vector_filled, mark[("mod", ada[0] - 1)])
                drained(act.activation(PART[:, :], b[:, :], ACT.Copy))
                ada[0] += 1

            for i in range(4):
                ada_copy()

            for k in range(KD):
                shift(hT[:, k, 0:T], MOD[:, 0, k, 0:1], True)
                shift(hT[:, k, T:2 * T], MOD[:, 0, k, 1:2], False).then_inc(h_ready, 1)
            act.wait_ge(small_in, 16 * n_small)
            act.activation(alog, alog, ACT.Exp)
            act.activation(salog, salog, ACT.Exp)
            b = take()
            drained(act.activation(XH[:, :, 0:META], bank(b, KD, META), ACT.Copy))

            def silu_qkv(t):
                act.wait_ge(conv_out, t + 1)
                v = QT[:, t, :] if t < 4 else KT[:, t - 4, :] if t < 8 else VTf[:, t - 8, :]
                act.activation(v, v, ACT.Silu).then_inc(conv_act, 1)
                if t >= 5:
                    l2_square(t - 5)

            def l2_square(i):
                act.wait_ge(conv_act, i + 5 if i < 4 else 8)
                v = KT[:, i, :] if i < 4 else QT[:, i - 4, :]
                act.activation(l2_buf(i), v, ACT.Square).then_inc(l2_squares, 1)

            for t in range(12):
                b = take()
                w = 1 if t < 4 else 2
                if t < 4:
                    act.wait_ge(edges_ready, 1)
                if t >= 4:
                    act.wait_ge(conv_out, t - 3)
                drained(act.activation(CB[:, t % 4, 0:w, 1:1 + T], bank(b, w, T), ACT.Copy))
                if t >= 1:
                    silu_qkv(t - 1)
            silu_qkv(11)
            for m in range(4):
                b = take()
                drained(act.activation(Z1[:, m, :], b[:, 0:T], ACT.Silu))
            l2_square(7)
            logs()
            for i in range(8):
                w = 2 * T if i < 4 else T
                b = take()
                drained(act.activation(l2_buf(i), b[:, 0:w], ACT.Ln, bias=EPSC))
                act.wait_ge(scalar_drained, n["s"])
                act.activation(l2_buf(i), l2_buf(i), ACT.Exp, scale=-0.5).then_inc(l2_rstd, 1)
            act.wait_ge(gate_args, 1)
            then(act.activation(g_e, g_e, ACT.Exp))
            act.activation(g_e, g_e, ACT.Ln, bias=ONE)
            act.activation(BETA, graw[:, :, 0:8], ACT.Exp, scale=-1.0).then_inc(gate_exps, 1)
            for h in range(HEADS):
                b = take()
                drained(act.activation(Ktok[:, h], bank(b, 4, P), ACT.Copy))
            act.wait_ge(vector_drained, mark["gc"])
            act.activation(EGC, GC, ACT.Exp).then_inc(gam_exps, 1)

            for d in range(2):
                g = 0
                for kind, a, h in mixer_steps(d):
                    if kind == "ada":
                        ada_copy()
                    elif kind == "gamma":
                        h = a
                        diff, Tlo, Thi, Tq = decay_bufs[h % 2]
                        act.wait_ge(diff_ready, HEADS * d + h + 1)
                        act.activation(Tlo, Tlo, ACT.Exp, scale=-1.0)
                        act.activation(Thi, Thi, ACT.Exp)
                        for u in range(TT):
                            ins = act.activation(Tq[:, u, :], diff[:, u, :], ACT.Exp, bias=GC[:, u, 4 * d + h:4 * d + h + 1])
                        ins.then_inc(decay_exps, 1)
                    elif kind == "turn" and a >= 1:
                        b = take()
                        if g >= 2:
                            act.wait_ge(vector_filled, mark[("grow", d, g - 2)])
                        drained(act.activation(Qs[:, g % 2], bank(b, 4, P), ACT.Copy))
                        g += 1
                    elif kind == "walk" and d == 0 and a >= 2:
                        b = take()
                        u = ORDER[d][a]
                        drained(act.activation(OT[:, :, u * P:u * P + P], bank(b, 4, P), ACT.Copy))

            act.wait_ge(vector_drained, mark[("o", 1, 3)])
            high()
            high()
            act.dma_start(PW, pool_w[0].rearrange("g c d -> c g d")).then_inc(poolw_in, 16)
            for ly in range(2):
                act.dma_start(RT[:, ly], router[ly].rearrange("(k p) e -> p k e", p=P)).then_inc(router_in, 16)
            for i in range(2):
                act.activation(OSQ[:, i, :].rearrange("p (h t) -> p h t", h=2), OT[:, 2 * i:2 * i + 2, :], ACT.Square)\
                    .then_inc(ones_ready, 1)
            for i in range(2):
                b = take()
                drained(act.activation(OSQ[:, i, :], b[:, :], ACT.Ln, bias=EPSC, scale=1.0 / P))
                act.wait_ge(scalar_drained, n["s"])
                act.activation(OSQ[:, i, :], OSQ[:, i, :], ACT.Exp, scale=-0.5).then_inc(o_rstd, 1)

            def experts(ly):
                act.wait_ge(sm_args, ly + 1)
                act.activation(AFFT, AFFT, ACT.Exp).then_inc(sm_exps, 1)
                for tt in range(TT):
                    for kh in range(2):
                        b = take()
                        drained(act.activation(H2[:, tt, 512 * kh:512 * kh + 512], b[:, :], ACT.Copy))
                s0 = n["s"]
                with act.Fori(0, GROUPS) as g:
                    def filled(i):
                        act.wait_ge(scalar_filled, g * 4 + (s0 + i + 1))
                        return SB[(s0 + i) % 4]
                    b = filled(0)
                    act.activation(XG[:, 0:4], bank(b, 4, P), ACT.Copy).then_inc(scalar_drained, 1)
                    b = filled(1)
                    act.activation(SG, b[:, :], ACT.Silu).then_inc(scalar_drained, 1)
                    b = filled(2)
                    act.activation(HT[:, 0:2], bank(b, 2, P), ACT.Copy).then_inc(scalar_drained, 1)
                    b = filled(3)
                    act.activation(Y[:, bass.ds(g, 1), 0:512].rearrange("p a n -> p (a n)"), b[:, :], ACT.Copy).then_inc(scalar_drained, 1)
                n["s"] += 4 * GROUPS
                logs()

            norm(1, ("out1",), mod=(0, 24))
            n["segment"] += 1
            experts(0)
            norm(2, ("combine", 0), mod=(1, 0))
            for m in range(KD):
                high()
                b = take()
                drained(act.activation(GCC[:, m, :], b[:, 0:T], ACT.Copy))
                if m % 4 == 3:
                    for _ in range(4):
                        high()
            for _ in range(KD):
                high()
            norm(3, ("out2",), mod=(1, 24))
            n["segment"] += 1
            experts(1)
            act.activation(SQn[:, :, T:L2], XH[:, :, 0:META], ACT.Square).then_inc(squares_ready, 1)
            rstd(slice(0, META), NRn[:, 0:META])
            act.wait_ge(vector_drained, mark[("combine", 1, 0)])
            act.dma_start(DTW, even_w_in_2[0][:, 4608:4624].rearrange("(k p) n -> p k n", p=P)).then_inc(dtw_in, 16)
            norm(4, ("combine", 1), nr=NR4)
            act.wait_ge(mean_ready, 1)
            then(act.activation(NRn[:, META:L2], NS5[:, 0:T], ACT.Ln, bias=EPSC, scale=1.0 / D))
            act.activation(NRn[:, META:L2], NRn[:, META:L2], ACT.Exp, scale=-0.5).then_inc(rstd_ready, 1)
            high_parts(hN)

            def silu3(t):
                act.wait_ge(conv_out, 12 + t + 1)
                act.activation(XB[:, t, :], XB[:, t, :], ACT.Silu).then_inc(conv_act, 1)

            act.wait_ge(edges_ready, 2)
            for t in range(20):
                high()
                b = take()
                if t >= 4:
                    act.wait_ge(conv_out, 12 + t - 3)
                drained(act.activation(CB3[:, t % 4, 3:3 + L2], b[:, 0:L2], ACT.Copy))
                if 1 <= t <= 12:
                    silu3(t - 1)
            act.wait_ge(dt_args, 1)
            logs()
            then(act.activation(DTn, DTn, ACT.Exp))
            then(act.activation(ln8, ln8, ACT.Exp))
            act.activation(DTn, DTn, ACT.Ln, bias=ONE)
            act.activation(ln8, ln8, ACT.Ln, bias=ONE).then_inc(dt_exps, 1)
            def lru_gate_silu(m):
                b = take()
                drained(act.activation(SLG[:, m, :], b[:, 0:L2], ACT.Silu))

            for m in range(4):
                high()
                lru_gate_silu(m)
            for m in range(KD):
                for g, (dst, name) in enumerate(((LR, "lru_b_a"), (LI, "lru_b_x"))):
                    b = take()
                    drained(act.activation(dst[:, m, :], b[:, 0:L2], ACT.Sigmoid, bias=vec(name, m)))
            act.wait_ge(scalar_drained, n["s"])
            act.wait_ge(lc_ready, 1)
            high()
            for m in range(KD):
                act.activation(LTH[:, m, :], LR[:, m, :], ACT.Tanh, scale=lc8[:, m:m + 1]).then_inc(tanh_ready, 1)
                if m % 4 == 3:
                    high()
            act.wait_ge(tanh_ready, KD)
            logs()

            def lru_gate_raw(m):
                b = take()
                drained(act.activation(SLG[:, m, :], b[:, 0:L2], ACT.Copy))

            for m in range(KD):
                act.activation(LR[:, m, :], LR[:, m, :], ACT.Exp, scale=lc8[:, m:m + 1])
                if m % 4 == 3:
                    lru_gate_raw(4 + m // 4)
                    high()
            act.wait_ge(mult_args, 1)
            then(act.activation(LX, LTH, ACT.Ln, bias=ONE))
            lru_gate_raw(6)
            high()
            act.activation(LTH, LTH, ACT.Ln, scale=2.0).then_inc(logs_ready, 1)
            lru_gate_raw(7)
            high()
            act.wait_ge(half_ready, 1)
            act.activation(LTH, LTH, ACT.Exp, scale=0.5).then_inc(mult_ready, 1)
            high()
            act.wait_ge(scalar_drained, n["s"])
            act.activation(SLG[:, 4:8, :], SLG[:, 4:8, :], ACT.Silu).then_inc(gate_silus, 1)
            for m in range(KD):
                if m >= 4:
                    high()
                b = take()
                drained(act.activation(SZ[:, m, :], b[:, 0:L2], ACT.Silu))
            for _ in range(KD):
                high()
            logs()
            for i, (_, _, r) in enumerate(SRC):
                for kh in range(2):
                    b = take()
                    drained(act.activation(XTK[0:r, i, 512 * kh:512 * kh + 512], b[0:r, :], ACT.Copy))

            def gated_square(m):
                act.wait_ge(gated, m + 1)
                act.activation(GSQ[:, m, :], MIX3[:, 8 + m, :], ACT.Square).then_inc(gate_sq, 1)

            for h in range(SSD_H):
                act.wait_ge(vector_drained, mark[("cumrow", h)])
                act.activation(EB[:, h % 3, :], EB[:, h % 3, :], ACT.Exp).then_inc(ssd_exps, 1)
                if h >= 4 and h % 2 == 0:
                    gated_square(h // 2 - 2)
            for g in range(2):
                if g == 1:
                    gated_square(6)
                    gated_square(7)
                b = take()
                drained(act.activation(GRR[:, g, :], b[:, 0:L2], ACT.Ln, bias=EPSC, scale=1.0 / 512))
                act.wait_ge(scalar_drained, n["s"])
                act.activation(GRR[:, g, :], GRR[:, g, :], ACT.Exp, scale=-0.5).then_inc(gate_rstd, 1)

            norm(6, ("out3",), 0, L2, SQ3, NR6)
            high_parts(hN)
            for m in range(KD):
                high()
                b = take()
                drained(act.activation(QS[:, m, :], b[:, 0:L2], ACT.Copy, scale=64 ** -0.5))
            for _ in range(2 * KD):
                high()
            for m in range(KD):
                high()
                b = take()
                drained(act.activation(SGT[:, m, :], b[:, 0:L2], ACT.Silu))

            logs()

            def stick_logs(h):
                b = take()
                act.activation(ZB[:, h % 3, :], b[:, 0:TRI], ACT.Copy)
                drained(act.activation(LB[:, h % 3, :], b[:, 0:TRI], ACT.Abs))
                act.wait_ge(scalar_drained, n["s"])
                then(act.activation(LB[:, h % 3, :], LB[:, h % 3, :], ACT.Exp, scale=-1.0))
                act.activation(LB[:, h % 3, :], LB[:, h % 3, :], ACT.Ln, bias=ONE).then_inc(sb_logs, 1)

            stick_logs(0)
            stick_logs(1)
            for h in range(SB_H):
                if h + 2 < SB_H:
                    stick_logs(h + 2)
                act.wait_ge(sb_args, h + 1)
                act.activation(EBS[:, h % 2, :], EBS[:, h % 2, :], ACT.Exp).then_inc(sb_w, 1)
            norm(7, ("out4",), sq=SQ3, nr=NR6)
            for tt in range(TT):
                b = take()
                drained(act.activation(OUTS[:, tt, 512:1024], b[:, :], ACT.Copy))
            assert n["s"] == mark["s_end"]

        @block.vector
        def _(dve):
            n = {"v": 0, "step": 0}

            def take():
                dve.wait_ge(vector_filled, n["v"] + 1)
                return VB[n["v"] % 4]

            def drained(ins, wait=False):
                n["v"] += 1
                ins.then_inc(vector_drained, 1)
                if wait:
                    dve.wait_ge(vector_drained, n["v"])

            def then(ins):
                n["step"] += 1
                ins.then_inc(vector_step, 1)
                dve.wait_ge(vector_step, n["step"])

            def tt(out_, a, b, op):
                return dve.tensor_tensor(out_, a, b, op)

            def stt(out_, a, s, b, op0, op1):
                return dve.scalar_tensor_tensor(out_, a, s, b, op0, op1)

            MUL, ADD, SUB, MAX, MIN = ALU.mult, ALU.add, ALU.subtract, ALU.max, ALU.min

            n["split"] = n["segment"] = 0

            def split():
                j = n["split"]
                if j == mark[("split", n["segment"])]:
                    return
                cn, m, _, _ = quarters[j]
                dve.wait_ge(weights_high, j + 1)
                w = chunk(cn)[:, :, m * P:m * P + P]
                tt(WLO[:, j % 2], w, WHI[:, j % 2].bitcast(F32), SUB).then_inc(weights_split, 1)
                n["split"] += 1

            def split_input(src, width, k0=0, tiles=KD):
                then(dve.tensor_copy(XHI[:, k0:k0 + tiles, 0:width], src[:, k0:k0 + tiles, :]))
                for k in range(k0, k0 + tiles):
                    tt(XLO[:, k, 0:width], src[:, k, :], XHI[:, k, 0:width].bitcast(F32), SUB).then_inc(input_split, 1)

            def vec_copies(tiles):
                b = take()
                for g in tiles:
                    ins = dve.tensor_copy(VT[:, g, 0:vec_at[g]], b[:, g * P:g * P + vec_at[g]])
                drained(ins, True)

            vec_copies((0,))
            dve.wait_ge(c_exp, 1)
            then(dve.tensor_scalar(ce, ce, 1.0, None, ADD))
            then(dve.reciprocal(ce, ce))
            dve.memset(CS[:, 2 * KD:], 0.0)
            tt(CS[:, 0:2 * KD].rearrange("p (k r) -> p r k", r=2), VT[:, 0, 0:16].rearrange("p (r k) -> p r k", r=2),
               ce.rearrange("p (r k) -> p r k", r=2), MUL).then_inc(c_ready, 1)
            for t_ in range(TT):
                for kh in range(2):
                    b = take()
                    drained(dve.tensor_copy(XH[:, 4 * kh:4 * kh + 4, META + t_ * P:META + t_ * P + P], bank(b, 4, P)))

            ada = [0]

            def ada_bias():
                i = ada[0]
                ly, c0 = i // 12, 4 * (i % 12)
                b = take()
                drained(tt(MOD[:, ly, c0:c0 + 4, :], bank(b, 4, 2), last(vec("ada_b", 48 * ly + c0, 4), 2), ADD))
                ada[0] += 1

            roots = [0]

            def negated_half(src, v):
                return dve.tensor_scalar(v, src, -0.5 / D, -0.5 * EPS, MUL, ADD)

            def newton(v, y, t_):
                roots[0] += 1
                dve.wait_ge(rstd_ready, roots[0])
                then(tt(t_, y, y, MUL))
                then(tt(t_, t_, v, MUL))
                then(stt(y, t_, 1.5, y, ADD, MUL))

            def root(name, width, nv, nr, nt):
                dve.wait_ge(scalar_drained, mark[name])
                negated_half(SB[(mark[name] - 1) % 4][:, 0:width], nv[:, 0:width])
                newton(nv[:, 0:width], nr[:, 0:width], nt[:, 0:width])

            def low_parts(i, src, width, mod=None):
                for k in range(KD):
                    dve.wait_ge(h_ready, h_count(i, k + 1))
                    high, low = XHI[:, k, 0:width].bitcast(F32), XLO[:, k, 0:width]
                    if mod is None:
                        ins = tt(low, src[:, k, :], high, SUB)
                    else:
                        ins = stt(low, src[:, k, :], MOD[:, mod[0], mod[1] + k, 0:1], high, ADD, SUB)
                    ins.then_inc(input_split, 1)

            def norm(i, g_name, g_at, t0=META, width=T, mod=None):
                dst = h2T if width == T else hN
                split_too = i in (2, 6)
                if mod is not None:
                    ly, piece = mod
                    stt(gain[:, :, 0], MOD[:, ly, piece + 8:piece + 16, 0], 1.0, vec(g_name, g_at, 8), ADD, MUL)
                nv, nr, nt = (NV6, NR6, NT6) if i >= 6 else (NVn, NRn, NTn)
                root(("norm", i), width, nv, nr, nt)
                for k in range(KD):
                    g = gain[:, k, 0:1] if mod is not None else vec(g_name, g_at + k)
                    stt(dst[:, k, :], XH[:, k, t0:t0 + width], g, nr[:, 0:width], MUL, MUL)\
                        .then_inc(h_scaled if mod is not None or split_too else h_ready, 1)
                if split_too:
                    low_parts(i, dst, width, mod)

            root(("norm", 0), 512, NV1, NR1, NT1)
            for i in range(4):
                ada_bias()
            dve.wait_ge(vector_drained, n["v"])
            for r in range(2):
                ins = stt(gain[:, :, r], MOD[:, 0, 8:16, r], 1.0, vec("norm_mix", 0, 8), ADD, MUL)
            then(ins)
            for k in range(KD):
                stt(hT[:, k, 0:T], XH[:, k, META:L2], gain[:, k, 0:1], NR1[:, 0:T], MUL, MUL)
                stt(hT[:, k, T:2 * T], XC[:, k, :], gain[:, k, 1:2], NR1[:, T:2 * T], MUL, MUL).then_inc(h_scaled, 1)
            vec_copies((1, 2))
            tt(gain_sq, vec("norm_final", 0, 8), vec("norm_final", 0, 8), MUL)
            dve.memset(CB[:, :, :, 0:1], 0.0)
            dve.memset(CB[:, :, :, T + 1:T + 2], 0.0).then_inc(edges_ready, 1)
            dve.memset(PADP, 0.0)

            for t in range(12):
                w = 1 if t < 4 else 2
                dst = QT[:, t, :] if t < 4 else KT[:, t - 4, :] if t < 8 else VTf[:, t - 8, :]
                dst = dst.rearrange("p (s t) -> p s t", s=w)
                src = CB[:, t % 4, 0:w, :]
                dve.wait_ge(scalar_drained, mark[("qkv", t)])
                then(dve.tensor_scalar(dst, src[:, :, 0:T], vec("dn_conv", t), None, MUL))
                then(stt(dst, src[:, :, 1:1 + T], vec("dn_conv", 12 + t), dst, MUL, ADD))
                stt(dst, src[:, :, 2:2 + T], vec("dn_conv", 24 + t), dst, MUL, ADD).then_inc(conv_out, 1)
            dve.wait_ge(iota_ready, 4)
            for g in range(4):
                b = take()
                group = PADP[:, 4 * g:4 * g + 4, :]
                drained(dve.tensor_copy(group[:, :, 8:72], bank(b, 4, 64)), True)
                sums, width = group, 80
                for lv in range(g + 1):
                    step = 1 << lv
                    width -= step
                    wider = (PTA, PTB)[lv % 2]
                    then(tt(wider[:, :, 0:width], sums[:, :, 0:width], sums[:, :, step:step + width], ADD))
                    sums = wider
                i0, i1 = IOT[:, 0, 64 * g:64 * g + 64], IOT[:, 1, 64 * g:64 * g + 64]
                then(stt(i0, i0, float(2 << g), i1, MIN, MIN))
                then(dve.reciprocal(RCNT[:, g, :], i0))
                sums = sums[:, :, 8 - (1 << g):72 - (1 << g)]
                then(tt(sums, sums, mid(RCNT[:, g, :], 4), MUL))
                tt(group[:, :, 8:72], sums, group[:, :, 8:72], SUB).then_inc(pooled_ready, 1)
            b = take()
            drained(dve.tensor_copy(graw, bank(b, 4, 16)), True)
            then(tt(g_s, graw[:, :, 8:16], mid(dtb, 4), ADD))
            then(dve.tensor_scalar(g_m, g_s, 0.0, None, MAX))
            stt(g_e, g_m, -2.0, g_s, MUL, ADD).then_inc(gate_args, 1)
            for i in range(8):
                dve.wait_ge(l2_rstd, i + 1)
                if i < 4:
                    tt(KT[:, i, :], KT[:, i, :], l2_buf(i), MUL).then_inc(l2_done, 1)
                else:
                    stt(QT[:, i - 4, :], QT[:, i - 4, :], float(P) ** -0.5, l2_buf(i), MUL, MUL).then_inc(l2_done, 1)
            for h in range(HEADS):
                b = take()
                drained(dve.tensor_copy(Vtok[:, h], bank(b, 4, P)))
            dve.wait_ge(gate_exps, 1)
            then(tt(g_m, g_m, g_e, ADD))
            then(dve.tensor_scalar(BETA, BETA, 1.0, None, ADD))
            then(dve.reciprocal(BETA, BETA))
            stt(G, g_m, -1.0, mid(alog, 4), MUL, MUL).then_inc(decay_ready, 1)
            b = take()
            for d in range(2):
                ins = dve.tensor_copy(GC[:, :, 4 * d:4 * d + 4], b[:, 16 * d:16 * d + 16].rearrange("p (u h) -> p u h", u=4))
            drained(ins, True)
            dve.wait_ge(gam_exps, 1)
            then(tt(BG, BETA, EGC, MUL))
            ada_steps = 0
            for d in range(2):
                M = (LE, GE)[d]
                lastc = P - 1 if d == 0 else 0
                grow = 0
                for kind, a, h in mixer_steps(d):
                    if kind == "ada":
                        if ada_steps:
                            ada_bias()
                        ada_steps += 1
                    elif kind == "gamma":
                        h = a
                        dh = 4 * d + h
                        diff, Tlo, Thi, _ = decay_bufs[h % 2]
                        b = take()
                        drained(tt(diff, bank(b, 4, P), last(GC[:, :, dh], P), SUB), True)
                        dve.tensor_scalar(Tlo, diff, 0.0, None, MAX)
                        dve.tensor_scalar(Thi, diff, 0.0, None, MIN).then_inc(diff_ready, 1)
                    elif kind == "setup":
                        h = a
                        dh = 4 * d + h
                        _, Tlo, Thi, Tq = decay_bufs[h % 2]
                        dve.wait_ge(decay_exps, dh + 1)
                        then(dve.tensor_copy(KS[:, h, :], Thi[:, :, lastc]))
                        tt(CDK[:, h, :], KS[:, h, :], EGC[:, :, dh], MUL)
                        b = take()
                        for u in range(UNITS):
                            ins = stt(Am[:, h, u, :], Tlo[:, u, :], BETA[:, u, dh:dh + 1], b[:, u * P:u * P + P], MUL, MUL)
                        drained(ins)
                        then(tt(Thi[:, 0:TT], Thi[:, 0:TT], mid(M[:, :], TT), MUL))
                        b = take()
                        drained(tt(qkT[:, h, :], Thi[:, 0:TT].rearrange("p u j -> p (u j)"), b[:, 0:T], MUL))
                        tt(qdT[:, h, :], QT[:, h, :], Tq.rearrange("p u j -> p (u j)"), MUL).then_inc(tri_ready, 1)
                        dve.wait_ge(tri_ready, dh + 1)
                    elif kind == "turn" and a == 0:
                        i = LEVELS * HEADS * d + h
                        dve.wait_ge(masked, i + 1)
                        tt(Xn[:, h], mid(ident[:, :], 4), Amask[:, i % 2], SUB)
                        b = take()
                        drained(tt(XnT[:, h], mid(ident[:, :], 4), bank(b, 4, P), SUB))
                    elif kind == "grow":
                        b = take()
                        drained(tt(XnT[:, h], XnT[:, h], bank(b, 4, P), SUB))
                        if a < LEVELS - 1:
                            b = take()
                            drained(tt(Xn[:, h], Xn[:, h], bank(b, 4, P), SUB))
                    elif kind == "solve":
                        h = a
                        b = take()
                        b2 = VB[(n["v"] + 1) % 4]
                        dve.wait_ge(vector_filled, n["v"] + 2)
                        drained(dve.tensor_copy(Xn[:, h], bank(b, 4, P)))
                        drained(dve.tensor_copy(XnT[:, h], bank(b2, 4, P)))
                    elif kind == "walk":
                        s, u = a, ORDER[d][a]
                        if s:
                            b = take()
                            drained(tt(Wt, Xn[:, :, u, :], bank(b, 4, P), SUB))
                        if u < TT and d == 1:
                            b = take()
                            o = OT[:, :, u * P:u * P + P]
                            drained(tt(o, o, bank(b, 4, P), ADD))
                        if s < UNITS - 1:
                            b = take()
                            if s == 0:
                                drained(dve.tensor_copy(St, bank(b, 4, P)), True)
                            else:
                                then(tt(St, St, last(CDK[:, :, u], P), MUL))
                                drained(tt(St, St, bank(b, 4, P), ADD), True)

            split()
            split()
            ada_bias()
            for i in range(2):
                dve.wait_ge(o_rstd, i + 1)
                o = OT[:, 2 * i:2 * i + 2, :]
                then(tt(o, o, OSQ[:, i, :].rearrange("p (h t) -> p h t", h=2), MUL))
                stt(MIX1[:, 2 * i:2 * i + 2, :], o, vec("dn_norm"), Z1[:, 2 * i:2 * i + 2, :], MUL, MUL)
            for g in range(4):
                b = take()
                drained(dve.tensor_scalar(MIX1[:, 4 + g, :], b[:, 0:T], vec("pool_scale", g), None, MUL))

            def residual(ly, piece, m):
                b = take()
                xm = XH[:, m, META:L2]
                drained(stt(xm, b[:, 0:T], MOD[:, ly, piece + m, 0:1], xm, MUL, ADD))

            dve.wait_ge(vector_drained, n["v"])
            split_input(MIX1, T)
            for m in range(KD):
                residual(0, 16, m)
                split()
            n["segment"] += 1

            def experts(ly):
                dve.wait_ge(vector_drained, n["v"])
                norm(1 + 2 * ly, "norm_ffn", 8 * ly, mod=(ly, 24))
                b = take()
                lg = bank(b, 2, 16)
                then(dve.reduce_max(rmax, lg, AX.X))
                drained(tt(AFFT, lg, last(rmax, 16), SUB), True)
                dve.tensor_copy(rsum, rmax).then_inc(sm_args, 1)
                dve.wait_ge(sm_exps, ly + 1)
                then(dve.reduce_sum(rsum, AFFT, AX.X))
                then(dve.reciprocal(rsum, rsum))
                tt(AFFT, AFFT, last(rsum, 16), MUL).then_inc(aff_ready, 1)
                b = take()
                drained(dve.tensor_copy(AT2[0:EXP, :], b[0:EXP, 0:T]), True)
                for r in range(CAP // 8):
                    src = AT2 if r == 0 else WT2
                    then(dve.max(m8[0:EXP, :], src[0:EXP, :]))
                    then(dve.match_replace(out=WT2[0:EXP, :], in_to_replace=m8[0:EXP, :], in_values=src[0:EXP, :], imm_value=-1.0))
                then(dve.tensor_scalar(MT2[0:EXP, :], WT2[0:EXP, :], 0.0, None, ALU.is_lt))
                then(dve.tensor_tensor_scan(PS2[0:EXP, :], WIDE[0:EXP, P:P + 1].broadcast_to([EXP, T]), MT2[0:EXP, :], 0.0, MUL, ADD))
                tt(PS2[0:EXP, :], PS2[0:EXP, :], MT2[0:EXP, :], MUL).then_inc(pos_ready, 1)
                b = take()
                drained(dve.tensor_copy(POS, bank(b, 2, 16)), True)
                pts = [PT[:, t_, :].rearrange("p (e s) -> p e s", e=EXP) for t_ in range(TT)]
                for t_, pt in enumerate(pts):
                    ins = tt(pt, last(POS[:, t_, :], CAP), mid(SLOTN, EXP), ALU.is_equal)
                ins.then_inc(pick_ready, 1)
                dve.wait_ge(pick_ready, 2 * ly + 1)
                for t_, pt in enumerate(pts):
                    ins = tt(GPT[:, t_, :].rearrange("p (e s) -> p e s", e=EXP), pt, last(AFFT[:, t_, :], CAP), MUL)
                ins.then_inc(pick_ready, 1)
                v0 = n["v"]
                s0 = mark[("group", ly)][1]
                with dve.Fori(0, GROUPS) as g:
                    def filled(i):
                        dve.wait_ge(vector_filled, g * 4 + (v0 + i + 1))
                        return VB[(v0 + i) % 4]
                    b = filled(0)
                    dve.tensor_copy(XG[:, 4:8], bank(b, 4, P)).then_inc(vector_drained, 1)
                    b = filled(1)
                    dve.wait_ge(scalar_drained, g * 4 + (s0 + 2))
                    tt(HIDD, SG, b[:, :], MUL).then_inc(vector_drained, 1)
                    b = filled(2)
                    dve.tensor_copy(HT[:, 2:4], bank(b, 2, P)).then_inc(vector_drained, 1)
                    b = filled(3)
                    dve.tensor_copy(Y[:, bass.ds(g, 1), 512:1024].rearrange("p a n -> p (a n)"), b[:, :]).then_inc(vector_drained, 1)
                n["v"] += 4 * GROUPS
                for gh in range(2):
                    b = take()
                    drained(dve.tensor_copy(CM[:, 2 * gh:2 * gh + 2, :], bank(b, 2, T)))
                if ly == 1:
                    root("meta_norm", META, NVn, NRn, NTn)
                for m in range(KD):
                    residual(ly, 40, m)
                    if m in (3, 4):
                        split()

            experts(0)

            dve.wait_ge(vector_drained, n["v"])
            norm(2, "norm_mix", 8, mod=(1, 0))
            dve.memset(CPAD[:, :, 0:1], 0.0)
            then(dve.memset(CPAD[:, :, T + 1:T + 2], 0.0))
            for m in range(KD):
                if m % 4 == 0:
                    for _ in range(4):
                        split()
                split()
                dve.wait_ge(scalar_drained, mark[("gc", m)])
                b = take()
                drained(tt(CPAD[:, m, 1:1 + T], b[:, 0:T], GCC[:, m, :], MUL), True)
                then(dve.tensor_scalar(CO[:, m, :], CPAD[:, m, 0:T], vec("sc_conv", m), None, MUL))
                then(stt(CO[:, m, :], CPAD[:, m, 1:1 + T], vec("sc_conv", 8 + m), CO[:, m, :], MUL, ADD))
                then(stt(CO[:, m, :], CPAD[:, m, 2:2 + T], vec("sc_conv", 16 + m), CO[:, m, :], MUL, ADD))
            for m in range(KD):
                split()
                b = take()
                drained(tt(MIX2[:, m, :], b[:, 0:T], CO[:, m, :], MUL))
            dve.wait_ge(vector_drained, n["v"])
            split_input(MIX2, T)
            for m in range(KD):
                residual(1, 16, m)
                split()
            n["segment"] += 1

            experts(1)

            dve.wait_ge(vector_drained, n["v"])
            dve.memset(CB3[:, :, 0:3], 0.0).then_inc(edges_ready, 1)
            root(("norm", 4), T, NVn, NR4, NTn)
            then(tt(NS5[:, 0:T], NR4[:, 0:T], NR4[:, 0:T], MUL))
            tt(NS5[:, 0:T], NS5[:, 0:T], SB[(mark[("norm", 4)] - 1) % 4][:, T:2 * T], MUL).then_inc(mean_ready, 1)
            for k in range(KD):
                v = XH[:, k, META:L2]
                ins = stt(v, v, vec("norm_final", k), NR4[:, 0:T], MUL, MUL)
            dve.wait_ge(mean_ready, 1)
            then(negated_half(NS5[:, 0:T], NVn[:, 0:T]))
            newton(NVn[:, 0:T], NRn[:, META:L2], NTn[:, 0:T])
            for k in range(KD):
                stt(hN[:, k, :], XH[:, k, :], vec("even_norm", k), NRn[:, 0:L2], MUL, MUL).then_inc(h_scaled, 1)
            low_parts(5, hN, L2)
            then(dve.tensor_scalar(lc8, vec("lru_lambda", 0, 8), -1.0, 0.0, MUL, MAX))
            then(stt(ln8, lc8, -2.0, vec("lru_lambda", 0, 8), MUL, SUB))

            for t in range(20):
                split()
                dve.wait_ge(scalar_drained, mark[("conv3", t)])
                dst = XB[:, t, :] if t < 12 else LX[:, t - 12, :]
                wn, wt, nt_, m = ("ssd_conv", 12, 12, t) if t < 12 else ("lru_conv", 8, 8, t - 12)
                src = CB3[:, t % 4, :]
                then(dve.tensor_scalar(dst, src[:, 0:L2], vec(wn + "_w", m), vec(wn + "_b", m), MUL, ADD))
                for j in range(1, 4):
                    ins = stt(dst, src[:, j:j + L2], vec(wn + "_w", j * wt + m), dst, MUL, ADD)
                    if j < 3:
                        then(ins)
                ins.then_inc(conv_out, 1)
            dve.memset(CUM, 0.0)
            then(dve.memset(DT3, 0.0))
            b = take()
            dve.tensor_copy(DT3[:, 0:2, :], bank(b, 2, 16))
            drained(dve.tensor_copy(DT3[0:META, 2, :], b[0:META, 32:48]), True)
            then(tt(DT3, DT3, mid(sdtb, 3), ADD))
            then(dve.tensor_scalar(DTm, DT3, 0.0, None, MAX))
            stt(DTn, DTm, -2.0, DT3, MUL, ADD).then_inc(dt_args, 1)
            split()
            dve.wait_ge(dt_exps, 1)
            then(tt(DT3, DTm, DTn, ADD))
            stt(ADT, DT3, -1.0, mid(salog, 3), MUL, MUL).then_inc(dt_ready, 1)
            then(tt(lc8, lc8, ln8, ADD))
            dve.tensor_scalar(lc8, lc8, -8.0, None, MUL).then_inc(lc_ready, 1)
            for _ in range(3):
                split()
            dve.wait_ge(scalar_drained, mark[("lru", KD - 1, 1)])
            split()
            then(tt(LI, LI, LX, MUL))
            split()
            split()
            dve.wait_ge(tanh_ready, KD)
            dve.tensor_scalar(LTH, LTH, -1.0, 1e-18, MUL, MAX).then_inc(mult_args, 1)
            split()
            split()
            split()
            split()
            dve.wait_ge(logs_ready, 1)
            tt(LTH, LTH, LX, SUB).then_inc(half_ready, 1)
            split()
            dve.wait_ge(mult_ready, 1)
            then(tt(LI, LI, LTH, MUL))
            for m in range(KD):
                ins = dve.tensor_tensor_scan(MIX3[:, m, :], LR[:, m, :], LI[:, m, :], 0.0, MUL, ADD)
                if m % 4 == 1:
                    split()
            then(ins)
            split()
            dve.wait_ge(gate_silus, 1)
            tt(MIX3[:, 0:8, :], MIX3[:, 0:8, :], SLG, MUL).then_inc(lru_done, 1)
            split()
            dve.wait_ge(lru_done, 1)
            dve.wait_ge(scalar_filled, mark[("ssd_z", KD - 1)])
            split_input(MIX3[:, 0:8, :], L2)
            for m in range(KD):
                b = take()
                drained(tt(XH[:, m, :], b[:, 0:L2], XH[:, m, :], ADD))
                split()
            b = take()
            dve.tensor_copy(CUM[:, 0:2, :], bank(b, 2, 16))
            drained(dve.tensor_copy(CUM[0:META, 2, :], b[0:META, 32:48]), True)
            dve.wait_ge(iota_ready, 7)
            then(dve.memset(CBM[:, :, 416:432], 0.0))
            for g in range(2):
                b = take()
                tt(CBM[:, g, 0:416], b[:, 0:416], MASK3[:, 0:416], MUL)
                drained(tt(CBM[0:META, g, 416:432], b[0:META, 416:432], MASK3[0:META, 416:432], MUL), True)

            def ssd_arg(h):
                b = take()
                e = EB[:, h % 3, :]
                dve.tensor_scalar(e[:, 0:272], b[:, 0:272], CUM[:, 0, h:h + 1], 0.0, SUB, MIN)
                dve.tensor_scalar(e[:, 272:416], b[:, 128:272], CUM[:, 1, h:h + 1], 0.0, SUB, MIN)
                drained(dve.tensor_scalar(e[:, 416:432], b[:, 256:272], CUM[:, 2, h:h + 1], 0.0, SUB, MIN))

            ssd_arg(0)
            ssd_arg(1)
            for i, (_, _, r) in enumerate(SRC):
                dve.wait_ge(scalar_drained, mark[("xtk", i, 1)])
                v = XTK[0:r, i, :].rearrange("p (h j) -> p h j", h=SSD_H)
                tt(v, v, last(DT3[0:r, i, :], 64), MUL).then_inc(tokens_scaled, 1)
            for h in range(SSD_H):
                if h + 2 < SSD_H:
                    ssd_arg(h + 2)
                r0, m = 64 * (h % 2), h // 2
                b = take()
                drained(stt(MIX3[r0:r0 + 64, 8 + m, :], XB[r0:r0 + 64, m, :], ssdd[r0:r0 + 64, m:m + 1], b[r0:r0 + 64, 0:L2], MUL, ADD),
                        h % 2 == 1)
                if h % 2 == 1:
                    tt(MIX3[:, 8 + m, :], MIX3[:, 8 + m, :], SZ[:, m, :], MUL).then_inc(gated, 1)
            for g in range(2):
                if g == 0:
                    dve.wait_ge(gated, KD)
                dve.wait_ge(gate_rstd, g + 1)
                for k in range(4):
                    v = MIX3[:, 8 + 4 * g + k, :]
                    ins = stt(v, v, vec("ssd_norm", 4 * g + k), GRR[:, g, :], MUL, MUL)
                then(ins)
                split_input(MIX3[:, 8:16, :], L2, 4 * g, 4)
            for m in range(KD):
                b = take()
                drained(tt(XH[:, m, :], b[:, 0:L2], XH[:, m, :], ADD))
                split()

            dve.wait_ge(vector_drained, n["v"])
            norm(6, "odd_norm", 0, 0, L2)
            dve.memset(KS2[:, :, L2:384], 0.0)
            for m in range(KD):
                split()
            for m in range(KD):
                split()
                b = take()
                drained(dve.tensor_copy(KS2[:, m, 0:L2], b[:, 0:L2]))
            for m in range(KD):
                split()
                b = take()
                drained(dve.tensor_copy(VS[:, m, :], b[:, 0:L2]))
            for m in range(KD):
                split()
            for i, (_, _, r) in enumerate(SRC):
                for kh in range(2):
                    b = take()
                    drained(dve.tensor_copy(VTK[0:r, i, 512 * kh:512 * kh + 512], b[0:r, :]))
            dve.wait_ge(iota_ready, 8)

            def soft(h):
                dve.wait_ge(sb_logs, h + 1)
                q = PB[:, h % 2, :]
                then(stt(q, ZB[:, h % 3, :], 0.0, LB[:, h % 3, :], MAX, ADD))
                tt(q, q, SMASK, MUL).then_inc(sb_soft, 1)

            def stick_o(h):
                r0, m = 64 * (h % 2), h // 2
                b = take()
                drained(tt(OS[r0:r0 + 64, m, :], b[r0:r0 + 64, 0:L2], SGT[r0:r0 + 64, m, :], MUL))

            soft(0)
            for h in range(SB_H):
                if h + 1 < SB_H:
                    soft(h + 1)
                b = take()
                e = EBS[:, h % 2, :]
                drained(stt(e, b[:, 0:TRI], -1.0, ZB[:, h % 3, :], MUL, ADD), True)
                stt(e, e, 0.0, NEG, MIN, ADD).then_inc(sb_args, 1)
                if h >= 1:
                    stick_o(h - 1)
            stick_o(SB_H - 1)
            dve.wait_ge(vector_drained, n["v"])
            split_input(OS, L2)
            for m in range(KD):
                b = take()
                drained(tt(XH[:, m, :], b[:, 0:L2], XH[:, m, :], ADD))
                split()
            assert n["split"] == len(quarters)
            dve.wait_ge(vector_drained, n["v"])
            norm(7, "final_norm", 0)
            for t_ in range(TT):
                b = take()
                n["v"] += 1
                dve.tensor_copy(OUTS[:, t_, 0:512], b[:, :]).then_inc(out_copied, 1)
            assert n["v"] == mark["v_end"]


_INS = ['x', 'c', 'ctx', 'c_ctx', 'ada_w', 'ada_b', 'norm_mix', 'norm_ffn', 'norm_final', 'ev_w_in', 'dn_conv',
        'dn_a_log', 'dn_dt_bias', 'dn_norm', 'pool_w', 'pool_scale', 'ev_w_out', 'sc_w_in', 'sc_conv', 'sc_w_out',
        'router', 'w_gate', 'w_up', 'w_down', 'meta_2', 'even_norm_2', 'even_w_in_2', 'lru_conv_w_2',
        'lru_conv_b_2', 'lru_w_a_2', 'lru_b_a_2', 'lru_w_x_2', 'lru_b_x_2', 'lru_lambda_2', 'ssd_conv_w_2',
        'ssd_conv_b_2', 'ssd_dt_bias_2', 'ssd_a_log_2', 'ssd_d_2', 'ssd_norm_2', 'even_w_out_2', 'odd_norm_2',
        'odd_w_in_2', 'odd_w_out_2', 'final_norm_2']
_OUTS = [((1, T, D), 'float32')]


def kernel(**inputs):
    import numpy as _np
    import concourse.bacc as _bacc
    from concourse import mybir as _mybir
    from concourse.bass_utils import run_bass_kernel_spmd as _run

    nc = _bacc.Bacc("TRN2", target_bir_lowering=False, num_devices=1)
    arrays, args = {}, []
    for name in _INS:
        a = _np.ascontiguousarray(inputs[name])
        arrays[f"in_{name}_dram"] = a
        args.append(nc.dram_tensor(f"in_{name}_dram", a.shape, _mybir.dt.from_np(a.dtype), kind="ExternalInput").ap())
    for i, (shape, dtype) in enumerate(_OUTS):
        dt = _mybir.dt.from_np(_np.dtype(dtype))
        args.append(nc.dram_tensor(f"out_{i}_dram", shape, dt, kind="ExternalOutput").ap())
    build(nc, *args)
    r = _run(nc, [arrays], core_ids=[0])
    got = tuple(r.results[0][f"out_{i}_dram"] for i in range(len(_OUTS)))
    return got[0]
```
